# Optimizing a Trainium2 kernel written in Bass

```python
import math
import jax
import jax.numpy as jnp
from jax import lax
import jax, jax.numpy as jnp
import numpy as np

D_MODEL = 1024
BATCH = 1
SEQ = 512
DEPTH = 2

MEM_LEN = 256
EPS = 1e-6
NEG_INF = -1e30
FORCE_SCORE = 1e4

POOL_WIDTH = D_MODEL // 2
POOL_WINDOWS = (2, 4, 8, 16)
POOL_GROUPS = len(POOL_WINDOWS)
POOL_GROUP_DIM = POOL_WIDTH // POOL_GROUPS
DN_WIDTH = D_MODEL - POOL_WIDTH
DN_HEAD_DIM = 128
DN_HEADS = DN_WIDTH // DN_HEAD_DIM
DN_CONV = 4
DN_CHUNK = 64
A_SIZES = (POOL_WIDTH, DN_WIDTH, DN_WIDTH, DN_WIDTH, DN_WIDTH, DN_HEADS, DN_HEADS)
IN_A_COLS = POOL_WIDTH + 4 * DN_WIDTH + 2 * DN_HEADS

NSA_HEAD_DIM = 64
NSA_HEADS = D_MODEL // NSA_HEAD_DIM
NSA_GROUPS = 4
NSA_REP = NSA_HEADS // NSA_GROUPS
NSA_KV = NSA_GROUPS * NSA_HEAD_DIM
CMP_LEN = 32
CMP_STRIDE = 16
CMP_HIDDEN = 2 * NSA_HEAD_DIM
SLC_LEN = 64
SLC_TOP = 16
WINDOW = 512
NSA_QBLOCK = 32
C_SIZES = (D_MODEL, NSA_KV, NSA_KV, NSA_KV, NSA_KV, NSA_KV, NSA_KV, 3 * NSA_HEADS)
IN_C_COLS = D_MODEL + 6 * NSA_KV + 3 * NSA_HEADS

XA_HEADS = 4
XA_HEAD_DIM = D_MODEL // XA_HEADS
FF_DIM = 4 * D_MODEL

N_EVEN = (DEPTH + 1) // 2
N_ODD = DEPTH // 2


def rmsnorm(x, g):
    xf = x.astype(jnp.float32)
    y = xf * lax.rsqrt(jnp.mean(xf * xf, axis=-1, keepdims=True) + EPS)
    return (y * g.astype(jnp.float32)).astype(x.dtype)

def l2norm(x):
    return x * lax.rsqrt(jnp.sum(x * x, axis=-1, keepdims=True) + EPS)

def alibi_slopes(n_heads):
    h = jnp.arange(1, n_heads + 1, dtype=jnp.float32)
    return jnp.exp2(-8.0 * h / n_heads)

def split_cols(z, sizes):
    outs, start = [], 0
    for n in sizes:
        outs.append(z[..., start:start + n])
        start += n
    return outs

def causal_depthwise_conv(x, w):
    width, ch = w.shape
    return lax.conv_general_dilated(
        x, w[:, None, :].astype(x.dtype), window_strides=(1,), padding=[(width - 1, 0)],
        dimension_numbers=('NWC', 'WIO', 'NWC'), feature_group_count=ch)

def multiscale_pool(u, pool_w, pool_scale):
    b, s, _ = u.shape
    uf = u.astype(jnp.float32)
    pos1 = jnp.arange(1, s + 1, dtype=jnp.float32)[None, :, None]
    outs = []
    for gi, win in enumerate(POOL_WINDOWS):
        ug = uf[..., gi * POOL_GROUP_DIM:(gi + 1) * POOL_GROUP_DIM]
        csum = jnp.pad(jnp.cumsum(ug, axis=1), ((0, 0), (1, 0), (0, 0)))
        lower = jnp.pad(csum, ((0, 0), (win - 1, 0), (0, 0)))[:, :s]
        mean = (csum[:, 1:] - lower) / jnp.minimum(pos1, float(win))
        outs.append(mean - ug)
    y = jnp.stack(outs, axis=2)
    y = jnp.einsum('bsgc,gcd->bsgd', y, pool_w.astype(jnp.float32)).reshape(b, s, POOL_WIDTH)
    return (y * pool_scale.astype(jnp.float32)).astype(u.dtype)

def gated_delta_rule(q, k, v, beta, log_decay):
    b, h, s, dk = q.shape
    dv = v.shape[-1]
    c = DN_CHUNK
    n = s // c
    q = q * (dk ** -0.5)
    q, k, v = (a.reshape(b, h, n, c, a.shape[-1]) for a in (q, k, v))
    beta = beta.reshape(b, h, n, c)
    gc = jnp.cumsum(log_decay.reshape(b, h, n, c), axis=-1)
    causal = jnp.tril(jnp.ones((c, c), dtype=bool))
    strict = jnp.tril(jnp.ones((c, c), dtype=bool), -1)
    diff = gc[..., :, None] - gc[..., None, :]
    decay_mat = jnp.where(causal, jnp.exp(jnp.where(causal, diff, 0.0)), 0.0)
    kb = k * beta[..., None]
    a_low = jnp.where(strict, jnp.einsum('bhnid,bhnjd->bhnij', kb, k) * decay_mat, 0.0)
    eye = jnp.eye(c, dtype=jnp.float32)
    t_mat = lax.linalg.triangular_solve(eye + a_low, jnp.broadcast_to(eye, a_low.shape),
                                        left_side=True, lower=True, unit_diagonal=True)
    w_c = jnp.matmul(t_mat, kb * jnp.exp(gc)[..., None])
    u_c = jnp.matmul(t_mat, v * beta[..., None])
    attn = jnp.where(causal, jnp.einsum('bhnid,bhnjd->bhnij', q, k) * decay_mat, 0.0)

    def step(state, xs):
        q_i, k_i, w_i, u_i, attn_i, gc_i = xs
        v_new = u_i - jnp.matmul(w_i, state)
        o_i = jnp.matmul(q_i * jnp.exp(gc_i)[..., None], state) + jnp.matmul(attn_i, v_new)
        g_last = gc_i[..., -1]
        k_dec = k_i * jnp.exp(g_last[..., None] - gc_i)[..., None]
        state = state * jnp.exp(g_last)[..., None, None] + jnp.einsum('bhcd,bhce->bhde', k_dec, v_new)
        return state, o_i

    xs = tuple(jnp.moveaxis(a, 2, 0) for a in (q, k, w_c, u_c, attn, gc))
    state0 = jnp.zeros((b, h, dk, dv), jnp.float32)
    _, o = lax.scan(step, state0, xs)
    return jnp.moveaxis(o, 0, 2).reshape(b, h, s, dv)

def gated_deltanet(q, k, v, gate, beta_logit, alpha_logit, conv_w, a_log, dt_bias, o_norm):
    b, s, _ = q.shape
    f32 = jnp.float32
    qkv = jax.nn.silu(causal_depthwise_conv(jnp.concatenate([q, k, v], axis=-1), conv_w))
    qkv = jnp.transpose(qkv.astype(f32).reshape(b, s, 3, DN_HEADS, DN_HEAD_DIM), (2, 0, 3, 1, 4))
    qh, kh, vh = l2norm(qkv[0]), l2norm(qkv[1]), qkv[2]
    beta = jnp.transpose(jax.nn.sigmoid(beta_logit.astype(f32)), (0, 2, 1))
    log_decay = -jnp.exp(a_log.astype(f32)) * jax.nn.softplus(alpha_logit.astype(f32) + dt_bias.astype(f32))
    o = gated_delta_rule(qh, kh, vh, beta, jnp.transpose(log_decay, (0, 2, 1)))
    o = jnp.transpose(o, (0, 2, 1, 3))
    o = rmsnorm(o, o_norm) * jax.nn.silu(gate.astype(f32).reshape(b, s, DN_HEADS, DN_HEAD_DIM))
    return o.reshape(b, s, DN_WIDTH).astype(q.dtype)

def pool_delta_mixer(h, w_in, pool_w, pool_scale, conv_w, a_log, dt_bias, o_norm, w_out):
    z = h @ w_in
    u, q, k, v, gate, beta_l, alpha_l = split_cols(z, A_SIZES)
    y_pool = multiscale_pool(u, pool_w, pool_scale)
    y_dn = gated_deltanet(q, k, v, gate, beta_l, alpha_l, conv_w, a_log, dt_bias, o_norm)
    return jnp.concatenate([y_pool, y_dn], axis=-1) @ w_out

def compress_kv(kv, pe, w1, w2):
    b, s, g, d = kv.shape
    n_str = s // CMP_STRIDE
    per = CMP_LEN // CMP_STRIDE
    n_cmp = n_str - per + 1
    c = kv.reshape(b, n_str, CMP_STRIDE, g, d)
    blocks = jnp.concatenate([c[:, j:j + n_cmp] for j in range(per)], axis=2)
    blocks = blocks + pe[None, None, :, None, :].astype(kv.dtype)
    flat = jnp.transpose(blocks, (0, 1, 3, 2, 4)).reshape(b, n_cmp, g, CMP_LEN * d)
    return jax.nn.silu(flat @ w1) @ w2

def nsa_attention(q, kc, vc, ks, vs, kw, vw, gate_logit, pe_k, w1_k, w2_k, pe_v, w1_v, w2_v):
    b, s, _ = q.shape
    dt = q.dtype
    f32 = jnp.float32
    g_, r_, d_ = NSA_GROUPS, NSA_REP, NSA_HEAD_DIM
    qh = q.reshape(b, s, g_, r_, d_)
    ck = compress_kv(kc.reshape(b, s, g_, d_), pe_k, w1_k, w2_k)
    cv = compress_kv(vc.reshape(b, s, g_, d_), pe_v, w1_v, w2_v)
    n_cmp = ck.shape[1]
    n_slc = s // SLC_LEN
    top_n = min(SLC_TOP, n_slc)
    ks_b = jnp.transpose(ks.reshape(b, n_slc, SLC_LEN, g_, d_), (0, 3, 1, 2, 4))
    vs_b = jnp.transpose(vs.reshape(b, n_slc, SLC_LEN, g_, d_), (0, 3, 1, 2, 4))
    kw_p = jnp.pad(kw.reshape(b, s, g_, d_), ((0, 0), (WINDOW, 0), (0, 0), (0, 0)))
    vw_p = jnp.pad(vw.reshape(b, s, g_, d_), ((0, 0), (WINDOW, 0), (0, 0), (0, 0)))
    gates = jax.nn.sigmoid(gate_logit.astype(f32)).reshape(b, s, g_, r_, 3)
    slopes = alibi_slopes(NSA_HEADS).reshape(g_, r_)
    scale = d_ ** -0.5
    c_lo = jnp.arange(n_cmp) * CMP_STRIDE
    cmp_end = c_lo + CMP_LEN - 1
    s_lo = jnp.arange(n_slc) * SLC_LEN
    overlap = jnp.clip(jnp.minimum(c_lo[:, None] + CMP_LEN, s_lo[None, :] + SLC_LEN)
                       - jnp.maximum(c_lo[:, None], s_lo[None, :]), 0, None).astype(f32) / CMP_LEN
    blk = jnp.arange(n_slc)
    in_blk = jnp.arange(SLC_LEN)
    win_off = jnp.arange(WINDOW + NSA_QBLOCK)
    b_idx = jnp.arange(b)[:, None, None, None]
    g_idx = jnp.arange(g_)[None, :, None, None]

    def one_block(i):
        q0 = i * NSA_QBLOCK
        qb = lax.dynamic_slice_in_dim(qh, q0, NSA_QBLOCK, axis=1)
        t = q0 + jnp.arange(NSA_QBLOCK)
        dist_c = (t[:, None] - cmp_end[None, :]).astype(f32)
        ok_c = dist_c >= 0
        sc = jnp.einsum('bqgrd,bcgd->bgrqc', qb, ck).astype(f32) * scale
        sc = jnp.where(ok_c, sc - slopes[:, :, None, None] * dist_c, NEG_INF)
        p_cmp = jnp.where(jnp.any(ok_c, axis=-1)[:, None], jax.nn.softmax(sc, axis=-1), 0.0)
        o_cmp = jnp.einsum('bgrqc,bcgd->bqgrd', p_cmp.astype(dt), cv)
        imp = jnp.einsum('bgrqc,cn->bgqn', p_cmp, overlap)
        cur = t[:, None] // SLC_LEN
        forced = (blk[None, :] == 0) | (blk[None, :] == cur) | (blk[None, :] == cur - 1)
        causal_blk = blk[None, :] * SLC_LEN <= t[:, None]
        imp = jnp.where(forced, FORCE_SCORE, jnp.where(causal_blk, imp, -1.0))
        _, idx = lax.top_k(imp, top_n)
        kg = ks_b[b_idx, g_idx, idx]
        vg = vs_b[b_idx, g_idx, idx]
        dist_s = (t[None, None, :, None, None] - (idx[..., None] * SLC_LEN + in_blk)).astype(f32)
        ss = jnp.einsum('bqgrd,bgqnld->bgrqnl', qb, kg).astype(f32) * scale
        ss = jnp.where(dist_s[:, :, None] >= 0,
                       ss - slopes[None, :, :, None, None, None] * dist_s[:, :, None], NEG_INF)
        p_slc = jax.nn.softmax(ss.reshape(b, g_, r_, NSA_QBLOCK, -1), axis=-1).reshape(ss.shape)
        o_slc = jnp.einsum('bgrqnl,bgqnld->bqgrd', p_slc.astype(dt), vg)
        kwb = lax.dynamic_slice_in_dim(kw_p, q0, WINDOW + NSA_QBLOCK, axis=1)
        vwb = lax.dynamic_slice_in_dim(vw_p, q0, WINDOW + NSA_QBLOCK, axis=1)
        kpos = q0 - WINDOW + win_off
        dist_w = t[:, None] - kpos[None, :]
        ok_w = (dist_w >= 0) & (dist_w < WINDOW) & (kpos[None, :] >= 0)
        sw = jnp.einsum('bqgrd,bkgd->bgrqk', qb, kwb).astype(f32) * scale
        sw = jnp.where(ok_w, sw - slopes[:, :, None, None] * dist_w.astype(f32), NEG_INF)
        p_win = jax.nn.softmax(sw, axis=-1)
        o_win = jnp.einsum('bgrqk,bkgd->bqgrd', p_win.astype(dt), vwb)
        gb = lax.dynamic_slice_in_dim(gates, q0, NSA_QBLOCK, axis=1)
        o = gb[..., 0:1] * o_cmp + gb[..., 1:2] * o_slc + gb[..., 2:3] * o_win
        return o.reshape(b, NSA_QBLOCK, NSA_HEADS * d_).astype(dt)

    out = lax.map(one_block, jnp.arange(s // NSA_QBLOCK))
    return jnp.moveaxis(out, 0, 1).reshape(b, s, NSA_HEADS * d_)

def nsa_mixer(h, w_in, pe_k, w1_k, w2_k, pe_v, w1_v, w2_v, w_out):
    z = h @ w_in
    q, kc, vc, ks, vs, kw, vw, gl = split_cols(z, C_SIZES)
    return nsa_attention(q, kc, vc, ks, vs, kw, vw, gl, pe_k, w1_k, w2_k, pe_v, w1_v, w2_v) @ w_out

def memory_xattn(h, mem_h, wq, wk, wv, wo):
    b, s, _ = h.shape
    m = mem_h.shape[1]
    q = (h @ wq).reshape(b, s, XA_HEADS, XA_HEAD_DIM)
    k = (mem_h @ wk).reshape(b, m, XA_HEADS, XA_HEAD_DIM)
    v = (mem_h @ wv).reshape(b, m, XA_HEADS, XA_HEAD_DIM)
    sc = jnp.einsum('bshd,bmhd->bhsm', q, k).astype(jnp.float32) * (XA_HEAD_DIM ** -0.5)
    p = jax.nn.softmax(sc, axis=-1).astype(h.dtype)
    o = jnp.einsum('bhsm,bmhd->bshd', p, v).reshape(b, s, D_MODEL)
    return o @ wo

def squared_relu_mlp(h, w1, w2):
    return jnp.square(jax.nn.relu(h @ w1)) @ w2

def first_inputs(seed: int = 0) -> dict:
    key = jax.random.key(seed)
    keys = iter(jax.random.split(key, 40))
    f32 = jnp.float32

    def dense(shape, fan_in):
        return jax.random.normal(next(keys), shape, f32) * (fan_in ** -0.5)

    def gain(shape):
        return 1.0 + 0.05 * jax.random.normal(next(keys), shape, f32)

    ne, no, dep = N_EVEN, N_ODD, DEPTH
    x = jax.random.normal(next(keys), (BATCH, SEQ, D_MODEL), f32)
    mem = jax.random.normal(next(keys), (BATCH, MEM_LEN, D_MODEL), f32)
    a_ln = gain((ne, D_MODEL))
    a_w_in = dense((ne, D_MODEL, IN_A_COLS), D_MODEL)
    a_pool_w = dense((ne, POOL_GROUPS, POOL_GROUP_DIM, POOL_GROUP_DIM), POOL_GROUP_DIM)
    a_pool_scale = gain((ne, POOL_WIDTH))
    a_conv_w = dense((ne, DN_CONV, 3 * DN_WIDTH), DN_CONV)
    a_a_log = jnp.log(jax.random.uniform(next(keys), (ne, DN_HEADS), f32, 1.0, 16.0))
    dt_init = jnp.exp(jax.random.uniform(next(keys), (ne, DN_HEADS), f32, math.log(1e-3), math.log(1e-1)))
    a_dt_bias = dt_init + jnp.log(-jnp.expm1(-dt_init))
    a_o_norm = gain((ne, DN_HEAD_DIM))
    a_w_out = dense((ne, D_MODEL, D_MODEL), D_MODEL)
    c_ln = gain((no, D_MODEL))
    c_w_in = dense((no, D_MODEL, IN_C_COLS), D_MODEL)
    c_pe_k = 0.1 * jax.random.normal(next(keys), (no, CMP_LEN, NSA_HEAD_DIM), f32)
    c_w1_k = dense((no, CMP_LEN * NSA_HEAD_DIM, CMP_HIDDEN), CMP_LEN * NSA_HEAD_DIM)
    c_w2_k = dense((no, CMP_HIDDEN, NSA_HEAD_DIM), CMP_HIDDEN)
    c_pe_v = 0.1 * jax.random.normal(next(keys), (no, CMP_LEN, NSA_HEAD_DIM), f32)
    c_w1_v = dense((no, CMP_LEN * NSA_HEAD_DIM, CMP_HIDDEN), CMP_LEN * NSA_HEAD_DIM)
    c_w2_v = dense((no, CMP_HIDDEN, NSA_HEAD_DIM), CMP_HIDDEN)
    c_w_out = dense((no, D_MODEL, D_MODEL), D_MODEL)
    xa_ln = gain((dep, D_MODEL))
    xa_mem_ln = gain((dep, D_MODEL))
    xa_wq = dense((dep, D_MODEL, D_MODEL), D_MODEL)
    xa_wk = dense((dep, D_MODEL, D_MODEL), D_MODEL)
    xa_wv = dense((dep, D_MODEL, D_MODEL), D_MODEL)
    xa_wo = dense((dep, D_MODEL, D_MODEL), D_MODEL)
    ff_ln = gain((dep, D_MODEL))
    ff_w1 = dense((dep, D_MODEL, FF_DIM), D_MODEL)
    ff_w2 = dense((dep, FF_DIM, D_MODEL), FF_DIM)
    final_ln = gain((D_MODEL,))
    return {'x': x, 'mem': mem,
            'a_ln': a_ln, 'a_w_in': a_w_in, 'a_pool_w': a_pool_w, 'a_pool_scale': a_pool_scale,
            'a_conv_w': a_conv_w, 'a_a_log': a_a_log, 'a_dt_bias': a_dt_bias, 'a_o_norm': a_o_norm,
            'a_w_out': a_w_out,
            'c_ln': c_ln, 'c_w_in': c_w_in, 'c_pe_k': c_pe_k, 'c_w1_k': c_w1_k, 'c_w2_k': c_w2_k,
            'c_pe_v': c_pe_v, 'c_w1_v': c_w1_v, 'c_w2_v': c_w2_v, 'c_w_out': c_w_out,
            'xa_ln': xa_ln, 'xa_mem_ln': xa_mem_ln, 'xa_wq': xa_wq, 'xa_wk': xa_wk, 'xa_wv': xa_wv,
            'xa_wo': xa_wo,
            'ff_ln': ff_ln, 'ff_w1': ff_w1, 'ff_w2': ff_w2, 'final_ln': final_ln}

def first_block(x, mem,
              a_ln, a_w_in, a_pool_w, a_pool_scale, a_conv_w, a_a_log, a_dt_bias, a_o_norm, a_w_out,
              c_ln, c_w_in, c_pe_k, c_w1_k, c_w2_k, c_pe_v, c_w1_v, c_w2_v, c_w_out,
              xa_ln, xa_mem_ln, xa_wq, xa_wk, xa_wv, xa_wo,
              ff_ln, ff_w1, ff_w2, final_ln):
    for l in range(DEPTH):
        i = l // 2
        if l % 2 == 0:
            x = x + pool_delta_mixer(rmsnorm(x, a_ln[i]), a_w_in[i], a_pool_w[i], a_pool_scale[i],
                                     a_conv_w[i], a_a_log[i], a_dt_bias[i], a_o_norm[i], a_w_out[i])
        else:
            x = x + nsa_mixer(rmsnorm(x, c_ln[i]), c_w_in[i], c_pe_k[i], c_w1_k[i], c_w2_k[i],
                              c_pe_v[i], c_w1_v[i], c_w2_v[i], c_w_out[i])
        x = x + memory_xattn(rmsnorm(x, xa_ln[l]), rmsnorm(mem, xa_mem_ln[l]),
                             xa_wq[l], xa_wk[l], xa_wv[l], xa_wo[l])
        x = x + squared_relu_mlp(rmsnorm(x, ff_ln[l]), ff_w1[l], ff_w2[l])
    return rmsnorm(x, final_ln)


CTX_LEN = 256
GRID_W = 64
N_EVEN_2 = (DEPTH + 1) // 2
N_ODD_2 = DEPTH // 2

D_FOURIER = D_MODEL // 2
N_FOURIER_GROUPS = 4
FOURIER_GROUP_DIM = D_FOURIER // N_FOURIER_GROUPS

D_HYENA = D_MODEL // 2
HYENA_EMB_DIM = 33
HYENA_BANDS = (HYENA_EMB_DIM - 1) // 2
HYENA_FILTER_WIDTH = 64
HYENA_TARGET = 1e-2
HYENA_FAST_DECAY_PCT = 0.3
HYENA_SLOW_DECAY_PCT = 1.5
HYENA_MIN_DECAY = math.log(HYENA_TARGET) / HYENA_FAST_DECAY_PCT
HYENA_MAX_DECAY = math.log(HYENA_TARGET) / HYENA_SLOW_DECAY_PCT

MLA_HEADS = 16
Q_LORA_RANK = 256
KV_LORA_RANK = 128
QK_NOPE_DIM = 64
QK_ROPE_DIM = 32
V_HEAD_DIM = 64
QK_HEAD_DIM = QK_NOPE_DIM + QK_ROPE_DIM
ROPE_THETA = 10000.0
Q_BLOCK = 128

D_FF = 2816


def _f32(a):
    return a.astype(jnp.float32)

def _rms_norm(x, g):
    x32 = _f32(x)
    y = x32 * lax.rsqrt(jnp.mean(x32 * x32, axis=-1, keepdims=True) + EPS)
    return (y * _f32(g)).astype(x.dtype)

def _dwconv3(x, w, b):
    xp = jnp.pad(x, ((0, 0), (1, 1), (0, 0)))
    return xp[:, :-2] * w[0] + xp[:, 1:-1] * w[1] + xp[:, 2:] * w[2] + b

def _adaln(cond, w_mod, b_mod):
    mod = jax.nn.silu(cond) @ w_mod + b_mod
    return jnp.split(mod[:, None, :], 6, axis=-1)

def _modulate(h, shift, scale):
    return h * (1 + scale) + shift

def _hyena_filter_spectrum(L, w1, b1, w2, b2, w3, b3, w4, freq):
    pos = jnp.arange(L, dtype=jnp.float32)
    t = pos / max(L - 1, 1)
    bands = jnp.linspace(1e-4, HYENA_BANDS - 1, HYENA_BANDS, dtype=jnp.float32)
    ang = (2.0 * math.pi / L) * pos[:, None] * bands[None, :]
    z = jnp.concatenate([t[:, None], jnp.cos(ang), -jnp.sin(ang)], axis=-1)
    f = _f32(freq)
    h = jnp.sin(f * (z @ _f32(w1) + _f32(b1)))
    h = jnp.sin(f * (h @ _f32(w2) + _f32(b2)))
    h = jnp.sin(f * (h @ _f32(w3) + _f32(b3)))
    h = h @ _f32(w4)
    deltas = jnp.linspace(HYENA_MIN_DECAY, HYENA_MAX_DECAY, D_HYENA, dtype=jnp.float32)
    decay = jnp.exp(-t[:, None] * jnp.abs(deltas)[None, :])
    h_fwd = h[:, :D_HYENA] * decay
    h_bwd = h[:, D_HYENA:] * decay
    two_sided = jnp.concatenate([h_fwd, jnp.zeros((1, D_HYENA), jnp.float32), h_bwd[:0:-1]], axis=0)
    two_sided = two_sided / jnp.sum(jnp.abs(two_sided), axis=0, keepdims=True)
    return jnp.fft.rfft(two_sided, axis=0)

def _long_conv(u, spectrum, bias):
    L = u.shape[1]
    u32 = _f32(u)
    y = jnp.fft.irfft(jnp.fft.rfft(u32, n=2 * L, axis=1) * spectrum[None], n=2 * L, axis=1)[:, :L]
    return (y + u32 * _f32(bias)).astype(u.dtype)

def _fourier_hyena_mixer(h, w_in, w_out, conv_w, conv_b, w1, b1, w2, b2, w3, b3, w4, freq, hy_bias):
    B, L, _ = h.shape
    proj = h @ w_in
    u_f = _f32(proj[..., :D_FOURIER]).reshape(B, L, N_FOURIER_GROUPS, FOURIER_GROUP_DIM)
    y_f = jnp.fft.fft2(u_f, axes=(1, 3), norm='ortho').real.reshape(B, L, D_FOURIER).astype(h.dtype)
    u_h = _dwconv3(proj[..., D_FOURIER:], conv_w, conv_b)
    x0, x1, v = jnp.split(u_h, 3, axis=-1)
    spectrum = _hyena_filter_spectrum(L, w1, b1, w2, b2, w3, b3, w4, freq)
    y_h = x0 * _long_conv(v * x1, spectrum, hy_bias)
    return jnp.concatenate([y_f, y_h], axis=-1) @ w_out

def _rope_2d(x, rope):
    cos_r, sin_r, cos_c, sin_c = rope
    q4 = QK_ROPE_DIM // 4
    half = QK_ROPE_DIM // 2

    def rot(xa, cos, sin):
        x1, x2 = xa[..., :q4], xa[..., q4:]
        cos = cos[None, :, None, :]
        sin = sin[None, :, None, :]
        return jnp.concatenate([x1 * cos - x2 * sin, x1 * sin + x2 * cos], axis=-1)

    out = jnp.concatenate([rot(x[..., :half], cos_r, sin_r), rot(x[..., half:], cos_c, sin_c)], axis=-1)
    return out.astype(x.dtype)

def _mla_queries(a_q, q_a_norm, w_uq, q_norm, rope):
    B, L, _ = a_q.shape
    q = (_rms_norm(a_q, q_a_norm) @ w_uq).reshape(B, L, MLA_HEADS, QK_HEAD_DIM)
    q = _rms_norm(q, q_norm)
    if rope is not None:
        q = jnp.concatenate([q[..., :QK_NOPE_DIM], _rope_2d(q[..., QK_NOPE_DIM:], rope)], axis=-1)
    return q

def _mla_keys_values(a_kv, kv_a_norm, w_ukv, k_norm, rope):
    B, L, _ = a_kv.shape
    ckv = _rms_norm(a_kv[..., :KV_LORA_RANK], kv_a_norm)
    k_pe = a_kv[..., KV_LORA_RANK:]
    kv = (ckv @ w_ukv).reshape(B, L, MLA_HEADS, QK_NOPE_DIM + V_HEAD_DIM)
    k_nope, v = kv[..., :QK_NOPE_DIM], kv[..., QK_NOPE_DIM:]
    k_pe = jnp.broadcast_to(k_pe[:, :, None, :], (B, L, MLA_HEADS, QK_ROPE_DIM))
    k = _rms_norm(jnp.concatenate([k_nope, k_pe], axis=-1), k_norm)
    if rope is not None:
        k = jnp.concatenate([k[..., :QK_NOPE_DIM], _rope_2d(k[..., QK_NOPE_DIM:], rope)], axis=-1)
    return k, v

def _attend_blocks(q, k, v):
    B, S, H, Dq = q.shape
    nb = S // Q_BLOCK
    qb = q.reshape(B, nb, Q_BLOCK, H, Dq).transpose(1, 0, 2, 3, 4)
    scale = QK_HEAD_DIM ** -0.5

    def one(qblk):
        s = jnp.einsum('bqhd,bkhd->bhqk', qblk, k, preferred_element_type=jnp.float32) * scale
        p = jax.nn.softmax(s, axis=-1).astype(v.dtype)
        return jnp.einsum('bhqk,bkhv->bqhv', p, v)

    o = lax.map(one, qb)
    return o.transpose(1, 0, 2, 3, 4).reshape(B, S, H * V_HEAD_DIM)

def _conv_ffn(h, w_up, conv_w, conv_b, w_down):
    gate, val = jnp.split(h @ w_up, 2, axis=-1)
    return (jax.nn.silu(_dwconv3(gate, conv_w, conv_b)) * val) @ w_down

def second_inputs(seed: int = 0) -> dict:
    key = jax.random.key(seed)
    ks = iter(jax.random.split(key, 40))

    def nrm(shape, scale):
        return scale * jax.random.normal(next(ks), shape, jnp.float32)

    def gain(shape):
        return 1.0 + 0.02 * jax.random.normal(next(ks), shape, jnp.float32)

    D = D_MODEL
    return {
        'x': nrm((BATCH, SEQ, D), 1.0),
        'c': nrm((BATCH, D), 1.0),
        'ctx': nrm((BATCH, CTX_LEN, D), 1.0),
        'c_ctx': nrm((D,), 1.0),
        'norm1': gain((DEPTH, D)),
        'norm2': gain((DEPTH, D)),
        'w_mod': nrm((DEPTH, D, 6 * D), 0.5 * D ** -0.5),
        'b_mod': nrm((DEPTH, 6 * D), 0.01),
        'ffn_w_up': nrm((DEPTH, D, 2 * D_FF), D ** -0.5),
        'ffn_conv_w': nrm((DEPTH, 3, D_FF), 3 ** -0.5),
        'ffn_conv_b': nrm((DEPTH, D_FF), 0.01),
        'ffn_w_down': nrm((DEPTH, D_FF, D), D_FF ** -0.5),
        'fh_w_in': nrm((N_EVEN_2, D, D_FOURIER + 3 * D_HYENA), D ** -0.5),
        'fh_w_out': nrm((N_EVEN_2, D_FOURIER + D_HYENA, D), (D_FOURIER + D_HYENA) ** -0.5),
        'hy_conv_w': nrm((N_EVEN_2, 3, 3 * D_HYENA), 3 ** -0.5),
        'hy_conv_b': nrm((N_EVEN_2, 3 * D_HYENA), 0.01),
        'hy_filt_w1': nrm((N_EVEN_2, HYENA_EMB_DIM, HYENA_FILTER_WIDTH), HYENA_EMB_DIM ** -0.5),
        'hy_filt_b1': nrm((N_EVEN_2, HYENA_FILTER_WIDTH), 0.1),
        'hy_filt_w2': nrm((N_EVEN_2, HYENA_FILTER_WIDTH, HYENA_FILTER_WIDTH), HYENA_FILTER_WIDTH ** -0.5),
        'hy_filt_b2': nrm((N_EVEN_2, HYENA_FILTER_WIDTH), 0.1),
        'hy_filt_w3': nrm((N_EVEN_2, HYENA_FILTER_WIDTH, HYENA_FILTER_WIDTH), HYENA_FILTER_WIDTH ** -0.5),
        'hy_filt_b3': nrm((N_EVEN_2, HYENA_FILTER_WIDTH), 0.1),
        'hy_filt_w4': nrm((N_EVEN_2, HYENA_FILTER_WIDTH, 2 * D_HYENA), HYENA_FILTER_WIDTH ** -0.5),
        'hy_freq': gain((N_EVEN_2, HYENA_FILTER_WIDTH)),
        'hy_bias': nrm((N_EVEN_2, D_HYENA), 0.5),
        'mla_w_in': nrm((N_ODD_2, D, Q_LORA_RANK + KV_LORA_RANK + QK_ROPE_DIM), D ** -0.5),
        'mla_q_a_norm': gain((N_ODD_2, Q_LORA_RANK)),
        'mla_w_uq': nrm((N_ODD_2, Q_LORA_RANK, MLA_HEADS * QK_HEAD_DIM), Q_LORA_RANK ** -0.5),
        'mla_kv_a_norm': gain((N_ODD_2, KV_LORA_RANK)),
        'mla_w_ukv': nrm((N_ODD_2, KV_LORA_RANK, MLA_HEADS * (QK_NOPE_DIM + V_HEAD_DIM)), KV_LORA_RANK ** -0.5),
        'mla_q_norm': gain((N_ODD_2, QK_HEAD_DIM)),
        'mla_k_norm': gain((N_ODD_2, QK_HEAD_DIM)),
        'mla_w_o': nrm((N_ODD_2, MLA_HEADS * V_HEAD_DIM, D), (MLA_HEADS * V_HEAD_DIM) ** -0.5),
    }

def second_block(x, c, ctx, c_ctx, norm1, norm2, w_mod, b_mod, ffn_w_up, ffn_conv_w, ffn_conv_b, ffn_w_down,
              fh_w_in, fh_w_out, hy_conv_w, hy_conv_b, hy_filt_w1, hy_filt_b1, hy_filt_w2, hy_filt_b2,
              hy_filt_w3, hy_filt_b3, hy_filt_w4, hy_freq, hy_bias, mla_w_in, mla_q_a_norm, mla_w_uq,
              mla_kv_a_norm, mla_w_ukv, mla_q_norm, mla_k_norm, mla_w_o):
    L = x.shape[1]
    ROWS = L // GRID_W
    rows = jnp.broadcast_to(jnp.arange(ROWS, dtype=jnp.float32)[:, None], (ROWS, GRID_W)).reshape(-1)
    cols = jnp.broadcast_to(jnp.arange(GRID_W, dtype=jnp.float32)[None, :], (ROWS, GRID_W)).reshape(-1)
    n_freq = QK_ROPE_DIM // 4
    inv_freq = ROPE_THETA ** (-jnp.arange(n_freq, dtype=jnp.float32) / n_freq)
    ang_r = rows[:, None] * inv_freq[None, :]
    ang_c = cols[:, None] * inv_freq[None, :]
    rope = (jnp.cos(ang_r), jnp.sin(ang_r), jnp.cos(ang_c), jnp.sin(ang_c))

    for i in range(DEPTH):
        last = i == DEPTH - 1
        odd = i % 2 == 1
        j = i // 2
        sh1, sc1, g1, sh2, sc2, g2 = _adaln(c, w_mod[i], b_mod[i])
        hx = _modulate(_rms_norm(x, norm1[i]), sh1, sc1)
        if (not last) or odd:
            csh1, csc1, cg1, csh2, csc2, cg2 = _adaln(c_ctx[None, :], w_mod[i], b_mod[i])
            hc = _modulate(_rms_norm(ctx, norm1[i]), csh1, csc1)
        if not odd:
            fh = (fh_w_in[j], fh_w_out[j], hy_conv_w[j], hy_conv_b[j], hy_filt_w1[j], hy_filt_b1[j],
                  hy_filt_w2[j], hy_filt_b2[j], hy_filt_w3[j], hy_filt_b3[j], hy_filt_w4[j], hy_freq[j], hy_bias[j])
            yx = _fourier_hyena_mixer(hx, *fh)
            if not last:
                yc = _fourier_hyena_mixer(hc, *fh)
        else:
            w_in = mla_w_in[j]
            q_args = (mla_q_a_norm[j], mla_w_uq[j], mla_q_norm[j])
            kv_args = (mla_kv_a_norm[j], mla_w_ukv[j], mla_k_norm[j])
            a_x = hx @ w_in
            q_x = _mla_queries(a_x[..., :Q_LORA_RANK], *q_args, rope)
            k_x, v_x = _mla_keys_values(a_x[..., Q_LORA_RANK:], *kv_args, rope)
            a_c = hc @ (w_in if not last else w_in[:, Q_LORA_RANK:])
            k_c, v_c = _mla_keys_values(a_c[..., -(KV_LORA_RANK + QK_ROPE_DIM):], *kv_args, None)
            k_all = jnp.concatenate([k_x, k_c], axis=1)
            v_all = jnp.concatenate([v_x, v_c], axis=1)
            yx = _attend_blocks(q_x, k_all, v_all) @ mla_w_o[j]
            if not last:
                q_c = _mla_queries(a_c[..., :Q_LORA_RANK], *q_args, None)
                yc = _attend_blocks(q_c, k_c, v_c) @ mla_w_o[j]
        ffn = (ffn_w_up[i], ffn_conv_w[i], ffn_conv_b[i], ffn_w_down[i])
        x = x + g1 * yx
        x = x + g2 * _conv_ffn(_modulate(_rms_norm(x, norm2[i]), sh2, sc2), *ffn)
        if not last:
            ctx = ctx + cg1 * yc
            ctx = ctx + cg2 * _conv_ffn(_modulate(_rms_norm(ctx, norm2[i]), csh2, csc2), *ffn)
    return x


def setup_inputs(seed=0):
    out = dict(first_inputs(seed))
    for name, value in second_inputs(seed + 1).items():
        if name != "x":
            out[name + "_2"] = value
    return out


def reference(
    x, mem, a_ln, a_w_in, a_pool_w, a_pool_scale, a_conv_w, a_a_log, a_dt_bias, a_o_norm,
    a_w_out, c_ln, c_w_in, c_pe_k, c_w1_k, c_w2_k, c_pe_v, c_w1_v, c_w2_v, c_w_out, xa_ln,
    xa_mem_ln, xa_wq, xa_wk, xa_wv, xa_wo, ff_ln, ff_w1, ff_w2, final_ln, c_2, ctx_2, c_ctx_2,
    norm1_2, norm2_2, w_mod_2, b_mod_2, ffn_w_up_2, ffn_conv_w_2, ffn_conv_b_2, ffn_w_down_2,
    fh_w_in_2, fh_w_out_2, hy_conv_w_2, hy_conv_b_2, hy_filt_w1_2, hy_filt_b1_2, hy_filt_w2_2,
    hy_filt_b2_2, hy_filt_w3_2, hy_filt_b3_2, hy_filt_w4_2, hy_freq_2, hy_bias_2, mla_w_in_2,
    mla_q_a_norm_2, mla_w_uq_2, mla_kv_a_norm_2, mla_w_ukv_2, mla_q_norm_2, mla_k_norm_2,
    mla_w_o_2,
):
    x = first_block(
        x, mem, a_ln, a_w_in, a_pool_w, a_pool_scale, a_conv_w, a_a_log, a_dt_bias, a_o_norm,
        a_w_out, c_ln, c_w_in, c_pe_k, c_w1_k, c_w2_k, c_pe_v, c_w1_v, c_w2_v, c_w_out, xa_ln,
        xa_mem_ln, xa_wq, xa_wk, xa_wv, xa_wo, ff_ln, ff_w1, ff_w2, final_ln,
    )
    return second_block(
        x, c_2, ctx_2, c_ctx_2, norm1_2, norm2_2, w_mod_2, b_mod_2, ffn_w_up_2, ffn_conv_w_2,
        ffn_conv_b_2, ffn_w_down_2, fh_w_in_2, fh_w_out_2, hy_conv_w_2, hy_conv_b_2,
        hy_filt_w1_2, hy_filt_b1_2, hy_filt_w2_2, hy_filt_b2_2, hy_filt_w3_2, hy_filt_b3_2,
        hy_filt_w4_2, hy_freq_2, hy_bias_2, mla_w_in_2, mla_q_a_norm_2, mla_w_uq_2,
        mla_kv_a_norm_2, mla_w_ukv_2, mla_q_norm_2, mla_k_norm_2, mla_w_o_2,
    )


_drawn_inputs = setup_inputs


def setup_inputs(seed=0):
    import zlib

    import numpy as np

    out = dict(_drawn_inputs(seed))
    spreads = {}
    factors = {'c_ln': 3.558,
     'c_pe_k': 8.0,
     'c_pe_v': 2.957,
     'xa_ln': 8.0,
     'xa_mem_ln': 6.044,
     'ctx_2': 15.955,
     'norm1_2': 8.0,
     'norm2_2': 55.048,
     'b_mod_2': 3.789,
     'ffn_conv_b_2': 200.0,
     'hy_conv_b_2': 30.084,
     'hy_filt_b1_2': 8.0,
     'hy_filt_b2_2': 7.064,
     'hy_filt_b3_2': 5.722,
     'hy_freq_2': 8.0,
     'mla_q_a_norm_2': 200.0,
     'mla_kv_a_norm_2': 200.0,
     'mla_q_norm_2': 200.0,
     'mla_k_norm_2': 200.0}
    for name, (base, spread) in spreads.items():
        noise = np.random.default_rng([zlib.crc32(name.encode()), seed]).standard_normal(out[name].shape)
        drawn = base * np.exp(spread * noise) if base else spread * noise
        out[name] = jnp.asarray(drawn.astype(out[name].dtype))
    for name, factor in factors.items():
        out[name] = (out[name] * factor).astype(out[name].dtype)
    return out
```

```python
import math
from contextlib import ExitStack

import numpy as np

import concourse.bass as bass
import concourse.mybir as mybir

ACT = mybir.ActivationFunctionType
ALU = mybir.AluOpType
F32 = mybir.dt.float32
AX_X = mybir.AxisListType.X

P = 128
BANK = 512
BANKS = 8
D = 1024
KT = D // P
SEQ, MEM, CTX = 512, 256, 256
TOK = SEQ + CTX
TT = SEQ // P
EPS = 1e-6
SLOT = 4096
DN_HEADS, DN_CONV = 4, 4
POOL_WINDOWS = (2, 4, 8, 16)
FF_TILES = 4 * D // P
NSA_HEADS, NSA_GROUPS, NSA_DIM = 16, 4, 64
NSA_REP = NSA_HEADS // NSA_GROUPS
CMP_LEN, CMP_STRIDE = 32, 16
N_CMP = SEQ // CMP_STRIDE - CMP_LEN // CMP_STRIDE + 1
NEG = -1e30
XA_HEADS, XA_DIM = 4, 256
D_FF = 2816
FC = D_FF // P
HY_EMB, HY_WIDTH, HY_CH = 33, 64, 512
MLA_HEADS, MLA_NOPE, MLA_ROPE, MLA_V = 16, 64, 32, 64
MLA_QK = MLA_NOPE + MLA_ROPE
GRID_W = 64
ROUND = 1.5 * 2.0 ** 23
TWO_PI_HI = 6.28125
TWO_PI_LO = 2 * math.pi - TWO_PI_HI



def place(entries):
    at, n = {}, 0
    for name, width in entries:
        at[name] = (n, width)
        n += width
    return at, n


VECTORS, N_VECTORS = place([
    ("a_ln", 8), ("pool_scale", 4), ("conv_w", 4 * 12), ("c_ln", 8), ("xa_ln", 16), ("xa_mem_ln", 16), ("ff_ln", 16),
    ("final_ln", 8), ("norm1", 16), ("norm2", 16), ("b_mod", 96), ("ffn_conv_w", 2 * 3 * FC), ("ffn_conv_b", 2 * FC),
    ("hy_conv_w", 36), ("hy_conv_b", 12), ("hy_bias", 4), ("hy_b", 3), ("hy_freq", 1), ("q_a_norm", 2),
    ("kv_a_norm", 1), ("q_norm", 1), ("k_norm", 1), ("a_log", 4), ("dt_bias", 4), ("o_norm", P), ("cond", 16),
])
LEVELS = 7
CONSTS, N_CONSTS = place([
    ("ident", P), ("ones", P), ("upto", P), ("levels", LEVELS * P), ("strip", 31), ("cmp_rows", 1), ("not_first", 1),
    ("rope_swap", 32),
])


class Counter:

    def __init__(self, nc, ctx, name):
        self.sem = ctx.enter_context(nc.semaphore(name))
        self.base = 0

    def at(self, n):
        return self.sem, self.base + n


class Kernel:

    def __init__(self, nc, ctx, dram):
        self.nc, self.ctx, self.dram = nc, ctx, dram
        self.counters = {}
        self.plan, self.loaded = [], 0

        def sb(name, width):
            return ctx.enter_context(nc.sbuf_tensor(name, [P, width], F32))

        self.x_all = sb("x_all", KT * TOK)
        self.h_all = sb("h_all", KT * TOK)
        self.ring = sb("ring", 2 * SLOT)
        self.vec = sb("vec", N_VECTORS)
        self.const = sb("const", N_CONSTS)
        self.mods = sb("mods", 2 * 48 + 2 * 2 * 8)
        self.arena_size = 30240
        self.arena = sb("arena", self.arena_size)
        self.psum = ctx.enter_context(nc.psum_tensor("psum", [P, BANKS * BANK], F32))
        self.x = self.x_all[:, :].rearrange("p (k t) -> p k t", k=KT)
        self.h = self.h_all[:, :].rearrange("p (k t) -> p k t", k=KT)

    def counter(self, name):
        if name not in self.counters:
            self.counters[name] = Counter(self.nc, self.ctx, name)
        return self.counters[name]

    def v(self, name, i=0, n=None):
        at, width = VECTORS[name]
        return self.vec[:, at + i:at + (width if n is None else i + n)]

    def c(self, name, i=0, n=None):
        at, width = CONSTS[name]
        return self.const[:, at + i:at + (width if n is None else i + n)]

    def bank(self, b, n=BANK, parts=slice(0, P)):
        return self.psum[parts, b * BANK:b * BANK + n]

    def region(self, at, *shape):
        n = math.prod(shape)
        assert at + n <= self.arena_size, (at, shape)
        v = self.arena[:, at:at + n]
        names = " ".join("abcd"[:len(shape)])
        if len(shape) > 1:
            sizes = {c: s for c, s in zip("abcd", shape)}
            v = v.rearrange(f"p ({names}) -> p {names}", **sizes)
        return v

    def load_chunk(self, sp, w, chunk, slot):
        n = w["width"]
        src = w["ap"][bass.ds(chunk, 1)].rearrange("a p n -> p (a n)")
        sp.dma_start(self.ring[:, slot * SLOT:slot * SLOT + n], src).then_inc(self.counter(f"weights_landed_{slot}").sem, 16)

    def prefetch(self, sp):
        if self.loaded < len(self.plan):
            w = self.plan[self.loaded]
            if not w["ahead"]:
                for c in range(min(2, w["chunks"])):
                    self.load_chunk(sp, w, c, c)
                w["ahead"] = True


def weight(dram, name, kt, cols, chunks):
    return {"name": name, "ap": dram[name], "kt": kt, "cols": cols, "chunks": chunks, "width": kt * cols, "ahead": False}




def product(k, name, operand, groups, vector=None, scalar=None, loop=True, stationary="weight",
            tile=P):
    nc = k.nc
    w = k.plan[k.loaded]
    kt, cols, chunks = w["kt"], w["cols"], w["chunks"]
    mt = -(-cols // tile) if stationary == "weight" else 1
    tiles = mt * len(groups)
    in_body = 2 * tiles
    held = in_body if in_body <= BANKS else BANKS
    assert in_body % held == 0
    landed = [k.counter("weights_landed_0"), k.counter("weights_landed_1")]
    ready, drained = k.counter("product_ready"), k.counter("bank_drained")
    pairs = chunks // 2
    looped = pairs if loop and pairs >= 2 else 0

    def over_chunks(engine, body):
        if looped:
            with engine.Fori(0, looped) as i:
                body(i, 0)
                body(i, 1)
        for c in range(2 * looped, chunks):
            body(c // 2, c % 2)

    with nc.Block() as block:

        @block.sync
        def _(sp):
            if not w["ahead"]:
                for c in range(min(2, chunks)):
                    k.load_chunk(sp, w, c, c)
                w["ahead"] = True

            def refill(i, s):
                sp.wait_ge(*ready.at((i * 2 + s + 1) * tiles))
                k.load_chunk(sp, w, i * 2 + s + 2, s)

            if chunks > 2:
                rest = chunks - 2
                if rest >= 4:
                    with sp.Fori(0, rest // 2) as i:
                        refill(i, 0)
                        refill(i, 1)
                    if rest % 2:
                        refill(rest // 2, 0)
                else:
                    for c in range(rest):
                        refill(c // 2, c % 2)
            k.loaded += 1
            sp.wait_ge(*ready.at(chunks * tiles))
            k.prefetch(sp)

        @block.tensor
        def _(pe):
            def body(i, s):
                pe.wait_ge(*landed[s].at(i * 16 + 16))
                slot = k.ring[:, s * SLOT:s * SLOT + w["width"]].rearrange("p (k n) -> p k n", k=kt)
                for m in range(mt):
                    for g, (start, n) in enumerate(groups):
                        pos = s * tiles + m * len(groups) + g
                        pe.wait_ge(*drained.at(i * in_body + (pos - held + 1)))
                        width = min(tile, cols - m * tile)
                        for t in range(kt):
                            if stationary == "weight":
                                out = k.bank(pos % held, n, slice(0, width))
                                lhs, rhs = slot[:, t, m * tile:m * tile + width], operand(t, start, n)
                            else:
                                out = k.bank(pos % held, cols)
                                lhs, rhs = operand(t, start, n), slot[:, t, :]
                            mm = nc.tensor.matmul(out, lhs, rhs, start=(t == 0), stop=(t == kt - 1))
                        mm.then_inc(ready.sem, 1)

            over_chunks(pe, body)

        def finish(engine, take):
            def body(i, s):
                for m in range(mt):
                    for g, (start, n) in enumerate(groups):
                        pos = s * tiles + m * len(groups) + g
                        engine.wait_ge(*ready.at(i * in_body + pos + 1))
                        take(engine, i * 2 + s, m, g, k.bank(pos % held), i * in_body + pos)

            over_chunks(engine, body)

        if vector:
            @block.vector
            def _(dve):
                finish(dve, vector)

        if scalar:
            @block.scalar
            def _(act):
                finish(act, scalar)

    for s in range(2):
        landed[s].base += 16 * ((chunks + 1 - s) // 2)
    ready.base += chunks * tiles
    drained.base += chunks * tiles


def copy_out(k, dst):
    drained = k.counter("bank_drained")

    def take(act, chunk, m, g, bank, before):
        out = dst(chunk, m, g)
        act.activation(out, bank[0:out.shape[0], 0:out.shape[-1]], ACT.Copy).then_inc(drained.sem, 1)

    return take


def add_to_residual(k, mt, groups, gate=None):
    drained = k.counter("bank_drained")

    def take(dve, chunk, m, g, bank, before):
        start, n = groups[g]
        tile = chunk * mt + m
        x = k.x[:, bass.ds(tile, 1), start:start + n].rearrange("p a t -> p (a t)")
        if gate is None:
            dve.tensor_tensor(x, x, bank[:, 0:n], ALU.add).then_inc(drained.sem, 1)
        else:
            scale = gate[g][:, bass.ds(tile, 1)]
            dve.scalar_tensor_tensor(out=x, in0=bank[:, 0:n], scalar=scale, in1=x, op0=ALU.mult,
                                     op1=ALU.add).then_inc(drained.sem, 1)

    return take




def rms_norm(k, jobs, scratch, parts=P):
    nc = k.nc
    sq, rows = k.region(scratch, KT, BANK), k.region(scratch + KT * BANK, 4, BANK)
    squared, summed, guess = k.counter("norm_squared"), k.counter("norm_summed"), k.counter("norm_guess")
    a_step, v_step, scaled = k.counter("norm_act_step"), k.counter("norm_dve_step"), k.counter("norm_scaled")
    total = 0
    first_tiles = []
    for job in jobs:
        first_tiles.append(total)
        total += job[0]
    with nc.Block() as block:

        @block.sync
        def _(sp):
            k.prefetch(sp)

        @block.tensor
        def _(pe):
            for j, (tiles, n, src, dst, gain, shift, width) in enumerate(jobs):
                for t in range(tiles):
                    pe.wait_ge(*squared.at(first_tiles[j] + t + 1))
                    mm = nc.tensor.matmul(k.bank(j, n), k.c("ones"), sq[:, t, 0:n], start=(t == 0), stop=(t == tiles - 1))
                mm.then_inc(summed.sem, 1)

        @block.scalar
        def _(act):
            for j, (tiles, n, src, dst, gain, shift, width) in enumerate(jobs):
                if j:
                    act.wait_ge(*summed.at(j))
                for t in range(tiles):
                    nc.scalar.activation(sq[:, t, 0:n], src(t), ACT.Square).then_inc(squared.sem, 1)
                act.wait_ge(*summed.at(j + 1))
                if j:
                    act.wait_ge(*scaled.at(first_tiles[j]))
                nc.scalar.activation(rows[:, 0, 0:n], k.bank(j, n), ACT.Ln, scale=1.0 / width, bias=EPS).then_inc(a_step.sem, 1)
                act.wait_ge(*a_step.at(2 * j + 1))
                nc.scalar.activation(rows[:, 1, 0:n], rows[:, 0, 0:n], ACT.Exp, scale=-0.5).then_inc(a_step.sem, 1)
                act.wait_ge(*a_step.at(2 * j + 2))
                nc.scalar.activation(rows[:, 0, 0:n], rows[:, 1, 0:n], ACT.Square).then_inc(guess.sem, 1)
                if shift is not None:
                    for t in range(tiles):
                        act.wait_ge(*scaled.at(first_tiles[j] + t + 1))
                        nc.scalar.activation(dst(t), dst(t), ACT.Identity, bias=shift[:, t:t + 1])

        @block.vector
        def _(dve):
            for j, (tiles, n, src, dst, gain, shift, width) in enumerate(jobs):
                dve.wait_ge(*guess.at(j + 1))
                nc.vector.tensor_scalar(rows[:, 2, 0:n], k.bank(j, n), 1.0 / width, EPS, ALU.mult, ALU.add).then_inc(v_step.sem, 1)
                dve.wait_ge(*v_step.at(3 * j + 1))
                nc.vector.scalar_tensor_tensor(out=rows[:, 3, 0:n], in0=rows[:, 0, 0:n], scalar=-0.5, in1=rows[:, 2, 0:n],
                                               op0=ALU.mult, op1=ALU.mult).then_inc(v_step.sem, 1)
                dve.wait_ge(*v_step.at(3 * j + 2))
                nc.vector.scalar_tensor_tensor(out=rows[:, 2, 0:n], in0=rows[:, 3, 0:n], scalar=1.5, in1=rows[:, 1, 0:n],
                                               op0=ALU.add, op1=ALU.mult).then_inc(v_step.sem, 1)
                dve.wait_ge(*v_step.at(3 * j + 3))
                for t in range(tiles):
                    nc.vector.scalar_tensor_tensor(out=dst(t), in0=src(t), scalar=gain[:, t:t + 1], in1=rows[:, 2, 0:n],
                                                   op0=ALU.mult, op1=ALU.mult).then_inc(scaled.sem, 1)

    squared.base += total
    summed.base += len(jobs)
    guess.base += len(jobs)
    a_step.base += 2 * len(jobs)
    v_step.base += 3 * len(jobs)
    scaled.base += total


def norm_of(k, start, n, gain, shift=None):
    return (KT, n, lambda t: k.x[:, t, start:start + n], lambda t: k.h[:, t, start:start + n], gain, shift, D)




def attention(k, units, scores, blocks, value_matmuls, finish, scale, arena, score_width, gates=None, bias=None, mask=None):
    nc = k.nc
    sb_banks = -(-score_width // BANK)
    probs = k.region(arena, 2, score_width)
    turned = k.region(arena + 2 * score_width, 2, score_width)
    small = k.region(arena + 4 * score_width, 4, 4)
    at = arena + 4 * score_width + 16
    biased = k.region(at, 2, score_width) if bias else None
    turn_bank, out_bank = 2 * sb_banks, 2 * sb_banks + 2
    assert out_bank + 2 <= BANKS
    s_ready, s_biased, s_max, s_shift = (k.counter(n) for n in ("scores_ready", "scores_biased", "scores_max", "scores_shift"))
    p_ready, p_sum, p_norm = (k.counter(n) for n in ("probs_ready", "probs_inverse", "probs_normed"))
    t_ready, t_copied, o_ready, o_copied = (k.counter(n) for n in ("turned_ready", "turned_copied", "heads_ready", "heads_copied"))
    pv_done = k.counter("values_used")
    U = len(units)
    part_of = []
    for u in range(U):
        b = blocks(u)
        half = 4 if len(b) <= 4 else 3
        part_of.append([b[i:i + half] for i in range(0, len(b), half)])
    parts_before = [0]
    for p in part_of:
        parts_before.append(parts_before[-1] + len(p))
    closes_before = [0]
    for u in units:
        closes_before.append(closes_before[-1] + int(u["closes"]))
    heads = closes_before[-1]

    def score_ap(u):
        return k.psum[:, (u % 2) * sb_banks * BANK:(u % 2) * sb_banks * BANK + units[u]["keys"]]

    with nc.Block() as block:

        @block.sync
        def _(sp):
            k.prefetch(sp)

        @block.tensor
        def _(pe):
            def score(u):
                if u >= 2:
                    pe.wait_ge(*(s_biased if bias else p_ready).at(u - 1))
                for cols, lhs, rhs, first, last in scores(u):
                    base = (u % 2) * sb_banks * BANK
                    mm = nc.tensor.matmul(k.psum[:, base + cols.start:base + cols.stop], lhs, rhs, start=first, stop=last)
                mm.then_inc(s_ready.sem, 1)

            def turn(u):
                pe.wait_ge(*p_norm.at(u + 1))
                for i, part in enumerate(part_of[u]):
                    n = parts_before[u] + i
                    if n >= 2:
                        pe.wait_ge(*t_copied.at(n - 1))
                    for j, (col, width) in enumerate(part):
                        mm = nc.tensor.transpose(k.bank(turn_bank + n % 2)[0:width, j * P:(j + 1) * P],
                                                 probs[:, u % 2, col:col + width], k.c("ident"))
                    mm.then_inc(t_ready.sem, 1)

            def values(u):
                pe.wait_ge(*t_copied.at(parts_before[u + 1]))
                h = closes_before[u]
                if units[u]["opens"] and h >= 2:
                    pe.wait_ge(*o_copied.at(h - 1))
                listed = value_matmuls(u, turned[:, u % 2, :])
                for rows, cols, lhs, rhs, first, last in listed:
                    mm = nc.tensor.matmul(k.bank(out_bank + h % 2)[rows, cols], lhs, rhs, start=first, stop=last)
                mm.then_inc(pv_done.sem, 1)

            for step in range(U + 2):
                if step < U:
                    score(step)
                if 1 <= step <= U:
                    turn(step - 1)
                if step >= 2:
                    values(step - 2)

        @block.scalar
        def _(act):
            def exponentials(u):
                n = units[u]["keys"]
                act.wait_ge(*s_shift.at(u + 1))
                if u >= 2:
                    act.wait_ge(*t_ready.at(parts_before[u - 1]))
                src = biased[:, u % 2, 0:n] if bias else score_ap(u)
                nc.scalar.activation(probs[:, u % 2, 0:n], src, ACT.Exp, scale=scale, bias=small[:, 1, u % 4:u % 4 + 1],
                                     accum_out=small[:, 2, u % 4:u % 4 + 1]).then_inc(p_ready.sem, 1)

            def copy_turned(u):
                if u >= 2:
                    act.wait_ge(*pv_done.at(u - 1))
                col = 0
                for i, part in enumerate(part_of[u]):
                    n = parts_before[u] + i
                    act.wait_ge(*t_ready.at(n + 1))
                    rows, width = part[0][1], len(part) * P
                    nc.scalar.activation(turned[0:rows, u % 2, col:col + width],
                                         k.bank(turn_bank + n % 2)[0:rows, 0:width], ACT.Copy).then_inc(t_copied.sem, 1)
                    col += width

            for step in range(U + 1):
                if step < U:
                    exponentials(step)
                if step >= 1:
                    copy_turned(step - 1)

        @block.vector
        def _(dve):
            def maximum(u):
                n = units[u]["keys"]
                dve.wait_ge(*s_ready.at(u + 1))
                src = score_ap(u)
                if bias:
                    table, factor = bias(u)
                    if u >= 2:
                        dve.wait_ge(*p_ready.at(u - 1))
                    nc.vector.scalar_tensor_tensor(out=biased[:, u % 2, 0:n], in0=table, scalar=factor, in1=src,
                                                   op0=ALU.mult, op1=ALU.add).then_inc(s_biased.sem, 1)
                    dve.wait_ge(*s_biased.at(u + 1))
                    src = biased[:, u % 2, 0:n]
                nc.vector.tensor_reduce(small[:, 0, u % 4:u % 4 + 1], src, AX_X, ALU.max).then_inc(s_max.sem, 1)
                dve.wait_ge(*s_max.at(u + 1))
                nc.vector.tensor_scalar(small[:, 1, u % 4:u % 4 + 1], small[:, 0, u % 4:u % 4 + 1], -scale, None,
                                        ALU.mult).then_inc(s_shift.sem, 1)

            def normalise(u):
                n = units[u]["keys"]
                dve.wait_ge(*p_ready.at(u + 1))
                nc.vector.reciprocal(small[:, 3, u % 4:u % 4 + 1], small[:, 2, u % 4:u % 4 + 1]).then_inc(p_sum.sem, 1)
                dve.wait_ge(*p_sum.at(u + 1))
                second = gates(u) if gates else None
                nc.vector.tensor_scalar(probs[:, u % 2, 0:n], probs[:, u % 2, 0:n], small[:, 3, u % 4:u % 4 + 1], second,
                                        ALU.mult, ALU.mult if gates else ALU.bypass).then_inc(p_norm.sem, 1)

            def copy_head(u):
                if units[u]["closes"]:
                    dve.wait_ge(*pv_done.at(u + 1))
                    dst, rows, cols = finish(u)
                    src = k.bank(out_bank + closes_before[u] % 2)[rows, cols]
                    if len(dst.shape) == 3:
                        src = src.rearrange("p (a t) -> p a t", a=dst.shape[1])
                    nc.vector.tensor_copy(dst, src).then_inc(o_copied.sem, 1)

            for step in range(U + 3):
                if step < U:
                    maximum(step)
                if 1 <= step <= U:
                    normalise(step - 1)
                if step >= 3:
                    copy_head(step - 3)

    for s in (s_ready, s_max, s_shift, p_ready, p_sum, p_norm, pv_done) + ((s_biased,) if bias else ()):
        s.base += U
    t_ready.base += parts_before[-1]
    t_copied.base += parts_before[-1]
    o_copied.base += heads




class Chain:

    def __init__(self, engine, counter):
        self.engine, self.count, self.n = engine, counter, 0

    def __call__(self, instruction):
        self.n += 1
        instruction.then_inc(self.count.sem, 1)
        self.engine.wait_ge(*self.count.at(self.n))


def load(k, pairs):
    landed = k.counter("operands_landed")
    with k.nc.Block() as block:

        @block.sync
        def _(sp):
            for dst, src in pairs:
                sp.dma_start(dst, src).then_inc(landed.sem, 16)
            sp.wait_ge(*landed.at(16 * len(pairs)))
            k.prefetch(sp)

    landed.base += 16 * len(pairs)


def flat(ap):
    names = "bcd"[:len(ap.shape) - 1]
    return ap.rearrange(f"a {' '.join(names)} -> a ({' '.join(names)})")


def conv_taps(dve, step, out, src, taps, bias, reach, starts, n):
    for j, (tap, r) in enumerate(zip(taps, reach)):
        if j == 0:
            if bias is None:
                step(dve.tensor_scalar(out[:, 0:n], src[:, 0:n], tap, None, ALU.mult))
            else:
                step(dve.tensor_scalar(out[:, 0:n], src[:, 0:n], tap, bias, ALU.mult, ALU.add))
        else:
            o = out[:, max(0, -r):n - max(0, r)]
            s = src[:, max(0, r):n - max(0, -r)]
            step(dve.scalar_tensor_tensor(out=o, in0=s, scalar=tap, in1=o, op0=ALU.mult, op1=ALU.add))




def pool_delta_inputs(k, U, QKV, G):
    nc = k.nc
    drained, step, convolved = k.counter("bank_drained"), k.counter("conv_step"), k.counter("conv_ready")
    done = {"n": 0}
    count = [0]

    def take(dve, chunk, m, g, bank, before):
        tile = chunk * 4 + m
        if tile < 4:
            dve.tensor_copy(U[:, tile, :], bank[:, 0:SEQ]).then_inc(drained.sem, 1)
            return
        j = tile - 4
        out = QKV[:, j, :]
        taps = [k.v("conv_w", tap * 12 + j, 1) for tap in range(DN_CONV)]

        def chained(ins):
            count[0] += 1
            ins.then_inc(step.sem, 1)
            dve.wait_ge(*step.at(count[0]))

        conv_taps(dve, chained, out, bank, taps[::-1], None, [0, -1, -2, -3], None, SEQ)
        dve.sem_inc(drained.sem, 1)
        dve.sem_inc(convolved.sem, 1)

    def silu(act, chunk, m, g, bank, before):
        tile = chunk * 4 + m
        if tile >= 4:
            act.wait_ge(*convolved.at(tile - 3))
            act.activation(QKV[:, tile - 4, :], QKV[:, tile - 4, :], ACT.Silu)

    product(k, "a_w_in", lambda t, s, n: k.h[:, t, s:s + n], [(0, SEQ)], vector=take, scalar=silu, loop=False)
    step.base += count[0]
    convolved.base += 12

    def gate(act, chunk, m, g, bank, before):
        act.activation(G[:, g, :], bank[:, 0:512], ACT.Silu).then_inc(drained.sem, 1)

    product(k, "a_w_gate", lambda t, s, n: k.h[:, t, s:s + n], [(i * P, P) for i in range(TT)], scalar=gate,
            stationary="tokens")


def delta_gates(k, wba, beta, ld, gcol, tmp):
    nc = k.nc
    made, a_step, v_step = k.counter("gates_product"), k.counter("gates_act"), k.counter("gates_dve")
    z, az, e, l, ea, eb = (tmp[:, i * 16:(i + 1) * 16] for i in range(6))
    ba = k.bank(0, 32).rearrange("p (t c) -> p t c", t=TT)

    def by_head(ap):
        return ap.rearrange("p (t h) -> p t h", t=TT)

    with nc.Block() as block:

        @block.sync
        def _(sp):
            k.prefetch(sp)

        @block.tensor
        def _(pe):
            for t in range(TT):
                for kt in range(KT):
                    mm = nc.tensor.matmul(k.bank(0)[:, t * 8:t * 8 + 8], k.h[:, kt, t * P:(t + 1) * P], wba[:, kt, :],
                                          start=(kt == 0), stop=(kt == KT - 1))
            mm.then_inc(made.sem, 1)
            pe.wait_ge(*v_step.at(12))
            nc.tensor.matmul(k.bank(1, 16), k.c("upto"), ld, start=True, stop=True).then_inc(made.sem, 1)

        @block.scalar
        def _(act):
            step = Chain(act, a_step)
            act.wait_ge(*made.at(1))
            step(nc.scalar.activation(by_head(eb), ba[:, :, 0:4], ACT.Exp, scale=-1.0))
            step(nc.scalar.activation(ea[:, 0:4], k.v("a_log"), ACT.Exp))
            act.wait_ge(*v_step.at(5))
            step(nc.scalar.activation(e, az, ACT.Exp, scale=-1.0))
            step(nc.scalar.activation(l, e, ACT.Ln, bias=1.0))

        @block.vector
        def _(dve):
            step = Chain(dve, v_step)
            dve.wait_ge(*a_step.at(2))
            for t in range(TT):
                step(nc.vector.tensor_tensor(by_head(z)[:, t, :], ba[:, t, 4:8], k.v("dt_bias"), ALU.add))
            step(nc.vector.scalar_tensor_tensor(out=az, in0=z, scalar=-1.0, in1=z, op0=ALU.mult, op1=ALU.max))
            step(nc.vector.tensor_scalar(eb, eb, 1.0, None, ALU.add))
            step(nc.vector.reciprocal(beta, eb))
            dve.wait_ge(*a_step.at(4))
            step(nc.vector.scalar_tensor_tensor(out=z, in0=z, scalar=0.0, in1=l, op0=ALU.max, op1=ALU.add))
            for t in range(TT):
                step(nc.vector.scalar_tensor_tensor(out=by_head(ld)[:, t, :], in0=by_head(z)[:, t, :], scalar=-1.0,
                                                    in1=ea[:, 0:4], op0=ALU.mult, op1=ALU.mult))
            dve.wait_ge(*made.at(2))
            step(nc.vector.tensor_copy(gcol, k.bank(1, 16)))

    made.base += 2
    a_step.base += 4
    v_step.base += 13


def pool_branch(k, U, pool_w, tmp):
    nc = k.nc
    v_step, made, meaned = k.counter("pool_step"), k.counter("pool_product"), k.counter("pool_mean")
    work = tmp[:, 0:2 * BANK].rearrange("p (a t) -> p a t", a=2)
    inv = tmp[:, 2 * BANK:6 * BANK].rearrange("p (g t) -> p g t", g=4)
    mean = tmp[:, 6 * BANK:10 * BANK].rearrange("p (g t) -> p g t", g=4)
    n_steps = [0]
    with nc.Block() as block:

        @block.sync
        def _(sp):
            k.prefetch(sp)

        @block.vector
        def _(dve):
            step = Chain(dve, v_step)
            for g, window in enumerate(POOL_WINDOWS):
                src, r, b = U[:, g, :], 1, 0
                while r < window:
                    out = work[:, b, :]
                    step(nc.vector.tensor_copy(out[:, 0:r], src[:, 0:r]))
                    step(nc.vector.tensor_tensor(out[:, r:SEQ], src[:, r:SEQ], src[:, 0:SEQ - r], ALU.add))
                    src, r, b = out, 2 * r, 1 - b
                step(nc.vector.tensor_tensor(mean[:, g, :], src, inv[:, g, :], ALU.mult))
                nc.vector.tensor_tensor(mean[:, g, :], mean[:, g, :], U[:, g, :], ALU.subtract).then_inc(meaned.sem, 1)
            n_steps[0] = step.n

        @block.tensor
        def _(pe):
            for g in range(4):
                pe.wait_ge(*meaned.at(g + 1))
                nc.tensor.matmul(k.bank(g), pool_w[:, g, :], mean[:, g, :], start=True, stop=True).then_inc(made.sem, 1)

        @block.scalar
        def _(act):
            for g in range(4):
                act.wait_ge(*made.at(g + 1))
                nc.scalar.activation(k.h[:, g, 0:SEQ], k.bank(g), ACT.Copy, scale=k.v("pool_scale", g, 1))

    v_step.base += n_steps[0]
    made.base += 4
    meaned.base += 4


def inverse_rows(k, tiles, heads, squares, rows, n_list, src_rows=P, scale=1.0, sel=None):
    nc = k.nc
    squared, summed = k.counter("rows_squared"), k.counter("rows_summed")
    a_step, v_step = k.counter("rows_act"), k.counter("rows_dve")
    strip = k.c("strip")
    nb = len(n_list)
    with nc.Block() as block:

        @block.sync
        def _(sp):
            k.prefetch(sp)

        @block.scalar
        def _(act):
            for j in range(heads):
                if j >= 2:
                    act.wait_ge(*summed.at(nb * (j - 1)))
                o = 0
                for n in n_list:
                    nc.scalar.activation(squares[0:src_rows, j % 2, o:o + n], tiles(j)[:, o:o + n], ACT.Square).then_inc(squared.sem, 1)
                    o += n
            step = Chain(act, a_step)
            act.wait_ge(*summed.at(nb * heads))
            o = 0
            for b, n in enumerate(n_list):
                step(nc.scalar.activation(rows[0:heads, 0, o:o + n], k.bank(b, n, slice(0, heads)), ACT.Ln, scale=scale, bias=EPS))
                step(nc.scalar.activation(rows[0:heads, 1, o:o + n], rows[0:heads, 0, o:o + n], ACT.Exp, scale=-0.5))
                step(nc.scalar.activation(rows[0:heads, 0, o:o + n], rows[0:heads, 1, o:o + n], ACT.Square))
                o += n

        @block.tensor
        def _(pe):
            for j in range(heads):
                o = 0
                for b, n in enumerate(n_list):
                    pe.wait_ge(*squared.at(nb * j + b + 1))
                    nc.tensor.matmul(k.bank(b, n, slice(0, heads)), strip[0:src_rows, 15 - j:15 - j + heads],
                                     squares[0:src_rows, j % 2, o:o + n], start=(j == 0), stop=(j == heads - 1)).then_inc(summed.sem, 1)
                    o += n

        @block.vector
        def _(dve):
            step = Chain(dve, v_step)
            o = 0
            for b, n in enumerate(n_list):
                dve.wait_ge(*a_step.at(3 * b + 3))
                r = [rows[0:heads, i, o:o + n] for i in range(4)]
                step(nc.vector.tensor_scalar(r[2], k.bank(b, n, slice(0, heads)), scale, EPS, ALU.mult, ALU.add))
                step(nc.vector.scalar_tensor_tensor(out=r[3], in0=r[0], scalar=-0.5, in1=r[2], op0=ALU.mult, op1=ALU.mult))
                step(nc.vector.scalar_tensor_tensor(out=r[2], in0=r[3], scalar=1.5, in1=r[1], op0=ALU.add, op1=ALU.mult))
                o += n

    squared.base += nb * heads
    summed.base += nb * heads
    a_step.base += 3 * nb
    v_step.base += 3 * nb
    return rows[:, 2, :]


def spread_rows(k, rows, jobs):
    nc = k.nc
    made, used = k.counter("spread_ready"), k.counter("spread_used")
    with nc.Block() as block:

        @block.sync
        def _(sp):
            k.prefetch(sp)

        @block.tensor
        def _(pe):
            for i, (j, heads, parts, start, n, outs) in enumerate(jobs):
                if i >= BANKS:
                    pe.wait_ge(*used.at(i - BANKS + 1))
                lhs = k.c("ident")[0:heads, j:j + 1].to_broadcast([heads, parts])
                nc.tensor.matmul(k.bank(i % BANKS, n, slice(0, parts)), lhs, rows[0:heads, start:start + n],
                                 start=True, stop=True).then_inc(made.sem, 1)

        @block.vector
        def _(dve):
            for i, (j, heads, parts, start, n, outs) in enumerate(jobs):
                dve.wait_ge(*made.at(i + 1))
                for dst, src, factor in outs:
                    lo = dst[1]
                    bank = k.bank(i % BANKS, n, slice(lo, lo + dst[0].shape[0]))
                    op = nc.vector.scalar_tensor_tensor(out=dst[0], in0=bank, scalar=factor, in1=src,
                                                        op0=ALU.mult, op1=ALU.mult)
                op.then_inc(used.sem, 1)

    made.base += len(jobs)
    used.base += len(jobs)


def delta_rule(k, QKV, beta, ld, gcol, col, A, attn, kdec, kbg, vb, dec, erow, Xi, XT, Aoff, WTs, G):
    nc = k.nc
    Q, K, V = QKV[:, 0:4, :], QKV[:, 4:8, :], QKV[:, 8:12, :]
    units = [(c, h) for c in range(TT) for h in range(DN_HEADS)]
    S2 = k.counter
    a, v, p = S2("delta_act"), S2("delta_dve"), S2("delta_pe")
    egc, ekd, ebg, ngc = (col[:, i * 16:(i + 1) * 16] for i in range(4))
    ldb = WTs

    def u128(ap, j):
        return ap[:, j * P:(j + 1) * P]

    with nc.Block() as block:

        @block.gpsimd
        def _(pool):
            for j in range(16):
                op = nc.gpsimd.tensor_copy(u128(ldb, j), ld[:, j:j + 1].to_broadcast([P, P]))
            op.then_inc(v.sem, 1)

        @block.tensor
        def _(pe):
            pe.wait_ge(*v.at(1))
            for j in range(16):
                mm = nc.tensor.matmul(k.psum[:, j * P:(j + 1) * P], u128(ldb, j), k.c("upto"), start=True, stop=True)
            mm.then_inc(p.sem, 1)

        @block.vector
        def _(dve):
            dve.wait_ge(*a.at(1))
            for j in range(16):
                g = gcol[:, j:j + 1]
                row = k.psum[:, j * P:(j + 1) * P]
                nc.vector.tensor_scalar(u128(dec, j), row, g, 0.0, ALU.subtract, ALU.max)
                nc.vector.tensor_scalar(u128(Xi, j), row, g, 0.0, ALU.subtract, ALU.min)
                op = nc.vector.tensor_tensor(ekd[:, j:j + 1], row[:, P - 1:P], g, ALU.subtract)
            op.then_inc(S2("delta_diff").sem, 1)

        @block.scalar
        def _(act):
            act.wait_ge(*p.at(1))
            nc.scalar.activation(egc, gcol, ACT.Exp)
            nc.scalar.activation(erow[:, :], k.psum[:, 0:16 * P], ACT.Exp).then_inc(a.sem, 1)
            act.wait_ge(*S2("delta_diff").at(1))
            nc.scalar.activation(dec[:, :], dec[:, :], ACT.Exp, scale=-1.0)
            nc.scalar.activation(Xi[:, :], Xi[:, :], ACT.Exp)
            nc.scalar.activation(ekd, ekd, ACT.Exp)

    v.base += 1
    p.base += 1
    a.base += 1
    S2("delta_diff").base += 1

    with nc.Block() as block:

        @block.tensor
        def _(pe):
            for n in range(8):
                c = n % 4
                for h in range(4):
                    rhs = (K if n < 4 else Q)[:, h, c * P:(c + 1) * P]
                    mm = nc.tensor.matmul(k.bank(n)[:, h * P:(h + 1) * P], K[:, h, c * P:(c + 1) * P], rhs, start=True, stop=True)
                mm.then_inc(p.sem, 1)

        @block.vector
        def _(dve):
            dve.tensor_tensor(ebg, beta, egc, ALU.mult)
            for c in range(4):
                dve.wait_ge(*p.at(c + 1))
                for h in range(4):
                    j = c * 4 + h
                    nc.vector.scalar_tensor_tensor(out=u128(A, j), in0=k.bank(c)[:, h * P:(h + 1) * P], scalar=beta[:, j:j + 1],
                                                   in1=u128(dec, j), op0=ALU.mult, op1=ALU.mult)
            for c in range(4):
                dve.wait_ge(*p.at(c + 5))
                op = nc.vector.tensor_tensor(attn[:, c * 512:(c + 1) * 512], k.bank(4 + c), Xi[:, c * 512:(c + 1) * 512], ALU.mult)
                op.then_inc(v.sem, 1)
                dve.wait_ge(*v.at(c + 1))
                for h in range(4):
                    j = c * 4 + h
                    nc.vector.tensor_tensor(u128(attn, j), u128(attn, j), k.c("upto"), ALU.mult)

        @block.gpsimd
        def _(pool):
            pool.wait_ge(*p.at(8))
            for c in range(4):
                for h in range(4):
                    q = Q[:, h, c * P:(c + 1) * P]
                    nc.gpsimd.tensor_tensor(q, q, u128(erow, c * 4 + h), ALU.mult)

    p.base += 8
    v.base += 4

    with nc.Block() as block:

        @block.tensor
        def _(pe):
            for n in range(8):
                c = n % 4
                for h in range(4):
                    src = (K if n < 4 else V)[:, h, c * P:(c + 1) * P]
                    mm = nc.tensor.transpose(k.bank(n)[:, h * P:(h + 1) * P], src, k.c("ident"))
                mm.then_inc(p.sem, 1)

        @block.vector
        def _(dve):
            for c in range(4):
                dve.wait_ge(*p.at(c + 1))
                for h in range(4):
                    j = c * 4 + h
                    src = k.bank(c)[:, h * P:(h + 1) * P]
                    nc.vector.tensor_scalar(u128(kbg, j), src, ebg[:, j:j + 1], None, ALU.mult)
                    op = nc.vector.tensor_scalar(u128(kdec, j), src, ekd[:, j:j + 1], None, ALU.mult)

        @block.scalar
        def _(act):
            for c in range(4):
                act.wait_ge(*p.at(c + 5))
                for h in range(4):
                    j = c * 4 + h
                    nc.scalar.activation(u128(vb, j), k.bank(4 + c)[:, h * P:(h + 1) * P], ACT.Copy, scale=beta[:, j:j + 1])

        @block.gpsimd
        def _(pool):
            for j in range(16):
                nc.gpsimd.tensor_copy(u128(Xi, j), k.c("ident"))
                nc.gpsimd.tensor_copy(u128(XT, j), k.c("ident"))

    p.base += 8

    masked, turned, joined, copied = (S2(n) for n in ("level_masked", "level_turned", "level_joined", "level_copied"))
    updated = S2("level_updated")
    with nc.Block() as block:

        @block.gpsimd
        def _(pool):
            for level in range(LEVELS):
                mask = k.c("levels", level * P, P)
                for c in range(4):
                    if level:
                        pool.wait_ge(*turned.at(4 * (level - 1) + c + 1))
                    for h in range(4):
                        op = nc.gpsimd.tensor_tensor(u128(Aoff, c * 4 + h), u128(A, c * 4 + h), mask, ALU.mult)
                    op.then_inc(masked.sem, 1)

        @block.tensor
        def _(pe):
            for level in range(LEVELS):
                for c in range(4):
                    n = 4 * level + c
                    pe.wait_ge(*masked.at(n + 1))
                    if level:
                        pe.wait_ge(*updated.at(n - 3))
                    b = 3 * (c % 2)
                    if n >= 2:
                        pe.wait_ge(*copied.at(n - 1))
                    for h in range(4):
                        j = c * 4 + h
                        mm = nc.tensor.matmul(k.bank(b)[:, h * P:(h + 1) * P], u128(Aoff, j), u128(XT, j), start=True, stop=True)
                    mm.then_inc(turned.sem, 1)
                    pe.wait_ge(*copied.at(n + 1))
                    if n >= 2:
                        pe.wait_ge(*updated.at(n - 1))
                    for h in range(4):
                        j = c * 4 + h
                        nc.tensor.matmul(k.bank(b + 1)[:, h * P:(h + 1) * P], u128(WTs, j), u128(Xi, j), start=True, stop=True)
                        mm = nc.tensor.matmul(k.bank(b + 2)[:, h * P:(h + 1) * P], u128(Xi, j), u128(WTs, j), start=True, stop=True)
                    mm.then_inc(joined.sem, 1)

        @block.scalar
        def _(act):
            for level in range(LEVELS):
                for c in range(4):
                    n = 4 * level + c
                    act.wait_ge(*turned.at(n + 1))
                    nc.scalar.activation(WTs[:, c * 512:(c + 1) * 512], k.bank(3 * (c % 2)), ACT.Copy).then_inc(copied.sem, 1)

        @block.vector
        def _(dve):
            for level in range(LEVELS):
                for c in range(4):
                    n = 4 * level + c
                    dve.wait_ge(*joined.at(n + 1))
                    b = 3 * (c % 2)
                    x, xt = Xi[:, c * 512:(c + 1) * 512], XT[:, c * 512:(c + 1) * 512]
                    nc.vector.tensor_tensor(x, x, k.bank(b + 1), ALU.subtract)
                    nc.vector.tensor_tensor(xt, xt, k.bank(b + 2), ALU.subtract).then_inc(updated.sem, 1)

    for s in (masked, turned, joined, copied, updated):
        s.base += 4 * LEVELS

    wT, u_ = A, dec
    with nc.Block() as block:

        @block.tensor
        def _(pe):
            for c in range(4):
                for h in range(4):
                    j = c * 4 + h
                    nc.tensor.matmul(k.bank(2 * c)[:, h * P:(h + 1) * P], u128(kbg, j), u128(XT, j), start=True, stop=True)
                    mm = nc.tensor.matmul(k.bank(2 * c + 1)[:, h * P:(h + 1) * P], u128(XT, j), u128(vb, j), start=True, stop=True)
                mm.then_inc(p.sem, 1)

        @block.vector
        def _(dve):
            for c in range(4):
                dve.wait_ge(*p.at(c + 1))
                nc.vector.tensor_copy(wT[:, c * 512:(c + 1) * 512], k.bank(2 * c))

        @block.scalar
        def _(act):
            for c in range(4):
                act.wait_ge(*p.at(c + 1))
                nc.scalar.activation(u_[:, c * 512:(c + 1) * 512], k.bank(2 * c + 1), ACT.Copy)

    p.base += 4

    state = Xi[:, 0:1024].rearrange("p (b n) -> p b n", b=2)
    vnew = Xi[:, 1024:2048].rearrange("p (b n) -> p b n", b=2)
    O = kbg
    inner, outer, news, states, outs = (S2(n) for n in ("scan_inner", "scan_outer", "scan_new", "scan_state", "scan_out"))
    with nc.Block() as block:

        @block.tensor
        def _(pe):
            for c in range(4):
                if c:
                    pe.wait_ge(*states.at(c))
                    for h in range(4):
                        mm = nc.tensor.matmul(k.bank(0)[:, h * P:(h + 1) * P], u128(wT, c * 4 + h), state[:, (c - 1) % 2, h * P:(h + 1) * P],
                                              start=True, stop=True)
                    mm.then_inc(inner.sem, 1)
                pe.wait_ge(*news.at(c + 1))
                if c >= 2:
                    pe.wait_ge(*outs.at(c - 1))
                for h in range(4):
                    j = c * 4 + h
                    out = k.bank(2 + c % 2)[:, h * P:(h + 1) * P]
                    if c:
                        nc.tensor.matmul(out, Q[:, h, c * P:(c + 1) * P], state[:, (c - 1) % 2, h * P:(h + 1) * P], start=True, stop=False)
                    nc.tensor.matmul(out, u128(attn, j), vnew[:, c % 2, h * P:(h + 1) * P], start=(c == 0), stop=True)
                    mm = nc.tensor.matmul(k.bank(1)[:, h * P:(h + 1) * P], u128(kdec, j), vnew[:, c % 2, h * P:(h + 1) * P],
                                          start=True, stop=True)
                mm.then_inc(outer.sem, 1)

        @block.vector
        def _(dve):
            for c in range(4):
                u = u_[:, c * 512:(c + 1) * 512]
                if c:
                    dve.wait_ge(*inner.at(c))
                    nc.vector.tensor_tensor(vnew[:, c % 2, :], u, k.bank(0), ALU.subtract).then_inc(news.sem, 1)
                else:
                    nc.vector.tensor_copy(vnew[:, 0, :], u).then_inc(news.sem, 1)
                dve.wait_ge(*outer.at(c + 1))
                if c == 3:
                    break
                if c:
                    for h in range(4):
                        j = c * 4 + h
                        left = erow[:, j * P + P - 1:j * P + P]
                        op = nc.vector.scalar_tensor_tensor(
                            out=state[:, c % 2, h * P:(h + 1) * P], in0=state[:, (c - 1) % 2, h * P:(h + 1) * P],
                            scalar=left, in1=k.bank(1)[:, h * P:(h + 1) * P], op0=ALU.mult, op1=ALU.add)
                else:
                    op = nc.vector.tensor_copy(state[:, 0, :], k.bank(1))
                op.then_inc(states.sem, 1)

        @block.scalar
        def _(act):
            for c in range(4):
                act.wait_ge(*outer.at(c + 1))
                nc.scalar.activation(O[:, c * 512:(c + 1) * 512], k.bank(2 + c % 2), ACT.Copy).then_inc(outs.sem, 1)

    inner.base += 3
    outer.base += 4
    news.base += 4
    states.base += 3
    outs.base += 4

    sums, y = col[:, 64:80], col[:, 80:144]
    sq = kdec
    with nc.Block() as block:

        @block.scalar
        def _(act):
            nc.scalar.activation(sq[:, :], O[:, :], ACT.Square).then_inc(a.sem, 1)
            act.wait_ge(*v.at(1))
            step = [1]

            def chained(ins):
                step[0] += 1
                ins.then_inc(a.sem, 1)
                act.wait_ge(*a.at(step[0]))

            chained(nc.scalar.activation(y[:, 0:16], sums, ACT.Ln, scale=1.0 / P, bias=EPS))
            chained(nc.scalar.activation(y[:, 16:32], y[:, 0:16], ACT.Exp, scale=-0.5))
            chained(nc.scalar.activation(y[:, 0:16], y[:, 16:32], ACT.Square))

        @block.vector
        def _(dve):
            step = Chain(dve, v)
            dve.wait_ge(*a.at(1))
            step(nc.vector.tensor_reduce(sums, sq[:, :].rearrange("p (j d) -> p j d", d=P), AX_X, ALU.add))
            dve.wait_ge(*a.at(4))
            step(nc.vector.tensor_scalar(y[:, 32:48], sums, 1.0 / P, EPS, ALU.mult, ALU.add))
            step(nc.vector.scalar_tensor_tensor(out=y[:, 48:64], in0=y[:, 0:16], scalar=-0.5, in1=y[:, 32:48], op0=ALU.mult, op1=ALU.mult))
            step(nc.vector.scalar_tensor_tensor(out=y[:, 32:48], in0=y[:, 48:64], scalar=1.5, in1=y[:, 16:32], op0=ALU.add, op1=ALU.mult))
            for j in range(16):
                op = nc.vector.scalar_tensor_tensor(out=u128(O, j), in0=u128(O, j), scalar=y[:, 32 + j:33 + j], in1=k.v("o_norm"),
                                                    op0=ALU.mult, op1=ALU.mult)
            step(op)
            gate = G.rearrange("p t n -> p (t n)")
            step(nc.vector.tensor_tensor(O[:, :], O[:, :], gate, ALU.mult))

        @block.tensor
        def _(pe):
            pe.wait_ge(*v.at(6))
            for h in range(4):
                for c in range(4):
                    mm = nc.tensor.transpose(k.bank(h)[:, c * P:(c + 1) * P], u128(O, c * 4 + h), k.c("ident"))
                mm.then_inc(p.sem, 1)

    a.base += 4
    v.base += 6
    p.base += 4
    with nc.Block() as block:

        @block.scalar
        def _(act):
            for h in range(4):
                nc.scalar.activation(k.h[:, 4 + h, 0:SEQ], k.bank(h), ACT.Copy)


def pool_delta_layer(k):
    U, QKV, G = k.region(0, 4, 512), k.region(2048, 12, 512), k.region(8192, 4, 512)
    small = k.region(10240, 256)
    beta, ld, gcol, tmp = small[:, 0:16], small[:, 16:32], small[:, 32:48], small[:, 48:144]
    r = lambda at: k.region(at, 2048)
    rms_norm(k, [norm_of(k, 0, SEQ, k.v("a_ln"))], 18688)
    pool_delta_inputs(k, U, QKV, G)
    wba, pool_w = k.region(10496, 8, 8), k.region(10560, 4, P)
    ptmp = k.region(18688, 10 * 512)
    load(k, [(flat(wba), k.dram["w_ba"]), (flat(pool_w), k.dram["pool_w"]), (ptmp[:, 1024:3072], k.dram["pool_inverse"])])
    delta_gates(k, wba, beta, ld, gcol, tmp)
    pool_branch(k, U, pool_w, ptmp)
    rows = k.region(20000, 4, 512)
    inverse = inverse_rows(k, lambda j: QKV[:, j, :], 8, k.region(18688, 2, 512), rows, [SEQ])
    spread_rows(k, inverse, [(j, 8, P, 0, SEQ, [((QKV[:, j, :], 0), QKV[:, j, :], float(P) ** -0.5 if j < 4 else 1.0)])
                             for j in range(8)])
    delta_rule(k, QKV, beta, ld, gcol, small[:, 48:192], r(14592), r(16640), r(18688), r(20736), r(22784), r(24832), r(26880),
               r(10496), r(12544), r(0), k.h_all[:, 4096:6144], G)
    product(k, "a_w_out", lambda t, s, n: k.h[:, t, s:s + n], [(0, SEQ)], vector=add_to_residual(k, 4, [(0, SEQ)]))




def cross_attention_layer(k, l):
    mem = k.region(0, KT, MEM)
    Q, K, V = k.region(2048, KT, SEQ), k.region(6144, KT, MEM), k.region(8192, 2, D)
    load(k, [(mem, k.dram["mem"])])
    rms_norm(k, [norm_of(k, 0, SEQ, k.v("xa_ln", 8 * l, 8)),
                 (KT, MEM, lambda t: mem[:, t, :], lambda t: k.h[:, t, SEQ:TOK], k.v("xa_mem_ln", 8 * l, 8), None, D)], 20000)
    drained = k.counter("bank_drained")
    tokens = lambda t, s, n: k.h[:, t, s:s + n]
    product(k, "xa_wq", tokens, [(0, SEQ)], scalar=copy_out(k, lambda c, m, g: Q[:, 4 * c + m, :]))
    product(k, "xa_wk", tokens, [(SEQ, MEM)], scalar=copy_out(k, lambda c, m, g: K[:, 4 * c + m, :]))
    product(k, "xa_wv", tokens, [(SEQ, P), (SEQ + P, P)], stationary="tokens",
            scalar=copy_out(k, lambda c, m, g: V[:, g, 512 * c:512 * c + 512]))
    heads = [(h, t) for h in range(XA_HEADS) for t in range(TT)]
    units = [{"keys": MEM, "opens": t % 2 == 0, "closes": t % 2 == 1} for h, t in heads]

    def scores(u):
        h, t = heads[u]
        return [(slice(0, MEM), Q[:, 2 * h + j, t * P:(t + 1) * P], K[:, 2 * h + j, :], j == 0, j == 1) for j in range(2)]

    def values(u, weights):
        h, t = heads[u]
        return [(slice(0, P), slice(half * 256 + (t % 2) * P, half * 256 + (t % 2) * P + P),
                 V[:, kb, h * XA_DIM + half * P:h * XA_DIM + half * P + P], weights[:, kb * P:(kb + 1) * P], kb == 0, kb == 1)
                for half in range(2) for kb in range(2)]

    def finish(u):
        h, t = heads[u]
        return k.h[:, 2 * h:2 * h + 2, (t // 2) * 256:(t // 2) * 256 + 256], slice(0, P), slice(0, 512)

    attention(k, units, scores, lambda u: [(0, P), (P, P)], values, finish, XA_DIM ** -0.5, 12000, MEM)
    product(k, "xa_wo", tokens, [(0, SEQ)], vector=add_to_residual(k, 4, [(0, SEQ)]))


def squared_relu_layer(k, l):
    hidden = k.region(0, FF_TILES, SEQ)
    positive = k.region(FF_TILES * SEQ, 2, SEQ)
    drained, rectified = k.counter("bank_drained"), k.counter("rectified")
    rms_norm(k, [norm_of(k, 0, SEQ, k.v("ff_ln", 8 * l, 8))], 20000)

    def relu(act, chunk, m, g, bank, before):
        act.wait_ge(*drained.at(before - 1))
        act.activation(positive[:, m % 2, :], bank[:, 0:SEQ], ACT.Relu).then_inc(rectified.sem, 1)

    def square(dve, chunk, m, g, bank, before):
        dve.wait_ge(*rectified.at(before + 1))
        out = hidden[:, bass.ds(chunk * 4 + m, 1), :].rearrange("p a t -> p (a t)")
        dve.scalar_tensor_tensor(out=out, in0=bank[:, 0:SEQ], scalar=0.0, in1=positive[:, m % 2, :], op0=ALU.max,
                                 op1=ALU.mult).then_inc(drained.sem, 1)

    product(k, "ff_w1", lambda t, s, n: k.h[:, t, s:s + n], [(0, SEQ)], scalar=relu, vector=square)
    rectified.base += FF_TILES
    product(k, "ff_w2", lambda t, s, n: hidden[:, t, s:s + n], [(0, SEQ)], vector=add_to_residual(k, 1, [(0, SEQ)]))




def nsa_layer(k):
    nc = k.nc
    Q, KS, KW = k.region(0, KT, SEQ), k.region(4096, 4, SEQ), k.region(6144, 4, SEQ)
    V, gates = k.region(8192, TT, 512), k.region(10240, TT, 48)
    w1 = [k.region(10500, 16, P), k.region(12548, 16, P)]
    w2 = [k.region(14596, P), k.region(14724, NSA_DIM)]
    pe = [k.region(14788, 16), k.region(14804, 16)]
    pebias = k.region(14820, 4)
    hid = [k.region(14824, 4 * N_CMP), k.region(14948, 4 * N_CMP)]
    CK, CV = k.region(15072, 4, N_CMP), k.region(15196, 4, NSA_DIM)
    pcT = k.region(15460, NSA_HEADS, SEQ)
    cmp_bias = k.region(23660, TT, NSA_HEADS * N_CMP)
    pc = k.region(25650, 2, NSA_HEADS * N_CMP)
    KC = [k.region(15460, 4, SEQ), k.region(17508, 4, SEQ)]
    wgl = k.region(19556, KT, 48)
    table = k.region(29728, 512)
    small = k.region(26642, 4, NSA_HEADS)
    tokens = lambda t, s, n: k.h[:, t, s:s + n]
    drained = k.counter("bank_drained")
    rms_norm(k, [norm_of(k, 0, SEQ, k.v("c_ln"))], 20000)
    load(k, [(flat(wgl), k.dram["w_gl"]), (flat(w1[0]), k.dram["cmp_w1_k"][0]), (flat(w1[1]), k.dram["cmp_w1_v"][0]),
             (w2[0][:, 0:64], k.dram["cmp_w2_k"]), (w2[0][:, 64:128], k.dram["cmp_w2_k"]), (w2[1], k.dram["cmp_w2_v"]),
             (pe[0], k.dram["cmp_pe_k"]), (pe[1], k.dram["cmp_pe_v"]), (flat(cmp_bias), k.dram["cmp_bias"]),
             (table, k.dram["key_minus_query"])])
    product(k, "c_w_q", tokens, [(0, SEQ)], scalar=copy_out(k, lambda c, m, g: Q[:, 4 * c + m, :]))

    lo, hi = slice(0, 64), slice(64, 128)

    def both_shifted(act, chunk, m, g, bank, before):
        dst = KC[m // 2]
        a, b = 2 * (m % 2), 2 * (m % 2) + 1
        act.activation(dst[lo, a, :], bank[lo, :], ACT.Copy)
        act.activation(dst[hi, a, 0:SEQ - 1], bank[lo, 1:SEQ], ACT.Copy)
        act.activation(dst[lo, b, :], bank[hi, :], ACT.Copy)
        act.activation(dst[hi, b, 0:SEQ - 1], bank[hi, 1:SEQ], ACT.Copy).then_inc(drained.sem, 1)

    def both_halves(act, chunk, m, g, bank, before):
        dst = (KS, KW)[m // 2]
        a, b = 2 * (m % 2), 2 * (m % 2) + 1
        act.activation(dst[lo, a, :], bank[lo, :], ACT.Copy)
        act.activation(dst[hi, a, :], bank[lo, :], ACT.Copy)
        act.activation(dst[lo, b, :], bank[hi, :], ACT.Copy)
        act.activation(dst[hi, b, :], bank[hi, :], ACT.Copy).then_inc(drained.sem, 1)

    product(k, "c_w_c", tokens, [(0, SEQ)], scalar=both_shifted)
    product(k, "c_w_k", tokens, [(0, SEQ)], scalar=both_halves)
    product(k, "c_w_v", tokens, [(i * P, P) for i in range(TT)], stationary="tokens",
            scalar=copy_out(k, lambda c, m, g: V[:, g, :]))

    made, acted = k.counter("cmp_made"), k.counter("cmp_acted")
    with nc.Block() as block:

        @block.sync
        def _(sp):
            k.prefetch(sp)

        @block.tensor
        def _(pe_):
            for t in range(TT):
                for kt in range(KT):
                    mm = nc.tensor.matmul(k.bank(0)[:, t * 48:t * 48 + 48], k.h[:, kt, t * P:(t + 1) * P], wgl[:, kt, :],
                                          start=(kt == 0), stop=(kt == KT - 1))
            mm.then_inc(made.sem, 1)
            for i in range(2):
                for l in range(16):
                    mm = nc.tensor.matmul(k.bank(1)[:, i:i + 1], w1[i][:, l, :], pe[i][:, l:l + 1], start=(l == 0), stop=(l == 15))
            mm.then_inc(made.sem, 1)
            for i in range(2):
                for l in range(16):
                    rhs = KC[i][:, :, 2 * l:2 * l + CMP_STRIDE * (N_CMP - 1) + 1:CMP_STRIDE]
                    mm = nc.tensor.matmul(k.bank(2 + i)[:, 0:4 * N_CMP], w1[i][:, l, :], rhs, start=(l == 0), stop=(l == 15))
                mm.then_inc(made.sem, 1)
            pe_.wait_ge(*acted.at(2))
            nc.tensor.matmul(k.bank(4, 4 * N_CMP), w2[0], hid[0], start=True, stop=True).then_inc(made.sem, 1)
            pe_.wait_ge(*acted.at(3))
            for g in range(4):
                mm = nc.tensor.matmul(k.bank(5)[0:N_CMP, g * 64:(g + 1) * 64], hid[1][:, g * N_CMP:(g + 1) * N_CMP], w2[1],
                                      start=True, stop=True)
            mm.then_inc(made.sem, 1)

        @block.scalar
        def _(act):
            act.wait_ge(*made.at(2))
            nc.scalar.activation(pebias[:, 0:2], k.bank(1, 2), ACT.Copy).then_inc(acted.sem, 1)
            act.wait_ge(*acted.at(1))
            for i in range(2):
                act.wait_ge(*made.at(3 + i))
                nc.scalar.activation(hid[i], k.bank(2 + i, 4 * N_CMP), ACT.Silu, bias=pebias[:, i:i + 1]).then_inc(acted.sem, 1)
            nc.scalar.activation(flat(gates), k.bank(0, TT * 48), ACT.Sigmoid)
            act.wait_ge(*made.at(5))
            nc.scalar.activation(flat(CK), k.bank(4, 4 * N_CMP), ACT.Copy)
            act.wait_ge(*made.at(6))
            nc.scalar.activation(flat(CV)[0:N_CMP, :], k.bank(5, 256)[0:N_CMP, :], ACT.Copy)

    made.base += 6
    acted.base += 3

    scale = NSA_DIM ** -0.5
    HN = NSA_HEADS * N_CMP
    s_ready, p_step, p_exp, t_ready, t_out = (k.counter(n) for n in ("cmp_scores", "cmp_step", "cmp_exp", "cmp_turned", "cmp_out"))
    by_head = lambda ap: ap.rearrange("p (h n) -> p h n", n=N_CMP)
    wide = lambda ap: ap.rearrange("p (h o) -> p h o", o=1).to_broadcast([P, NSA_HEADS, N_CMP])
    steps = [0]
    with nc.Block() as block:

        @block.tensor
        def _(pe_):
            def score(t):
                if t >= 2:
                    pe_.wait_ge(*p_step.at(8 * (t - 2) + 2))
                for h in range(NSA_HEADS):
                    rows, at = (lo, hi)[h % 2], (h // 2) * N_CMP
                    mm = nc.tensor.matmul(k.bank(2 * (t % 2) + h % 2)[:, at:at + N_CMP], Q[rows, h // 2, t * P:(t + 1) * P],
                                          CK[rows, h // NSA_REP, :], start=True, stop=True)
                mm.then_inc(s_ready.sem, 1)

            score(0)
            score(1)
            for t in range(TT):
                pe_.wait_ge(*p_step.at(8 * t + 8))
                if t:
                    pe_.wait_ge(*t_out.at(t))
                for h in range(NSA_HEADS):
                    mm = nc.tensor.transpose(k.bank(4 + h // 4)[0:N_CMP, (h % 4) * P:(h % 4 + 1) * P],
                                             pc[:, t % 2, h * N_CMP:(h + 1) * N_CMP], k.c("ident"))
                mm.then_inc(t_ready.sem, 1)
                if t + 2 < TT:
                    score(t + 2)

        @block.vector
        def _(dve):
            step = Chain(dve, p_step)
            for t in range(TT):
                p = pc[:, t % 2, :]
                dve.wait_ge(*s_ready.at(t + 1))
                if t >= 2:
                    dve.wait_ge(*t_ready.at(t - 1))
                for par in range(2):
                    step(nc.vector.scalar_tensor_tensor(out=by_head(p)[:, par::2, :], in0=by_head(k.bank(2 * (t % 2) + par, HN // 2)),
                                                        scalar=scale, in1=by_head(cmp_bias[:, t, :])[:, par::2, :],
                                                        op0=ALU.mult, op1=ALU.add))
                step(nc.vector.tensor_reduce(small[:, 0, :], by_head(p), AX_X, ALU.max))
                step(nc.vector.tensor_tensor(by_head(p), by_head(p), wide(small[:, 0, :]), ALU.subtract))
                dve.wait_ge(*p_exp.at(t + 1))
                step(nc.vector.tensor_reduce(small[:, 1, :], by_head(p), AX_X, ALU.add))
                step(nc.vector.reciprocal(small[:, 2, :], small[:, 1, :]))
                gate = gates[:, t, 0:48:3]
                some = k.c("cmp_rows") if t == 0 else 1.0
                step(nc.vector.scalar_tensor_tensor(out=small[:, 3, :], in0=small[:, 2, :], scalar=some, in1=gate, op0=ALU.mult, op1=ALU.mult))
                step(nc.vector.tensor_tensor(by_head(p), by_head(p), wide(small[:, 3, :]), ALU.mult))

        @block.scalar
        def _(act):
            for t in range(TT):
                p = pc[:, t % 2, :]
                act.wait_ge(*p_step.at(8 * t + 4))
                nc.scalar.activation(p, p, ACT.Exp).then_inc(p_exp.sem, 1)
                act.wait_ge(*t_ready.at(t + 1))
                for b in range(4):
                    src = k.bank(4 + b)[0:N_CMP, :].rearrange("p (h q) -> p h q", h=4)
                    op = nc.scalar.activation(pcT[0:N_CMP, 4 * b:4 * b + 4, t * P:(t + 1) * P], src, ACT.Copy)
                op.then_inc(t_out.sem, 1)

    s_ready.base += TT
    p_step.base += 8 * TT
    p_exp.base += TT
    t_ready.base += TT
    t_out.base += TT

    slopes = [2.0 ** (-8.0 * (h + 1) / NSA_HEADS) for h in range(NSA_HEADS)]
    which = [(h, t, b) for h in range(NSA_HEADS) for t in range(TT) for b in range(2)]
    units = [{"keys": (t + 1) * P, "opens": t == 0 and b == 0, "closes": t == TT - 1 and b == 1} for h, t, b in which]

    def scores(u):
        h, t, b = which[u]
        rows = (lo, hi)[h % 2]
        return [(slice(0, (t + 1) * P), Q[rows, h // 2, t * P:(t + 1) * P], (KS, KW)[b][rows, h // NSA_REP, 0:(t + 1) * P], True, True)]

    def values(u, weights):
        h, t, b = which[u]
        rows, cols, g = (lo, hi)[h % 2], slice(t * P, (t + 1) * P), h // NSA_REP
        out = [(rows, cols, V[:, kb, b * 256 + g * 64:b * 256 + g * 64 + 64], weights[:, kb * P:(kb + 1) * P], b == 0 and kb == 0, False)
               for kb in range(t + 1)]
        if b == 1:
            out.append((rows, cols, CV[0:N_CMP, g, :], pcT[0:N_CMP, h, cols], False, True))
        return out

    def finish(u):
        h = which[u][0]
        rows = (lo, hi)[h % 2]
        return k.h[rows, h // 2, 0:SEQ], rows, slice(0, SEQ)

    attention(k, units, scores, lambda u: [(kb * P, P) for kb in range(which[u][1] + 1)], values, finish, scale, 26640, 512,
              gates=lambda u: gates[:, which[u][1], 3 * which[u][0] + 1 + which[u][2]:3 * which[u][0] + 2 + which[u][2]],
              bias=lambda u: (table[:, 384 - P * which[u][1]:512], slopes[which[u][0]] / scale))
    product(k, "c_w_out", tokens, [(0, SEQ)], vector=add_to_residual(k, 4, [(0, SEQ)]))




def modulation(k, l):
    nc = k.nc
    cond = k.region(0, KT, 2)
    mod = k.mods[:, 0:96].rearrange("p (c n) -> p c n", c=2)
    gains = k.mods[:, 96:128].rearrange("p (c j n) -> p c j n", c=2, j=2)
    drained, step = k.counter("bank_drained"), k.counter("modulation_step")
    with nc.Block() as block:

        @block.sync
        def _(sp):
            k.prefetch(sp)

        @block.scalar
        def _(act):
            nc.scalar.activation(flat(cond), k.v("cond"), ACT.Silu)

    at = VECTORS["b_mod"][0] + 48 * l

    def take(dve, chunk, m, g, bank, before):
        tile = chunk * 4 + m
        bias = k.vec[:, bass.ds(at + tile, 1)]
        out = mod[:, :, bass.ds(tile, 1)].rearrange("p c o -> p (c o)")
        dve.tensor_scalar(out, bank[:, 0:2], bias, None, ALU.add).then_inc(drained.sem, 1)

    product(k, "w_mod", lambda t, s, n: cond[:, t, :], [(0, 2)], vector=take)
    with nc.Block() as block:

        @block.sync
        def _(sp):
            k.prefetch(sp)

        @block.vector
        def _(dve):
            for c in range(2):
                for j, norm in enumerate(("norm1", "norm2")):
                    sc = mod[:, c, 24 * j + 8:24 * j + 16]
                    nc.vector.scalar_tensor_tensor(out=gains[:, c, j, :], in0=sc, scalar=1.0, in1=k.v(norm, 8 * l, 8),
                                                   op0=ALU.add, op1=ALU.mult)

    parts = lambda c, i: mod[:, c, 8 * i:8 * i + 8]
    return {"gain": [[gains[:, c, j, :] for j in range(2)] for c in range(2)],
            "shift": [[parts(c, 0), parts(c, 3)] for c in range(2)], "gate": [[parts(c, 2), parts(c, 5)] for c in range(2)]}


def modulated_norm(k, mod, j, groups):
    rms_norm(k, [norm_of(k, s, n, mod["gain"][c][j], mod["shift"][c][j]) for c, (s, n) in enumerate(groups)], 20000)


def conv_ffn(k, l, mod, groups):
    modulated_norm(k, mod, 1, groups)
    hidden = k.region(0, FC, TOK)
    G = len(groups)
    drained, step, convolved, gated = (k.counter(n) for n in ("bank_drained", "ffn_conv_step", "ffn_convolved", "ffn_gated"))
    w_at, b_at = VECTORS["ffn_conv_w"][0] + 3 * FC * l, VECTORS["ffn_conv_b"][0] + FC * l

    def hidden_tile(chunk, m, g):
        s, n = groups[g]
        return hidden[:, bass.ds(chunk * 2 + m, 1), s:s + n].rearrange("p a t -> p (a t)")

    def take(dve, chunk, m, g, bank, before):
        n = groups[g][1]
        out = hidden_tile(chunk, m % 2, g)
        if m < 2:
            tap = lambda i: k.vec[:, bass.ds(w_at + i * FC + chunk * 2 + m, 1)]
            nth = ((chunk * 2 + m) * G + g) * 2
            dve.tensor_scalar(out, bank[:, 0:n], tap(1), k.vec[:, bass.ds(b_at + chunk * 2 + m, 1)], ALU.mult, ALU.add).then_inc(step.sem, 1)
            dve.wait_ge(*step.at(nth + 1))
            o = hidden[:, bass.ds(chunk * 2 + m, 1), groups[g][0] + 1:groups[g][0] + n].rearrange("p a t -> p (a t)")
            dve.scalar_tensor_tensor(out=o, in0=bank[:, 0:n - 1], scalar=tap(0), in1=o, op0=ALU.mult, op1=ALU.add).then_inc(step.sem, 1)
            dve.wait_ge(*step.at(nth + 2))
            o = hidden[:, bass.ds(chunk * 2 + m, 1), groups[g][0]:groups[g][0] + n - 1].rearrange("p a t -> p (a t)")
            dve.scalar_tensor_tensor(out=o, in0=bank[:, 1:n], scalar=tap(2), in1=o, op0=ALU.mult, op1=ALU.add).then_inc(drained.sem, 1)
        else:
            dve.wait_ge(*gated.at((chunk * 2 + m - 2) * G + g + 1))
            dve.tensor_tensor(out, out, bank[:, 0:n], ALU.mult).then_inc(drained.sem, 1)

    def silu(act, chunk, m, g, bank, before):
        if m < 2:
            act.wait_ge(*drained.at(before + 1))
            out = hidden_tile(chunk, m, g)
            act.activation(out, out, ACT.Silu).then_inc(gated.sem, 1)

    product(k, "ffn_up", lambda t, s, n: k.h[:, t, s:s + n], groups, vector=take, scalar=silu)
    step.base += 2 * FC * G
    gated.base += FC * G
    product(k, "ffn_down", lambda t, s, n: hidden[:, t, s:s + n], groups,
            vector=add_to_residual(k, 1, groups, [mod["gate"][c][1] for c in range(G)]))


def fourier(k, UF, n, start, name):
    nc = k.nc
    nt = n // P
    PQ = k.region(12288, 4, nt, 256)
    group = k.region(16384, 256)
    table = k.region(16640, 2, nt * n)
    load(k, [(group, k.dram["group_dft"])] + [(table[:, i, :], k.dram["seq_dft_" + name][i]) for i in range(2)])
    rotated = table[:, :, :].rearrange("p i (t n) -> p i t n", t=nt)
    made, copied = k.counter("fourier_made"), k.counter("fourier_copied")
    U = 4 * nt
    with nc.Block() as block:

        @block.sync
        def _(sp):
            k.prefetch(sp)

        @block.tensor
        def _(pe):
            for u in range(U):
                g, t = u // nt, u % nt
                if u >= 4:
                    pe.wait_ge(*copied.at(u - 3))
                nc.tensor.matmul(k.bank(u % 4, 256), UF[:, g, start + t * P:start + (t + 1) * P], group, start=True,
                                 stop=True).then_inc(made.sem, 1)
            for g in range(4):
                pe.wait_ge(*copied.at((g + 1) * nt))
                for t in range(nt):
                    for i in range(2):
                        mm = nc.tensor.matmul(k.bank(4 + g, n), PQ[:, g, t, i * P:(i + 1) * P], rotated[:, i, t, :],
                                              start=(t == 0 and i == 0), stop=(t == nt - 1 and i == 1))
                mm.then_inc(made.sem, 1)

        @block.scalar
        def _(act):
            for u in range(U):
                act.wait_ge(*made.at(u + 1))
                nc.scalar.activation(PQ[:, u // nt, u % nt, :], k.bank(u % 4, 256), ACT.Copy).then_inc(copied.sem, 1)

        @block.vector
        def _(dve):
            for g in range(4):
                dve.wait_ge(*made.at(U + g + 1))
                nc.vector.tensor_copy(k.h[:, g, start:start + n], k.bank(4 + g, n))

    made.base += U + 4
    copied.base += U


def hyena(k, X0, W, n, start, name):
    nc = k.nc
    nt = n // P
    decay, WT = k.region(0, nt, 512), k.region(12288, nt, 512)
    total, diff = k.region(14336, nt, 512), k.region(16384, nt, 512)
    tables = k.region(18432, 4, nt * n)
    w1, w23, w4 = k.region(26624, 64), k.region(26688, 128), k.region(26816, 1024)
    pos = k.region(27840, n)
    hcur = k.region(28352, 2, 512)
    arg = k.region(29376, 512)
    norm = k.region(29888, 8)
    work = k.region(27840, 4, 512)
    Yre, Yim = k.region(0, nt, 512), k.region(6144, nt, 512)
    tab = tables[:, :, :].rearrange("p i (t n) -> p i t n", t=nt)
    load(k, [(w1[0:HY_EMB, :], k.dram["hy_w1"]), (w23[0:64, :], k.dram["hy_w23"]), (w4[0:64, :], k.dram["hy_w4"]),
             (pos[0:HY_EMB, :], k.dram["hy_pos_" + name]), (flat(decay), k.dram["hy_decay_" + name])]
         + [(tables[:, i, :], k.dram["odd_dft_" + name][i]) for i in range(4)])

    made, v_step, sine = k.counter("filter_made"), k.counter("filter_step"), k.counter("filter_sine")
    F64 = slice(0, HY_WIDTH)
    with nc.Block() as block:

        @block.sync
        def _(sp):
            k.prefetch(sp)

        @block.tensor
        def _(pe):
            for layer in range(3):
                if layer == 0:
                    lhs, rhs = w1[0:HY_EMB, :], pos[0:HY_EMB, :]
                else:
                    pe.wait_ge(*sine.at(layer))
                    lhs, rhs = w23[F64, (layer - 1) * 64:layer * 64], hcur[F64, (layer - 1) % 2, 0:n]
                nc.tensor.matmul(k.bank(layer, n, F64), lhs, rhs, start=True, stop=True).then_inc(made.sem, 1)

        @block.vector
        def _(dve):
            step = Chain(dve, v_step)
            for layer in range(3):
                dve.wait_ge(*made.at(layer + 1))
                a, r = arg[F64, 0:n], hcur[F64, layer % 2, 0:n]
                step(nc.vector.tensor_scalar(a, k.bank(layer, n, F64), k.v("hy_b", layer, 1)[F64], k.v("hy_freq")[F64], ALU.add, ALU.mult))
                step(nc.vector.tensor_scalar(r, a, 1.0 / (2 * math.pi), ROUND, ALU.mult, ALU.add))
                step(nc.vector.tensor_scalar(r, r, ROUND, None, ALU.subtract))
                step(nc.vector.scalar_tensor_tensor(out=a, in0=r, scalar=-TWO_PI_HI, in1=a, op0=ALU.mult, op1=ALU.add))
                step(nc.vector.scalar_tensor_tensor(out=a, in0=r, scalar=-TWO_PI_LO, in1=a, op0=ALU.mult, op1=ALU.add))
                step(nc.vector.tensor_scalar(r, a, 3.141592, -3.141592, ALU.min, ALU.max))
                if layer < 2:
                    dve.wait_ge(*sine.at(layer + 1))

        @block.scalar
        def _(act):
            for layer in range(3):
                act.wait_ge(*v_step.at(6 * layer + 6))
                h = hcur[F64, layer % 2, 0:n]
                nc.scalar.activation(h, h, ACT.Sin).then_inc(sine.sem, 1)

    made.base += 3
    v_step.base += 18
    sine.base += 3

    last = hcur[F64, 0, :]
    p, v, a = k.counter("hyena_pe"), k.counter("hyena_dve"), k.counter("hyena_act")
    sides = k.region(28864, 2, 512)
    with nc.Block() as block:

        @block.sync
        def _(sp):
            k.prefetch(sp)

        @block.tensor
        def _(pe):
            for t in range(nt):
                if t:
                    pe.wait_ge(*v.at(4 * t - 2))
                for side in range(2):
                    mm = nc.tensor.matmul(k.bank(side), last[:, t * P:(t + 1) * P], w4[F64, side * 512:(side + 1) * 512],
                                          start=True, stop=True)
                mm.then_inc(p.sem, 1)
                if t >= 2:
                    pe.wait_ge(*k.counter("hyena_turned").at(t - 1))
                for c in range(4):
                    mm = nc.tensor.transpose(k.bank(2 + t % 2)[:, c * P:(c + 1) * P], W[:, c, start + t * P:start + (t + 1) * P], k.c("ident"))
                mm.then_inc(k.counter("hyena_transposed").sem, 1)
                pe.wait_ge(*a.at(t + 1))
                for c in range(4):
                    for side in range(2):
                        mm = nc.tensor.matmul(k.bank(4 + c, 1), sides[:, side, c * P:(c + 1) * P], k.c("ones", 0, 1),
                                              start=(t == 0 and side == 0), stop=(t == nt - 1 and side == 1))
                mm.then_inc(k.counter("hyena_summed").sem, 1)

        @block.vector
        def _(dve):
            for t in range(nt):
                dve.wait_ge(*p.at(t + 1))
                if t:
                    dve.wait_ge(*k.counter("hyena_summed").at(t))
                first = k.c("not_first") if t == 0 else 1.0
                nc.vector.tensor_tensor(sides[:, 0, :], k.bank(0), decay[:, t, :], ALU.mult).then_inc(v.sem, 1)
                nc.vector.scalar_tensor_tensor(out=sides[:, 1, :], in0=k.bank(1), scalar=first, in1=decay[:, t, :],
                                               op0=ALU.mult, op1=ALU.mult).then_inc(v.sem, 1)
                dve.wait_ge(*v.at(4 * t + 2))
                nc.vector.tensor_tensor(total[:, t, :], sides[:, 0, :], sides[:, 1, :], ALU.add).then_inc(v.sem, 1)
                nc.vector.tensor_tensor(diff[:, t, :], sides[:, 0, :], sides[:, 1, :], ALU.subtract).then_inc(v.sem, 1)
            dve.wait_ge(*k.counter("hyena_summed").at(nt))
            sums = k.psum[:, 4 * BANK:8 * BANK].rearrange("p (b n) -> p b n", b=4)[:, :, 0:1].rearrange("p b n -> p (b n)")
            nc.vector.reciprocal(norm[:, 0:4], sums)

        @block.scalar
        def _(act):
            for t in range(nt):
                act.wait_ge(*k.counter("hyena_transposed").at(t + 1))
                nc.scalar.activation(WT[:, t, :], k.bank(2 + t % 2), ACT.Copy).then_inc(k.counter("hyena_turned").sem, 1)
                act.wait_ge(*v.at(4 * t + 4))
                nc.scalar.activation(flat(sides), flat(sides), ACT.Abs).then_inc(a.sem, 1)

    p.base += nt
    v.base += 4 * nt
    a.base += nt
    for s in ("hyena_turned", "hyena_transposed", "hyena_summed"):
        k.counter(s).base += nt

    spectra, copied, multiplied = k.counter("spectra_made"), k.counter("spectra_copied"), k.counter("spectra_multiplied")
    back = k.counter("hyena_back")
    with nc.Block() as block:

        @block.sync
        def _(sp):
            k.prefetch(sp)

        @block.tensor
        def _(pe):
            for f in range(nt):
                if f:
                    pe.wait_ge(*multiplied.at(6 * f))
                for bank, table, src in ((0, 0, WT), (1, 1, WT), (2, 0, total), (3, 1, diff)):
                    for t in range(nt):
                        mm = nc.tensor.matmul(k.bank(bank), tab[:, table, t, f * P:(f + 1) * P], src[:, t, :], start=(t == 0), stop=(t == nt - 1))
                mm.then_inc(spectra.sem, 1)
            pe.wait_ge(*multiplied.at(6 * nt))
            for c in range(4):
                for f in range(nt):
                    for i, Y in enumerate((Yre, Yim)):
                        mm = nc.tensor.matmul(k.bank(4 + c, n), Y[:, f, c * P:(c + 1) * P], tab[:, 2 + i, f, :],
                                              start=(f == 0 and i == 0), stop=(f == nt - 1 and i == 1))
                mm.then_inc(back.sem, 1)

        @block.scalar
        def _(act):
            for f in range(nt):
                act.wait_ge(*spectra.at(f + 1))
                if f:
                    act.wait_ge(*multiplied.at(6 * f))
                nc.scalar.activation(work[:, 0, :], k.bank(2), ACT.Copy)
                nc.scalar.activation(work[:, 1, :], k.bank(3), ACT.Copy).then_inc(copied.sem, 1)

        @block.vector
        def _(dve):
            step = Chain(dve, multiplied)
            for f in range(nt):
                dve.wait_ge(*copied.at(f + 1))
                hre, him = work[:, 0, :], work[:, 1, :]
                step(nc.vector.tensor_tensor(Yre[:, f, :], k.bank(0), hre, ALU.mult))
                step(nc.vector.tensor_tensor(work[:, 2, :], k.bank(1), him, ALU.mult))
                step(nc.vector.tensor_tensor(Yre[:, f, :], Yre[:, f, :], work[:, 2, :], ALU.subtract))
                step(nc.vector.tensor_tensor(Yim[:, f, :], k.bank(0), him, ALU.mult))
                step(nc.vector.tensor_tensor(work[:, 2, :], k.bank(1), hre, ALU.mult))
                step(nc.vector.tensor_tensor(Yim[:, f, :], Yim[:, f, :], work[:, 2, :], ALU.add))
            for c in range(4):
                y, w = work[:, 3, 0:n], W[:, c, start:start + n]
                step(nc.vector.tensor_scalar(y, w, k.v("hy_bias", c, 1), None, ALU.mult))
                dve.wait_ge(*back.at(c + 1))
                step(nc.vector.scalar_tensor_tensor(out=y, in0=k.bank(4 + c, n), scalar=norm[:, c:c + 1], in1=y, op0=ALU.mult, op1=ALU.add))
                step(nc.vector.tensor_tensor(k.h[:, 4 + c, start:start + n], y, X0[:, c, start:start + n], ALU.mult))

    spectra.base += nt
    copied.base += nt
    multiplied.base += 6 * nt + 12
    back.base += 4


def fourier_hyena_layer(k, mod, groups):
    nc = k.nc
    UF, HY = k.region(0, 4, TOK), k.region(3072, 12, TOK)
    modulated_norm(k, mod, 0, groups)
    drained, step = k.counter("bank_drained"), k.counter("hy_conv_step")
    count = [0]

    def take(dve, chunk, m, g, bank, before):
        tile = chunk * 4 + m
        s, n = groups[g]
        if tile < 4:
            dve.tensor_copy(UF[:, tile, s:s + n], bank[:, 0:n]).then_inc(drained.sem, 1)
            return
        j = tile - 4

        def chained(ins):
            count[0] += 1
            ins.then_inc(step.sem, 1)
            dve.wait_ge(*step.at(count[0]))

        taps = [k.v("hy_conv_w", i * 12 + j, 1) for i in (1, 0, 2)]
        conv_taps(dve, chained, HY[:, j, s:s + n], bank, taps, k.v("hy_conv_b", j, 1), [0, -1, 1], None, n)
        dve.sem_inc(drained.sem, 1)

    product(k, "fh_w_in", lambda t, s, n: k.h[:, t, s:s + n], groups, vector=take, loop=False)
    step.base += count[0]
    X0, X1, W = HY[:, 0:4, :], HY[:, 4:8, :], HY[:, 8:12, :]
    with nc.Block() as block:

        @block.gpsimd
        def _(pool):
            for c in range(4):
                nc.gpsimd.tensor_tensor(W[:, c, :], W[:, c, :], X1[:, c, :], ALU.mult)

    for (s, n), name in zip(groups, "xc"):
        fourier(k, UF, n, s, name)
    for (s, n), name in zip(groups, "xc"):
        hyena(k, X0, W, n, s, name)
    product(k, "fh_w_out", lambda t, s, n: k.h[:, t, s:s + n], groups,
            vector=add_to_residual(k, 4, groups, [mod["gate"][c][0] for c in range(2)]))


def mla_layer(k, mod, groups):
    nc = k.nc
    K, Q, V = k.region(0, MLA_HEADS, TOK), k.region(12288, MLA_HEADS, SEQ), k.region(20480, TOK // P, D)
    A = k.region(26624, 4, TOK)
    aq = k.h_all[:, 0:1024].rearrange("p (k t) -> p k t", k=2)
    akv = k.h_all[:, 1024:1792]
    wukv, rope = k.h_all[:, 2048:4096], k.h_all[:, 4096:5120]
    pe_rows = slice(MLA_NOPE, MLA_QK)
    modulated_norm(k, mod, 0, groups)
    drained = k.counter("bank_drained")

    def latent(act, chunk, m, g, bank, before):
        s, n = groups[g]
        if m < 3:
            act.activation(A[:, m, s:s + n], bank[:, 0:n], ACT.Copy).then_inc(drained.sem, 1)
        else:
            act.activation(A[pe_rows, 3, s:s + n], bank[0:MLA_ROPE, 0:n], ACT.Copy).then_inc(drained.sem, 1)

    product(k, "mla_w_in", lambda t, s, n: k.h[:, t, s:s + n], groups, scalar=latent)
    load(k, [(wukv, k.dram["mla_w_ukv"][0]), (rope, k.dram["rope"])])
    rms_norm(k, [(2, SEQ, lambda t: A[:, t, 0:SEQ], lambda t: aq[:, t, :], k.v("q_a_norm"), None, 2 * P)]
             + [(1, n, lambda t, s=s, n=n: A[:, 2, s:s + n], lambda t, s=s, n=n: akv[:, s:s + n], k.v("kv_a_norm"), None, P)
                for s, n in groups], 20480)
    product(k, "mla_w_uq", lambda t, s, n: aq[:, t, s:s + n], [(0, SEQ)], tile=MLA_QK,
            scalar=copy_heads(k, Q))

    made, used = k.counter("kv_made"), k.counter("kv_copied")
    jobs = [(h, s, n) for h in range(MLA_HEADS) for s, n in groups]
    with nc.Block() as block:

        @block.sync
        def _(sp):
            k.prefetch(sp)

        @block.tensor
        def _(pe):
            for i, (h, s, n) in enumerate(jobs):
                if i >= 4:
                    pe.wait_ge(*used.at(i - 3))
                nc.tensor.matmul(k.bank(i % 4, n, slice(0, 64)), wukv[:, h * 64:(h + 1) * 64], akv[:, s:s + n],
                                 start=True, stop=True).then_inc(made.sem, 1)
            for i in range(12):
                if i >= 4:
                    pe.wait_ge(*k.counter("values_copied").at(i - 3))
                nc.tensor.matmul(k.bank(4 + i % 4), akv[:, (i // 2) * P:(i // 2 + 1) * P],
                                 wukv[:, 1024 + (i % 2) * 512:1536 + (i % 2) * 512], start=True, stop=True).then_inc(made.sem, 1)

        @block.scalar
        def _(act):
            for i, (h, s, n) in enumerate(jobs):
                act.wait_ge(*made.at(i + 1))
                nc.scalar.activation(K[0:64, h, s:s + n], k.bank(i % 4, n, slice(0, 64)), ACT.Copy).then_inc(used.sem, 1)

        @block.vector
        def _(dve):
            for i in range(12):
                dve.wait_ge(*made.at(len(jobs) + i + 1))
                nc.vector.tensor_copy(V[:, i // 2, (i % 2) * 512:(i % 2 + 1) * 512], k.bank(4 + i % 4)).then_inc(
                    k.counter("values_copied").sem, 1)

        @block.gpsimd
        def _(pool):
            for h in range(MLA_HEADS):
                nc.gpsimd.tensor_copy(K[pe_rows, h, :], A[pe_rows, 3, :])

    made.base += len(jobs) + 12
    used.base += len(jobs)
    k.counter("values_copied").base += 12

    squares = k.region(26624, 2, TOK)
    rows = k.h_all[:, 0:3072].rearrange("p (i t) -> p i t", i=4)
    qn = slice(0, MLA_QK)
    inverse = inverse_rows(k, lambda j: K[qn, j, :], MLA_HEADS, squares, rows, [n for _, n in groups], src_rows=MLA_QK, scale=1.0 / MLA_QK)
    turn_rotary(k, A[:, 3, :], rope, k.v("k_norm"))
    spread_rows(k, inverse, [(h, MLA_HEADS, MLA_QK, s, n,
                              [((K[0:64, h, s:s + n], 0), K[0:64, h, s:s + n], k.v("k_norm")[0:64]),
                               ((K[pe_rows, h, s:s + n], 64), A[pe_rows, 3, s:s + n], 1.0)]) for h, s, n in jobs])
    inverse = inverse_rows(k, lambda j: Q[qn, j, :], MLA_HEADS, squares, rows, [SEQ], src_rows=MLA_QK, scale=1.0 / MLA_QK)
    spread_rows(k, inverse, [(h, MLA_HEADS, MLA_QK, 0, SEQ, [((Q[qn, h, :], 0), Q[qn, h, :], k.v("q_norm")[qn])])
                             for h in range(MLA_HEADS)])
    turn_queries(k, Q, rope)

    heads = [(h, t) for h in range(MLA_HEADS) for t in range(TT)]
    units = [{"keys": TOK, "opens": t == 0, "closes": t == TT - 1} for h, t in heads]

    def scores(u):
        h, t = heads[u]
        return [(slice(s, s + n), Q[qn, h, t * P:(t + 1) * P], K[qn, h, s:s + n], True, True) for s, n in groups]

    def values(u, weights):
        h, t = heads[u]
        rows_ = slice(64 * (h % 2), 64 * (h % 2) + 64)
        return [(rows_, slice(t * P, (t + 1) * P), V[:, kb, h * 64:(h + 1) * 64], weights[:, kb * P:(kb + 1) * P], kb == 0, kb == 5)
                for kb in range(6)]

    def finish(u):
        h = heads[u][0]
        rows_ = slice(64 * (h % 2), 64 * (h % 2) + 64)
        return k.h[rows_, h // 2, 0:SEQ], rows_, slice(0, SEQ)

    attention(k, units, scores, lambda u: [(kb * P, P) for kb in range(6)], values, finish, float(MLA_QK) ** -0.5, 26624, TOK)
    product(k, "mla_w_o", lambda t, s, n: k.h[:, t, s:s + n], [(0, SEQ)],
            vector=add_to_residual(k, 4, [(0, SEQ)], [mod["gate"][0][0]]))


def copy_heads(k, Q):
    drained = k.counter("bank_drained")

    def take(act, chunk, m, g, bank, before):
        act.activation(Q[0:MLA_QK, m, :], bank[0:MLA_QK, 0:SEQ], ACT.Copy).then_inc(drained.sem, 1)

    return take


def turn_rotary(k, kpe, rope, gain):
    nc = k.nc
    rows = slice(MLA_NOPE, MLA_QK)
    tmp = k.h_all[:, 5120:5632]
    step, made = k.counter("rotary_step"), k.counter("rotary_made")
    with nc.Block() as block:

        @block.tensor
        def _(pe):
            pe.wait_ge(*step.at(1))
            nc.tensor.matmul(k.bank(0, SEQ, rows), k.c("rope_swap")[rows, :], kpe[rows, 0:SEQ], start=True, stop=True).then_inc(made.sem, 1)

        @block.vector
        def _(dve):
            chain = Chain(dve, step)
            chain(nc.vector.tensor_scalar(kpe[rows, :], kpe[rows, :], gain[rows], None, ALU.mult))
            dve.wait_ge(*made.at(1))
            chain(nc.vector.tensor_tensor(tmp[rows, :], k.bank(0, SEQ, rows), rope[rows, SEQ:2 * SEQ], ALU.mult))
            chain(nc.vector.tensor_tensor(kpe[rows, 0:SEQ], kpe[rows, 0:SEQ], rope[rows, 0:SEQ], ALU.mult))
            chain(nc.vector.tensor_tensor(kpe[rows, 0:SEQ], kpe[rows, 0:SEQ], tmp[rows, :], ALU.add))

    step.base += 4
    made.base += 1


def turn_queries(k, Q, rope):
    nc = k.nc
    rows = slice(MLA_NOPE, MLA_QK)
    tmp = k.h_all[:, 5120:6144].rearrange("p (b t) -> p b t", b=2)
    step, made, turned = k.counter("turn_step"), k.counter("turn_made"), k.counter("turn_cosine")
    with nc.Block() as block:

        @block.sync
        def _(sp):
            k.prefetch(sp)

        @block.tensor
        def _(pe):
            for h in range(MLA_HEADS):
                if h >= 4:
                    pe.wait_ge(*step.at(2 * (h - 4) + 1))
                nc.tensor.matmul(k.bank(h % 4, SEQ, rows), k.c("rope_swap")[rows, :], Q[rows, h, :], start=True, stop=True).then_inc(made.sem, 1)

        @block.gpsimd
        def _(pool):
            for h in range(MLA_HEADS):
                pool.wait_ge(*made.at(h + 1))
                nc.gpsimd.tensor_tensor(Q[rows, h, :], Q[rows, h, :], rope[rows, 0:SEQ], ALU.mult).then_inc(turned.sem, 1)

        @block.vector
        def _(dve):
            chain = Chain(dve, step)
            for h in range(MLA_HEADS):
                dve.wait_ge(*made.at(h + 1))
                chain(nc.vector.tensor_tensor(tmp[rows, h % 2, :], k.bank(h % 4, SEQ, rows), rope[rows, SEQ:2 * SEQ], ALU.mult))
                dve.wait_ge(*turned.at(h + 1))
                chain(nc.vector.tensor_tensor(Q[rows, h, :], Q[rows, h, :], tmp[rows, h % 2, :], ALU.add))

    step.base += 2 * MLA_HEADS
    made.base += MLA_HEADS
    turned.base += MLA_HEADS



PLAN = [("a_w_in", KT, 512, 4), ("a_w_gate", KT, 512, 1), ("a_w_out", KT, 512, 2)]
XA = lambda l: [(f"xa_w{n}_{l}", KT, 512, 2) for n in "qkvo"]
FF = lambda l: [(f"ff_w1_{l}", KT, 512, 8), (f"ff_w2_{l}", FF_TILES, P, 8)]
FFN = lambda l: [(f"ffn_up_{l}", KT, 512, FC // 2), (f"ffn_down_{l}", FC, P, KT)]
PLAN += XA(0) + FF(0)
PLAN += [("c_w_q", KT, 512, 2), ("c_w_c", KT, 512, 1), ("c_w_k", KT, 512, 1), ("c_w_v", KT, 512, 1), ("c_w_out", KT, 512, 2)]
PLAN += XA(1) + FF(1)
PLAN += [("w_mod_0", KT, 512, 12), ("fh_w_in", KT, 512, 4), ("fh_w_out", KT, 512, 2)] + FFN(0)
PLAN += [("w_mod_1", KT, 512, 12), ("mla_w_in", KT, 416, 1), ("mla_w_uq", 2, 1536, 1), ("mla_w_o", KT, 512, 2)] + FFN(1)


def final_norm(k):
    rms_norm(k, [(KT, SEQ, lambda t: k.x[:, t, 0:SEQ], lambda t: k.x[:, t, 0:SEQ], k.v("final_ln"), None, D)], 20000)


def build(nc, dram, out):
    with ExitStack() as ctx:
        k = Kernel(nc, ctx, dram)
        k.plan = [weight(dram, *entry) for entry in PLAN]
        drained, stored = k.counter("bank_drained"), k.counter("output_stored")
        with nc.Block() as block:

            @block.vector
            def _(dve):
                dve.sem_inc(drained.sem, BANKS)

        drained.base += BANKS
        load(k, [(k.vec[:, :], dram["vectors"]), (k.const[:, :], dram["consts"]), (k.x[:, :, 0:SEQ], dram["x"]),
                 (k.x[:, :, SEQ:TOK], dram["ctx"])])
        pool_delta_layer(k)
        cross_attention_layer(k, 0)
        squared_relu_layer(k, 0)
        nsa_layer(k)
        cross_attention_layer(k, 1)
        squared_relu_layer(k, 1)
        final_norm(k)
        both, x_only = [(0, SEQ), (SEQ, CTX)], [(0, SEQ)]
        mod = modulation(k, 0)
        fourier_hyena_layer(k, mod, both)
        conv_ffn(k, 0, mod, both)
        mod = modulation(k, 1)
        mla_layer(k, mod, both)
        conv_ffn(k, 1, mod, x_only)
        with nc.Block() as block:

            @block.sync
            def _(sp):
                sp.dma_start(out, k.x[:, :, 0:SEQ]).then_inc(stored.sem, 16)
                sp.wait_ge(*stored.at(16))




def chunked(w, cols, rows=P):
    kt, chunks = w.shape[0] // rows, w.shape[1] // cols
    return np.ascontiguousarray(w.reshape(kt, rows, chunks, cols).transpose(2, 1, 0, 3)).reshape(chunks, rows, kt * cols)


def by_feature(x):
    n, d = x.shape
    return np.ascontiguousarray(x.T.reshape(d // P, P, n).transpose(1, 0, 2))


def columns(v):
    d = v.shape[-1]
    if d % P:
        out = np.zeros((P, v.size // d), v.dtype)
        out[:d] = v.reshape(-1, d).T
        return out
    return np.ascontiguousarray(v.reshape(-1, P).T)


def spread(v):
    return np.broadcast_to(v.reshape(1, -1), (P, v.size))


def pack(entries, total, parts):
    out = np.zeros((P, total), np.float32)
    for name, (at, width) in entries.items():
        value = parts[name]
        assert value.shape[1] == width and value.shape[0] <= P, (name, value.shape, width)
        out[:value.shape[0], at:at + width] = value
    return out


def shape_constants():
    f = np.float32
    i = np.arange(P)
    levels = []
    for level in range(LEVELS):
        half = 1 << level
        pair = i // (2 * half)
        low = (i // half) % 2
        levels.append(((pair[:, None] == pair[None, :]) & (low[:, None] == 1) & (low[None, :] == 0)).astype(f))
    strip = np.zeros((P, 31), f)
    strip[:, 15] = 1
    swap = np.zeros((P, 32), f)
    for half in range(2):
        for j in range(8):
            a, b = MLA_NOPE + half * 16 + j, MLA_NOPE + half * 16 + 8 + j
            swap[b, half * 16 + j] = -1
            swap[a, half * 16 + 8 + j] = 1
    consts = pack(CONSTS, N_CONSTS, {
        "ident": np.eye(P, dtype=f), "ones": np.ones((P, P), f), "upto": (i[:, None] <= i[None, :]).astype(f),
        "levels": np.concatenate(levels, 1), "strip": strip, "cmp_rows": (i[:, None] >= CMP_LEN - 1).astype(f),
        "not_first": (i[:, None] > 0).astype(f), "rope_swap": swap,
    })
    out = {"consts": consts}
    pos1 = np.arange(1, SEQ + 1, dtype=f)
    out["pool_inverse"] = np.ascontiguousarray(np.broadcast_to(
        np.concatenate([f(1) / np.minimum(pos1, f(w)) for w in POOL_WINDOWS]).reshape(1, -1), (P, 4 * SEQ))).astype(f)
    c = np.arange(SEQ)
    dist = (c[None, :] - 384 - i[:, None]).astype(f)
    out["key_minus_query"] = np.where(dist > 0, f(NEG * 1e3), dist).astype(f)
    end = np.arange(N_CMP) * CMP_STRIDE + CMP_LEN - 1
    slopes = np.exp2(-8.0 * np.arange(1, NSA_HEADS + 1) / NSA_HEADS)
    t = np.arange(SEQ)
    dc = t[:, None] - end[None, :]
    cb = np.where(dc[:, None, :] >= 0, -slopes[None, :, None] * dc[:, None, :], NEG)
    out["cmp_bias"] = np.ascontiguousarray(cb.reshape(TT, P, -1).transpose(1, 0, 2)).reshape(P, -1).astype(f)
    g = 128
    cc = 2 * np.pi * np.outer(np.arange(g), np.arange(g)) / g
    out["group_dft"] = np.concatenate([np.cos(cc), np.sin(cc)], 1).astype(f)
    for name, n in (("x", SEQ), ("c", CTX)):
        ss = 2 * np.pi * (np.outer(np.arange(n), np.arange(n)) % n) / n
        tiled = lambda a: np.ascontiguousarray(a.reshape(-1, P, a.shape[1]).transpose(1, 0, 2)).reshape(P, -1).astype(f)
        norm = (n * g) ** -0.5
        out["seq_dft_" + name] = np.stack([tiled(np.cos(ss) * norm), tiled(-np.sin(ss) * norm)])
        th = np.pi * (np.outer(np.arange(n), 2 * np.arange(n) + 1) % (4 * n)) / (2 * n)
        out["odd_dft_" + name] = np.stack([tiled(np.cos(th)), tiled(-np.sin(th)), tiled(np.cos(th).T / n), tiled(-np.sin(th).T / n)])
        pos = np.arange(n, dtype=f)
        tt = pos / f(max(n - 1, 1))
        bands = np.linspace(1e-4, (HY_EMB - 1) // 2 - 1, (HY_EMB - 1) // 2, dtype=f)
        ang = f(2.0 * math.pi / n) * pos[:, None] * bands[None, :]
        z = np.concatenate([tt[:, None], np.cos(ang), -np.sin(ang)], -1)
        out["hy_pos_" + name] = np.ascontiguousarray(z.T).astype(f)
        deltas = np.linspace(math.log(1e-2) / 0.3, math.log(1e-2) / 1.5, HY_CH, dtype=f)
        decay = np.exp(-tt[:, None] * np.abs(deltas)[None, :])
        out["hy_decay_" + name] = tiled(decay)
    rows = np.repeat(np.arange(SEQ // GRID_W, dtype=f), GRID_W)
    cols = np.tile(np.arange(GRID_W, dtype=f), SEQ // GRID_W)
    inv = (f(10000.0) ** (-np.arange(8, dtype=f) / 8)).astype(f)
    ar, ac = rows[None, :] * inv[:, None], cols[None, :] * inv[:, None]
    ang = np.concatenate([ar, ar, ac, ac])
    rope = np.zeros((P, 2 * SEQ), f)
    rope[MLA_NOPE:MLA_QK] = np.concatenate([np.cos(ang), np.sin(ang)], 1)
    out["rope"] = rope
    return out


def device_arrays(a):
    out = shape_constants()
    out["x"], out["mem"], out["ctx"] = by_feature(a["x"][0]), by_feature(a["mem"][0]), by_feature(a["ctx_2"][0])
    cond = np.stack([a["c_2"][0], a["c_ctx_2"]])
    out["vectors"] = pack(VECTORS, N_VECTORS, {
        "a_ln": columns(a["a_ln"]), "pool_scale": columns(a["a_pool_scale"]), "conv_w": columns(a["a_conv_w"][0]),
        "c_ln": columns(a["c_ln"]), "xa_ln": columns(a["xa_ln"]), "xa_mem_ln": columns(a["xa_mem_ln"]),
        "ff_ln": columns(a["ff_ln"]), "final_ln": columns(a["final_ln"]), "norm1": columns(a["norm1_2"]),
        "norm2": columns(a["norm2_2"]), "b_mod": columns(a["b_mod_2"]), "ffn_conv_w": columns(a["ffn_conv_w_2"]),
        "ffn_conv_b": columns(a["ffn_conv_b_2"]), "hy_conv_w": columns(a["hy_conv_w_2"]), "hy_conv_b": columns(a["hy_conv_b_2"]),
        "hy_bias": columns(a["hy_bias_2"]), "hy_b": columns(np.stack([a[f"hy_filt_b{i}_2"][0] for i in (1, 2, 3)])),
        "hy_freq": columns(a["hy_freq_2"]), "q_a_norm": columns(a["mla_q_a_norm_2"]), "kv_a_norm": columns(a["mla_kv_a_norm_2"]),
        "q_norm": columns(a["mla_q_norm_2"]), "k_norm": columns(a["mla_k_norm_2"]), "a_log": spread(a["a_a_log"]),
        "dt_bias": spread(a["a_dt_bias"]), "o_norm": spread(a["a_o_norm"]),
        "cond": by_feature(cond).reshape(P, 16),
    })
    w = a["a_w_in"][0]
    out["a_w_in"] = chunked(w[:, 0:2048], 512)
    out["a_w_gate"] = chunked(w[:, 2048:2560], 512)
    out["w_ba"] = chunked(w[:, 2560:2568], 8)[0]
    out["pool_w"] = np.ascontiguousarray(a["a_pool_w"][0].transpose(1, 0, 2)).reshape(P, -1)
    out["a_w_out"] = chunked(a["a_w_out"][0], 512)
    for l in range(2):
        for n in "qkvo":
            out[f"xa_w{n}_{l}"] = chunked(a[f"xa_w{n}"][l], 512)
        out[f"ff_w1_{l}"] = chunked(a["ff_w1"][l], 512)
        out[f"ff_w2_{l}"] = chunked(a["ff_w2"][l], P)
        up = a["ffn_w_up_2"][l].reshape(D, 2, FC // 2, 2 * P).transpose(0, 2, 1, 3).reshape(D, -1)
        out[f"ffn_up_{l}"] = chunked(up, 512)
        out[f"ffn_down_{l}"] = chunked(a["ffn_w_down_2"][l], P)
        out[f"w_mod_{l}"] = chunked(a["w_mod_2"][l], 512)
    w = a["c_w_in"][0]
    out["c_w_q"] = chunked(w[:, 0:1024], 512)
    out["c_w_c"] = chunked(w[:, 1024:1536], 512)
    kk = np.concatenate([w[:, 1536:1792], w[:, 2048:2304]], 1)
    out["c_w_k"] = chunked(kk, 512)
    out["c_w_v"] = chunked(np.concatenate([w[:, 1792:2048], w[:, 2304:2560]], 1), 512)
    out["w_gl"] = chunked(w[:, 2560:2608], 48)[0]
    for n in "kv":
        out["cmp_w1_" + n] = chunked(a[f"c_w1_{n}"][0], 128)
        out["cmp_w2_" + n] = np.ascontiguousarray(a[f"c_w2_{n}"][0])
        out["cmp_pe_" + n] = np.ascontiguousarray(a[f"c_pe_{n}"][0].reshape(16, 128).T)
    out["c_w_out"] = chunked(a["c_w_out"][0], 512)
    out["fh_w_in"] = chunked(a["fh_w_in_2"][0], 512)
    out["fh_w_out"] = chunked(a["fh_w_out_2"][0], 512)
    out["hy_w1"] = np.ascontiguousarray(a["hy_filt_w1_2"][0])
    out["hy_w23"] = np.concatenate([a["hy_filt_w2_2"][0], a["hy_filt_w3_2"][0]], 1)
    out["hy_w4"] = np.ascontiguousarray(a["hy_filt_w4_2"][0])
    out["mla_w_in"] = chunked(a["mla_w_in_2"][0], 416)
    out["mla_w_uq"] = chunked(a["mla_w_uq_2"][0], 1536)
    ukv = a["mla_w_ukv_2"][0].reshape(128, MLA_HEADS, 2, 64)
    out["mla_w_ukv"] = np.ascontiguousarray(ukv.transpose(0, 2, 1, 3)).reshape(1, P, 2048)
    out["mla_w_o"] = chunked(a["mla_w_o_2"][0], 512)
    return {n: np.ascontiguousarray(v, dtype=np.float32) if v.dtype != np.float32 else np.ascontiguousarray(v) for n, v in out.items()}




def kernel(**inputs):
    import concourse.bacc as bacc
    from concourse.bass_utils import run_bass_kernel_spmd

    arrays = device_arrays({n: np.asarray(v) for n, v in inputs.items()})
    nc = bacc.Bacc("TRN2", target_bir_lowering=False, num_devices=1)
    dram = {n: nc.dram_tensor("in_" + n, v.shape, mybir.dt.from_np(v.dtype), kind="ExternalInput").ap() for n, v in arrays.items()}
    out = nc.dram_tensor("out_x", (P, KT, SEQ), F32, kind="ExternalOutput").ap()
    build(nc, dram, out)
    r = run_bass_kernel_spmd(nc, [{"in_" + n: v for n, v in arrays.items()}], core_ids=[0])
    y = r.results[0]["out_x"]
    return np.ascontiguousarray(y.transpose(2, 1, 0)).reshape(1, SEQ, D)
```

```python
import math
from contextlib import ExitStack

import numpy as np

import concourse.bass as bass
import concourse.mybir as mybir

ACT = mybir.ActivationFunctionType
ALU = mybir.AluOpType
F32 = mybir.dt.float32
F32R = mybir.dt.float32r
AX_X = mybir.AxisListType.X

P = 128
BANK = 512
BANKS = 8
D = 1024
KT = D // P
SEQ, MEM, CTX = 512, 256, 256
TOK = SEQ + CTX
TT = SEQ // P
EPS = 1e-6
SLOT = 4096
ROWS_OF_CHUNK = 4
SMALL_ARENA = 31136 - 2 * (KT * SEQ + 2 * KT * P)
DN_HEADS, DN_CONV = 4, 4
POOL_WINDOWS = (2, 4, 8, 16)
FF_TILES = 4 * D // P
NSA_HEADS, NSA_GROUPS, NSA_DIM = 16, 4, 64
NSA_REP = NSA_HEADS // NSA_GROUPS
CMP_LEN, CMP_STRIDE = 32, 16
N_CMP = SEQ // CMP_STRIDE - CMP_LEN // CMP_STRIDE + 1
NEG = -1e30
XA_HEADS, XA_DIM = 4, 256
D_FF = 2816
FC = D_FF // P
HY_EMB, HY_WIDTH, HY_CH = 33, 64, 512
MLA_HEADS, MLA_NOPE, MLA_ROPE, MLA_V = 16, 64, 32, 64
MLA_QK = MLA_NOPE + MLA_ROPE
GRID_W = 64
ROUND = 1.5 * 2.0 ** 23
TWO_PI_HI = 6.28125
TWO_PI_LO = 2 * math.pi - TWO_PI_HI



def place(entries):
    at, n = {}, 0
    for name, width in entries:
        at[name] = (n, width)
        n += width
    return at, n


VECTORS, N_VECTORS = place([
    ("a_ln", 8), ("pool_scale", 4), ("conv_w", 4 * 12), ("c_ln", 8), ("xa_ln", 16), ("xa_mem_ln", 16), ("ff_ln", 16),
    ("final_ln", 8), ("norm1", 16), ("norm2", 16), ("b_mod", 96), ("ffn_conv_w", 2 * 3 * FC), ("ffn_conv_b", 2 * FC),
    ("hy_conv_w", 36), ("hy_conv_b", 12), ("hy_bias", 4), ("hy_b", 3), ("hy_freq", 1), ("q_a_norm", 2),
    ("kv_a_norm", 1), ("q_norm", 1), ("k_norm", 1), ("a_log", 4), ("dt_bias", 4), ("o_norm", P), ("cond", 16),
])
LEVELS = 7
CONSTS, N_CONSTS = place([
    ("ident", P), ("ones", P), ("upto", P), ("strip", 31), ("cmp_rows", 1), ("not_first", 1),
    ("rope_swap", 32),
])


class Counter:

    def __init__(self, nc, ctx, name):
        self.sem = ctx.enter_context(nc.semaphore(name))
        self.base = 0

    def at(self, n):
        return self.sem, self.base + n


class Kernel:

    def __init__(self, nc, ctx, dram):
        self.nc, self.ctx, self.dram = nc, ctx, dram
        self.counters = {}
        self.plan, self.loaded, self.pending = [], 0, []

        def sb(name, width):
            return ctx.enter_context(nc.sbuf_tensor(name, [P, width], F32))

        self.x_all = sb("x_all", KT * TOK)
        self.h_all = sb("h_all", KT * TOK)
        self.ring = sb("ring", 2 * SLOT)
        self.vec = sb("vec", N_VECTORS)
        self.const = sb("const", N_CONSTS)
        self.mods = sb("mods", 2 * 48 + 2 * 2 * 8)
        self.arena, self.arenas, self.arena_scope = None, 0, None
        self.placed = 0
        self.open_arena()
        ctx.callback(lambda: self.arena_scope.close())
        self.psum = ctx.enter_context(nc.psum_tensor("psum", [P, BANKS * BANK], F32))
        self.x = self.x_all[:, :].rearrange("p (k t) -> p k t", k=KT)
        self.h = self.h_all[:, :].rearrange("p (k t) -> p k t", k=KT)

    def open_arena(self, size=31136):
        self.arena_size = size
        self.arena_scope = ExitStack()
        self.arena = self.arena_scope.enter_context(self.nc.sbuf_tensor(f"arena_{self.arenas}", [P, self.arena_size], F32))
        self.arenas += 1

    def change_arena(self, size=31136):
        self.arena_scope.close()
        self.open_arena(size)

    def place_parts(self, operand_tiles=KT):
        scope = ExitStack()
        self.placed += 1
        views = {}
        for name, count, width in (("operand", operand_tiles, SEQ), ("weights", 2, KT * P)):
            for part in ("rounded", "rest"):
                tensor = scope.enter_context(self.nc.sbuf_tensor(f"{name}_{part}_{self.placed}", [P, count * width], F32R))
                views[f"{name}_{part}"] = tensor[:, :].rearrange("p (k n) -> p k n", k=count)
        return scope, views

    def counter(self, name):
        if name not in self.counters:
            self.counters[name] = Counter(self.nc, self.ctx, name)
        return self.counters[name]

    def v(self, name, i=0, n=None):
        at, width = VECTORS[name]
        return self.vec[:, at + i:at + (width if n is None else i + n)]

    def c(self, name, i=0, n=None):
        at, width = CONSTS[name]
        return self.const[:, at + i:at + (width if n is None else i + n)]

    def bank(self, b, n=BANK, parts=slice(0, P)):
        return self.psum[parts, b * BANK:b * BANK + n]

    def region(self, at, *shape):
        n = math.prod(shape)
        assert at + n <= self.arena_size, (at, shape)
        v = self.arena[:, at:at + n]
        names = " ".join("abcd"[:len(shape)])
        if len(shape) > 1:
            sizes = {c: s for c, s in zip("abcd", shape)}
            v = v.rearrange(f"p ({names}) -> p {names}", **sizes)
        return v

    def load_chunk(self, sp, w, chunk, slot):
        n = w["width"]
        src = w["ap"][bass.ds(chunk, 1)].rearrange("a p n -> p (a n)")
        sp.dma_start(self.ring[:, slot * SLOT:slot * SLOT + n], src).then_inc(self.counter(f"weights_landed_{slot}").sem, 16)

    def load_head(self, sp, w, upto):
        while w["ahead"] < min(upto, w["chunks"]):
            self.load_chunk(sp, w, w["ahead"], (w["first"] + w["ahead"]) % 2)
            w["ahead"] += 1

    def prefetch(self, sp, upto=2):
        if self.loaded < len(self.plan):
            self.load_head(sp, self.plan[self.loaded], upto)

    def load_later(self, pairs, name):
        self.pending.append((pairs, name))

    def start_loads(self, sp):
        for pairs, name in self.pending:
            for dst, src in pairs:
                sp.dma_start(dst, src).then_inc(self.counter(name).sem, 16)
        self.pending = []


def weight(dram, name, kt, cols, chunks):
    return {"name": name, "ap": dram[name], "kt": kt, "cols": cols, "chunks": chunks, "width": kt * cols, "ahead": 0, "first": 0}




def product(k, name, operand, groups, vector=None, scalar=None, loop=True, stationary="weight",
            tile=P, norm=None, parts=None):
    nc = k.nc
    w = k.plan[k.loaded]
    kt, cols, chunks = w["kt"], w["cols"], w["chunks"]
    mt = -(-cols // tile) if stationary == "weight" else 1
    tiles = mt * len(groups)
    in_body = 2 * tiles
    held = in_body if in_body <= BANKS else BANKS
    assert in_body % held == 0
    slots = [(w["first"] + s) % 2 for s in range(2)]
    landed = [k.counter(f"weights_landed_{slot}") for slot in slots]
    ready, drained = k.counter("product_ready"), k.counter("bank_drained")
    if parts:
        norm.parts = parts
    tile_rounded, tile_cut = k.counter("weight_tile_rounded"), k.counter("weight_tile_cut")
    pairs = chunks // 2
    looped = pairs if loop and pairs >= 2 else 0

    def over_chunks(engine, body):
        if looped:
            with engine.Fori(0, looped) as i:
                body(i, 0)
                body(i, 1)
        for c in range(2 * looped, chunks):
            body(c // 2, c % 2)

    with nc.Block() as block:

        @block.sync
        def _(sp):
            k.load_head(sp, w, 2)
            k.start_loads(sp)

            def refill(i, s):
                sp.wait_ge(*ready.at((i * 2 + s + 1) * tiles))
                k.load_chunk(sp, w, i * 2 + s + 2, slots[s])

            if chunks > 2:
                rest = chunks - 2
                if rest >= 4:
                    with sp.Fori(0, rest // 2) as i:
                        refill(i, 0)
                        refill(i, 1)
                    if rest % 2:
                        refill(rest // 2, 0)
                else:
                    for c in range(rest):
                        refill(c // 2, c % 2)
            k.loaded += 1
            if chunks > 1:
                sp.wait_ge(*ready.at((chunks - 1) * tiles))
            k.prefetch(sp, 1)
            sp.wait_ge(*ready.at(chunks * tiles))
            k.prefetch(sp)

        @block.tensor
        def _(pe):
            if norm:
                norm.sums(pe)

            def body(i, s):
                pe.wait_ge(*landed[s].at(i * 16 + 16))
                at = slots[s] * SLOT
                slot = k.ring[:, at:at + w["width"]].rearrange("p (k n) -> p k n", k=kt)
                for m in range(mt):
                    if parts:
                        pe.wait_ge(*tile_cut.at(i * (2 * mt) + (s * mt + m + 1)))
                    for g, (start, n) in enumerate(groups):
                        pos = s * tiles + m * len(groups) + g
                        pe.wait_ge(*drained.at(i * in_body + (pos - held + 1)))
                        width = min(tile, cols - m * tile)
                        if norm and pos < len(norm.jobs):
                            pe.wait_ge(*norm.read.at(pos + 1))
                        for t in range(kt):
                            if norm and s == 0 and m == 0:
                                pe.wait_ge(*norm.ready_at(start, t))
                            if stationary == "weight":
                                out = k.bank(pos % held, n, slice(0, width))
                                lhs, rhs = slot[:, t, m * tile:m * tile + width], operand(t, start, n)
                            else:
                                out = k.bank(pos % held, cols)
                                lhs, rhs = operand(t, start, n), slot[:, t, :]
                            if not (parts and start < SEQ):
                                mm = nc.tensor.matmul(out, lhs, rhs, start=(t == 0), stop=(t == kt - 1))
                                continue
                            top, rest = (parts[f"weights_{part}"][:, m % 2, t * P:(t + 1) * P] for part in ("rounded", "rest"))
                            top_in, rest_in = (parts[f"operand_{part}"][:, t, start:start + n] for part in ("rounded", "rest"))
                            nc.tensor.matmul(out, rest, top_in, start=(t == 0), stop=False)
                            nc.tensor.matmul(out, top, top_in, start=False, stop=False)
                            mm = nc.tensor.matmul(out, top, rest_in, start=False, stop=(t == kt - 1))
                        mm.then_inc(ready.sem, 1)

            over_chunks(pe, body)

        def round_tile(act, i, pair, s, m, free=False):
            if m == 0:
                act.wait_ge(*landed[s].at(i * 16 + 16 * (pair + 1)))
            if not free:
                act.wait_ge(*ready.at(i * in_body + (pair * in_body + (s * mt + m - 1) * len(groups))))
            act.activation(buffer("rounded", m), weight_tile(s, m), ACT.Copy).then_inc(tile_rounded.sem, 1)

        def subtract_tile(dve, i, pair, s, m, free=False):
            dve.wait_ge(*tile_rounded.at(i * (2 * mt) + ((2 * pair + s) * mt + m + 1)))
            dve.tensor_tensor(buffer("rest", m), weight_tile(s, m), buffer("rounded", m).bitcast(F32),
                              ALU.subtract).then_inc(tile_cut.sem, 1)

        def buffer(part, m):
            return parts[f"weights_{part}"][:, m % 2, :].rearrange("p (k n) -> p k n", k=kt)

        def weight_tile(s, m):
            at = slots[s] * SLOT
            return k.ring[:, at:at + w["width"]].rearrange("p (k n) -> p k n", k=kt)[:, :, m * P:(m + 1) * P]

        def finish(engine, take, cut):
            def body(i, s, last=False):
                for m in range(mt):
                    if parts and not (last and m == mt - 1):
                        following = s * mt + m + 1
                        cut(engine, i, following // (2 * mt), following // mt % 2, following % mt)
                    for g, (start, n) in enumerate(groups):
                        if take:
                            pos = s * tiles + m * len(groups) + g
                            engine.wait_ge(*ready.at(i * in_body + pos + 1))
                            take(engine, i * 2 + s, m, g, k.bank(pos % held), i * in_body + pos)

            if not parts:
                over_chunks(engine, body)
                return
            cut(engine, 0, 0, 0, 0, free=True)
            in_loop = (chunks - 1) // 2
            if in_loop > 1:
                with engine.Fori(0, in_loop) as i:
                    body(i, 0)
                    body(i, 1)
            for c in range(2 * in_loop if in_loop > 1 else 0, chunks):
                body(c // 2, c % 2, last=(c == chunks - 1))

        if vector or norm:
            @block.vector
            def _(dve):
                if norm:
                    norm.scale(dve)
                if vector or parts:
                    finish(dve, vector, subtract_tile)

        if scalar or norm:
            @block.scalar
            def _(act):
                if norm:
                    norm.guesses(act)
                if scalar or parts:
                    finish(act, scalar, round_tile)

    if norm:
        norm.close()
    if parts:
        tile_rounded.base += chunks * mt
        tile_cut.base += chunks * mt
    for s in range(2):
        landed[s].base += 16 * ((chunks + 1 - s) // 2)
    ready.base += chunks * tiles
    drained.base += chunks * tiles


def copy_out(k, dst):
    drained = k.counter("bank_drained")

    def take(act, chunk, m, g, bank, before):
        out = dst(chunk, m, g)
        act.activation(out, bank[0:out.shape[0], 0:out.shape[-1]], ACT.Copy).then_inc(drained.sem, 1)

    return take


def add_to_residual(k, mt, groups, gate=None):
    drained = k.counter("bank_drained")

    def take(dve, chunk, m, g, bank, before):
        start, n = groups[g]
        tile = chunk * mt + m
        x = k.x[:, bass.ds(tile, 1), start:start + n].rearrange("p a t -> p (a t)")
        if gate is None:
            dve.tensor_tensor(x, x, bank[:, 0:n], ALU.add).then_inc(drained.sem, 1)
        else:
            scale = gate[g][:, bass.ds(tile, 1)]
            dve.scalar_tensor_tensor(out=x, in0=bank[:, 0:n], scalar=scale, in1=x, op0=ALU.mult,
                                     op1=ALU.add).then_inc(drained.sem, 1)

    return take


def output_product(k, gate=None):
    k.change_arena(SMALL_ARENA)
    product_by_rows(k, k.h[:, :, 0:SEQ], gate)
    k.change_arena()


def product_by_rows(k, hidden, gate=None, start=0, n=SEQ):
    nc = k.nc
    w = k.plan[k.loaded]
    rows, chunks = w["kt"], w["chunks"]
    scope, parts = k.place_parts(2)
    slots = [(w["first"] + s) % 2 for s in range(2)]
    landed = [k.counter(f"weights_landed_{slot}") for slot in slots]
    ready, drained = k.counter("product_ready"), k.counter("bank_drained")
    rounded, cut, used = k.counter("row_tile_rounded"), k.counter("row_tile_cut"), k.counter("row_tile_used")
    free = 2
    in_loop = (chunks - 1) // 2

    def over_chunks(engine, body):
        body(0, 0)
        body(0, 1)
        if chunks == 2:
            return
        with engine.Fori(1, in_loop) as i:
            body(i, 0)
            body(i, 1)
        for c in range(2 * in_loop, chunks):
            body(c // 2, c % 2)

    def hidden_tile(i, s, r):
        return hidden[:, bass.ds(i * (2 * rows) + (s * rows + r), 1), :].rearrange("p a t -> p (a t)")

    def weight_rows(s, r):
        return k.ring[:, slots[s] * SLOT + r * D:slots[s] * SLOT + (r + 1) * D]

    with nc.Block() as block:

        @block.sync
        def _(sp):
            k.load_head(sp, w, 2)
            k.start_loads(sp)
            for c in range(2, chunks):
                sp.wait_ge(*used.at(free + rows * (c - 1)))
                k.load_chunk(sp, w, c, slots[c % 2])
            k.loaded += 1
            sp.wait_ge(*used.at(free + rows * (chunks - 1)))
            k.prefetch(sp, 1)
            sp.wait_ge(*ready.at(KT))
            k.prefetch(sp)

        @block.scalar
        def _(act):
            def body(i, s):
                for r in range(rows):
                    if r == 0:
                        act.wait_ge(*landed[s].at(i * 16 + 16))
                    act.wait_ge(*used.at(i * (2 * rows) + (s * rows + r + free - 1)))
                    act.activation(parts["weights_rounded"][:, r % 2, :], weight_rows(s, r), ACT.Copy).then_inc(rounded.sem, 1)
                    act.activation(parts["operand_rounded"][:, r % 2, 0:n], hidden_tile(i, s, r), ACT.Copy).then_inc(rounded.sem, 1)

            over_chunks(act, body)

        @block.vector
        def _(dve):
            def body(i, s):
                for r in range(rows):
                    dve.wait_ge(*rounded.at(i * (4 * rows) + (2 * (s * rows + r) + 2)))
                    dve.tensor_tensor(parts["weights_rest"][:, r % 2, :], weight_rows(s, r),
                                      parts["weights_rounded"][:, r % 2, :].bitcast(F32), ALU.subtract).then_inc(cut.sem, 1)
                    dve.tensor_tensor(parts["operand_rest"][:, r % 2, 0:n], hidden_tile(i, s, r),
                                      parts["operand_rounded"][:, r % 2, 0:n].bitcast(F32), ALU.subtract).then_inc(cut.sem, 1)

            over_chunks(dve, body)
            for m in range(KT):
                dve.wait_ge(*ready.at(m + 1))
                x = k.x[:, m, start:start + n]
                if gate is None:
                    dve.tensor_tensor(x, x, k.bank(m, n), ALU.add).then_inc(drained.sem, 1)
                else:
                    dve.scalar_tensor_tensor(out=x, in0=k.bank(m, n), scalar=gate[:, m:m + 1], in1=x, op0=ALU.mult,
                                             op1=ALU.add).then_inc(drained.sem, 1)

        @block.tensor
        def _(pe):
            pe.sem_inc(used.sem, free)
            pe.wait_ge(*drained.at(0))

            def body(i, s):
                for r in range(rows):
                    first = isinstance(i, int) and i == 0 and s == 0 and r == 0
                    last = isinstance(i, int) and 2 * i + s == chunks - 1 and r == rows - 1
                    pe.wait_ge(*cut.at(i * (4 * rows) + (2 * (s * rows + r) + 2)))
                    top_in, rest_in = (parts[f"operand_{part}"][:, r % 2, 0:n] for part in ("rounded", "rest"))
                    for m in range(KT):
                        top, rest = (parts[f"weights_{part}"][:, r % 2, m * P:(m + 1) * P] for part in ("rounded", "rest"))
                        nc.tensor.matmul(k.bank(m, n), rest, top_in, start=first, stop=False)
                        nc.tensor.matmul(k.bank(m, n), top, top_in, start=False, stop=False)
                        mm = nc.tensor.matmul(k.bank(m, n), top, rest_in, start=False, stop=last)
                        if last:
                            mm.then_inc(ready.sem, 1)
                    if not last:
                        mm.then_inc(used.sem, 1)

            over_chunks(pe, body)

    scope.close()
    for s in range(2):
        landed[s].base += 16 * ((chunks + 1 - s) // 2)
    rounded.base += 2 * rows * chunks
    cut.base += 2 * rows * chunks
    used.base += free + rows * chunks - 1
    ready.base += KT
    drained.base += KT




class Norm:

    def __init__(self, k, jobs, scratch):
        self.k, self.jobs = k, jobs
        self.squared, self.summed, self.guess = k.counter("norm_squared"), k.counter("norm_summed"), k.counter("norm_guess")
        self.a_step, self.v_step, self.scaled = k.counter("norm_act_step"), k.counter("norm_dve_step"), k.counter("norm_scaled")
        self.read, self.shifted = k.counter("norm_sums_read"), k.counter("norm_shifted")
        self.first, self.sq, self.rows = [], [], []
        at, total = scratch, 0
        for job in jobs:
            self.first.append(total)
            total += job[0]
            self.sq.append(k.region(at, job[0], job[1]))
            at += job[0] * job[1]
            self.rows.append(k.region(at, 4, job[1]))
            at += 4 * job[1]
        self.total = total
        self.parts = None
        self.tile_rounded, self.tile_cut = k.counter("norm_rounded"), k.counter("norm_cut")

    def is_cut(self, j):
        return self.parts is not None and self.jobs[j][7] < SEQ

    def ready_at(self, start, t):
        j = max(i for i, job in enumerate(self.jobs) if job[7] <= start)
        counter = self.scaled if self.jobs[j][5] is None else self.shifted
        if self.is_cut(j):
            counter = self.tile_cut
        return counter.at(self.first[j] + t + 1)

    def sums(self, pe):
        k = self.k
        for j, (tiles, n, src, dst, gain, shift, width, start) in enumerate(self.jobs):
            for t in range(tiles):
                pe.wait_ge(*self.squared.at(self.first[j] + t + 1))
                mm = pe.matmul(k.bank(j, n), k.c("ones"), self.sq[j][:, t, :], start=(t == 0), stop=(t == tiles - 1))
            mm.then_inc(self.summed.sem, 1)

    def guesses(self, act):
        k = self.k
        for j, (tiles, n, src, dst, gain, shift, width, start) in enumerate(self.jobs):
            for t in range(tiles):
                act.activation(self.sq[j][:, t, :], src(t), ACT.Square).then_inc(self.squared.sem, 1)
        for j, (tiles, n, src, dst, gain, shift, width, start) in enumerate(self.jobs):
            rows = self.rows[j]
            act.wait_ge(*self.summed.at(j + 1))
            act.activation(rows[:, 0, :], k.bank(j, n), ACT.Ln, scale=1.0 / width, bias=EPS).then_inc(self.a_step.sem, 1)
            act.wait_ge(*self.a_step.at(2 * j + 1))
            act.activation(rows[:, 1, :], rows[:, 0, :], ACT.Exp, scale=-0.5).then_inc(self.a_step.sem, 1)
            act.wait_ge(*self.a_step.at(2 * j + 2))
            act.activation(rows[:, 0, :], rows[:, 1, :], ACT.Square).then_inc(self.guess.sem, 1)
        for j, (tiles, n, src, dst, gain, shift, width, start) in enumerate(self.jobs):
            for t in range(tiles):
                nth = self.first[j] + t + 1
                if shift is not None:
                    act.wait_ge(*self.scaled.at(nth))
                    act.activation(dst(t), dst(t), ACT.Identity, bias=shift[:, t:t + 1]).then_inc(self.shifted.sem, 1)
                if self.is_cut(j):
                    act.wait_ge(*(self.scaled if shift is None else self.shifted).at(nth))
                    act.activation(self.parts["operand_rounded"][:, t, start:start + n], dst(t), ACT.Copy).then_inc(
                        self.tile_rounded.sem, 1)

    def scale(self, dve):
        k = self.k
        for j, (tiles, n, src, dst, gain, shift, width, start) in enumerate(self.jobs):
            rows = self.rows[j]
            dve.wait_ge(*self.a_step.at(2 * j + 1))
            dve.tensor_scalar(rows[:, 2, :], k.bank(j, n), 1.0 / width, EPS, ALU.mult, ALU.add).then_inc(self.read.sem, 1)
            dve.wait_ge(*self.read.at(j + 1))
            dve.wait_ge(*self.guess.at(j + 1))
            dve.scalar_tensor_tensor(out=rows[:, 3, :], in0=rows[:, 0, :], scalar=-0.5, in1=rows[:, 2, :],
                                     op0=ALU.mult, op1=ALU.mult).then_inc(self.v_step.sem, 1)
            dve.wait_ge(*self.v_step.at(2 * j + 1))
            dve.scalar_tensor_tensor(out=rows[:, 2, :], in0=rows[:, 3, :], scalar=1.5, in1=rows[:, 1, :],
                                     op0=ALU.add, op1=ALU.mult).then_inc(self.v_step.sem, 1)
            dve.wait_ge(*self.v_step.at(2 * j + 2))
            for t in range(tiles):
                dve.scalar_tensor_tensor(out=dst(t), in0=src(t), scalar=gain[:, t:t + 1], in1=rows[:, 2, :],
                                         op0=ALU.mult, op1=ALU.mult).then_inc(self.scaled.sem, 1)
            if self.is_cut(j):
                for t in range(tiles):
                    dve.wait_ge(*self.tile_rounded.at(self.first[j] + t + 1))
                    rounded, rest = (self.parts[f"operand_{part}"][:, t, start:start + n] for part in ("rounded", "rest"))
                    dve.tensor_tensor(rest, dst(t), rounded.bitcast(F32), ALU.subtract).then_inc(self.tile_cut.sem, 1)

    def close(self):
        n = len(self.jobs)
        cut = sum(job[0] for j, job in enumerate(self.jobs) if self.is_cut(j))
        for counter, steps in ((self.tile_rounded, cut), (self.tile_cut, cut), (self.squared, self.total), (self.summed, n), (self.guess, n), (self.read, n),
                               (self.a_step, 2 * n), (self.v_step, 2 * n), (self.scaled, self.total),
                               (self.shifted, sum(job[0] for job in self.jobs if job[5] is not None))):
            counter.base += steps

    def alone(self):
        with self.k.nc.Block() as block:

            @block.sync
            def _(sp):
                self.k.start_loads(sp)
                self.k.prefetch(sp)

            @block.tensor
            def _(pe):
                self.sums(pe)

            @block.scalar
            def _(act):
                self.guesses(act)

            @block.vector
            def _(dve):
                self.scale(dve)

        self.close()


def norm_of(k, start, n, gain, shift=None):
    return (KT, n, lambda t: k.x[:, t, start:start + n], lambda t: k.h[:, t, start:start + n], gain, shift, D, start)




def attention(k, units, scores, blocks, value_matmuls, finish, scale, arena, score_width, gates=None, bias=None, mask=None):
    nc = k.nc
    sb_banks = -(-score_width // BANK)
    probs = k.region(arena, 3, score_width)
    turned = k.region(arena + 3 * score_width, 2, score_width)
    small = k.region(arena + 5 * score_width, 4, 4)
    at = arena + 5 * score_width + 16
    biased = k.region(at, 2, score_width) if bias else None
    turn_bank, out_bank = 2 * sb_banks, 2 * sb_banks + 2
    assert out_bank + 2 <= BANKS
    s_ready, s_biased, s_max, s_shift = (k.counter(n) for n in ("scores_ready", "scores_biased", "scores_max", "scores_shift"))
    p_ready, p_sum, p_norm = (k.counter(n) for n in ("probs_ready", "probs_inverse", "probs_normed"))
    t_ready, t_copied, o_ready, o_copied = (k.counter(n) for n in ("turned_ready", "turned_copied", "heads_ready", "heads_copied"))
    pv_done = k.counter("values_used")
    U = len(units)
    part_of = []
    for u in range(U):
        b = blocks(u)
        half = 4 if len(b) <= 4 else 3
        part_of.append([b[i:i + half] for i in range(0, len(b), half)])
    parts_before = [0]
    for p in part_of:
        parts_before.append(parts_before[-1] + len(p))
    closes_before = [0]
    for u in units:
        closes_before.append(closes_before[-1] + int(u["closes"]))
    heads = closes_before[-1]

    def score_ap(u):
        return k.psum[:, (u % 2) * sb_banks * BANK:(u % 2) * sb_banks * BANK + units[u]["keys"]]

    with nc.Block() as block:

        @block.sync
        def _(sp):
            k.prefetch(sp)

        @block.tensor
        def _(pe):
            def score(u):
                if u >= 2:
                    pe.wait_ge(*(s_biased if bias else p_ready).at(u - 1))
                for cols, lhs, rhs, first, last in scores(u):
                    base = (u % 2) * sb_banks * BANK
                    mm = nc.tensor.matmul(k.psum[:, base + cols.start:base + cols.stop], lhs, rhs, start=first, stop=last)
                mm.then_inc(s_ready.sem, 1)

            def turn(u):
                pe.wait_ge(*p_norm.at(u + 1))
                for i, part in enumerate(part_of[u]):
                    n = parts_before[u] + i
                    if n >= 2:
                        pe.wait_ge(*t_copied.at(n - 1))
                    for j, (col, width) in enumerate(part):
                        mm = nc.tensor.transpose(k.bank(turn_bank + n % 2)[0:width, j * P:(j + 1) * P],
                                                 probs[:, u % 3, col:col + width], k.c("ident"))
                    mm.then_inc(t_ready.sem, 1)

            def values(u):
                pe.wait_ge(*t_copied.at(parts_before[u + 1]))
                h = closes_before[u]
                if units[u]["opens"] and h >= 2:
                    pe.wait_ge(*o_copied.at(h - 1))
                listed = value_matmuls(u, turned[:, u % 2, :])
                for rows, cols, lhs, rhs, first, last in listed:
                    mm = nc.tensor.matmul(k.bank(out_bank + h % 2)[rows, cols], lhs, rhs, start=first, stop=last)
                mm.then_inc(pv_done.sem, 1)

            for step in range(U + 3):
                if step < U:
                    score(step)
                if 2 <= step < U + 2:
                    turn(step - 2)
                if step >= 3:
                    values(step - 3)

        @block.scalar
        def _(act):
            def exponentials(u):
                n = units[u]["keys"]
                act.wait_ge(*s_shift.at(u + 1))
                if u >= 3:
                    act.wait_ge(*t_ready.at(parts_before[u - 2]))
                src = biased[:, u % 2, 0:n] if bias else score_ap(u)
                nc.scalar.activation(probs[:, u % 3, 0:n], src, ACT.Exp, scale=scale, bias=small[:, 1, u % 4:u % 4 + 1],
                                     accum_out=small[:, 2, u % 4:u % 4 + 1]).then_inc(p_ready.sem, 1)

            def copy_turned(u):
                if u >= 2:
                    act.wait_ge(*pv_done.at(u - 1))
                col = 0
                for i, part in enumerate(part_of[u]):
                    n = parts_before[u] + i
                    act.wait_ge(*t_ready.at(n + 1))
                    rows, width = part[0][1], len(part) * P
                    nc.scalar.activation(turned[0:rows, u % 2, col:col + width],
                                         k.bank(turn_bank + n % 2)[0:rows, 0:width], ACT.Copy).then_inc(t_copied.sem, 1)
                    col += width

            for step in range(U + 2):
                if step < U:
                    exponentials(step)
                if step >= 2:
                    copy_turned(step - 2)

        @block.vector
        def _(dve):
            def maximum(u):
                n = units[u]["keys"]
                dve.wait_ge(*s_ready.at(u + 1))
                src = score_ap(u)
                if bias:
                    table, factor = bias(u)
                    if u >= 2:
                        dve.wait_ge(*p_ready.at(u - 1))
                    nc.vector.scalar_tensor_tensor(out=biased[:, u % 2, 0:n], in0=table, scalar=factor, in1=src,
                                                   op0=ALU.mult, op1=ALU.add).then_inc(s_biased.sem, 1)
                    dve.wait_ge(*s_biased.at(u + 1))
                    src = biased[:, u % 2, 0:n]
                nc.vector.tensor_reduce(small[:, 0, u % 4:u % 4 + 1], src, AX_X, ALU.max).then_inc(s_max.sem, 1)
                dve.wait_ge(*s_max.at(u + 1))
                nc.vector.tensor_scalar(small[:, 1, u % 4:u % 4 + 1], small[:, 0, u % 4:u % 4 + 1], -scale, None,
                                        ALU.mult).then_inc(s_shift.sem, 1)

            def normalise(u):
                n = units[u]["keys"]
                dve.wait_ge(*p_ready.at(u + 1))
                nc.vector.reciprocal(small[:, 3, u % 4:u % 4 + 1], small[:, 2, u % 4:u % 4 + 1]).then_inc(p_sum.sem, 1)
                dve.wait_ge(*p_sum.at(u + 1))
                second = gates(u) if gates else None
                nc.vector.tensor_scalar(probs[:, u % 3, 0:n], probs[:, u % 3, 0:n], small[:, 3, u % 4:u % 4 + 1], second,
                                        ALU.mult, ALU.mult if gates else ALU.bypass).then_inc(p_norm.sem, 1)

            def copy_head(u):
                if units[u]["closes"]:
                    dve.wait_ge(*pv_done.at(u + 1))
                    dst, rows, cols = finish(u)
                    src = k.bank(out_bank + closes_before[u] % 2)[rows, cols]
                    if len(dst.shape) == 3:
                        src = src.rearrange("p (a t) -> p a t", a=dst.shape[1])
                    nc.vector.tensor_copy(dst, src).then_inc(o_copied.sem, 1)

            for step in range(U + 4):
                if step < U:
                    maximum(step)
                if 1 <= step <= U:
                    normalise(step - 1)
                if step >= 4:
                    copy_head(step - 4)

    for s in (s_ready, s_max, s_shift, p_ready, p_sum, p_norm, pv_done) + ((s_biased,) if bias else ()):
        s.base += U
    t_ready.base += parts_before[-1]
    t_copied.base += parts_before[-1]
    o_copied.base += heads




class Chain:

    def __init__(self, engine, counter):
        self.engine, self.count, self.n = engine, counter, 0

    def __call__(self, instruction):
        self.n += 1
        instruction.then_inc(self.count.sem, 1)
        self.engine.wait_ge(*self.count.at(self.n))


def load(k, pairs):
    landed = k.counter("operands_landed")
    with k.nc.Block() as block:

        @block.sync
        def _(sp):
            k.start_loads(sp)
            for dst, src in pairs:
                sp.dma_start(dst, src).then_inc(landed.sem, 16)
            sp.wait_ge(*landed.at(16 * len(pairs)))
            k.prefetch(sp)

    landed.base += 16 * len(pairs)


def arrived(k, name, count):
    with k.nc.Block() as block:

        @block.sync
        def _(sp):
            sp.wait_ge(*k.counter(name).at(16 * count))
            k.prefetch(sp)

    k.counter(name).base += 16 * count


def flat(ap):
    names = "bcd"[:len(ap.shape) - 1]
    return ap.rearrange(f"a {' '.join(names)} -> a ({' '.join(names)})")


def conv_taps(dve, step, out, src, taps, bias, reach, n):
    for j, (tap, r) in enumerate(zip(taps, reach)):
        if j == 0:
            if bias is None:
                step(dve.tensor_scalar(out[:, 0:n], src[:, 0:n], tap, None, ALU.mult))
            else:
                step(dve.tensor_scalar(out[:, 0:n], src[:, 0:n], tap, bias, ALU.mult, ALU.add))
        else:
            o = out[:, max(0, -r):n - max(0, r)]
            s = src[:, max(0, r):n - max(0, -r)]
            step(dve.scalar_tensor_tensor(out=o, in0=s, scalar=tap, in1=o, op0=ALU.mult, op1=ALU.add))




def pool_delta_inputs(k, U, QKV, G, norm):
    nc = k.nc
    drained, step, convolved = k.counter("bank_drained"), k.counter("conv_step"), k.counter("conv_ready")
    count = [0]

    def take(dve, chunk, m, g, bank, before):
        tile = chunk * 4 + m
        if tile < 4:
            dve.tensor_copy(U[:, tile, :], bank[:, 0:SEQ]).then_inc(drained.sem, 1)
            return
        j = tile - 4
        out = QKV[:, j, :]
        taps = [k.v("conv_w", tap * 12 + j, 1) for tap in range(DN_CONV)]

        def chained(ins):
            count[0] += 1
            ins.then_inc(step.sem, 1)
            dve.wait_ge(*step.at(count[0]))

        conv_taps(dve, chained, out, bank, taps[::-1], None, [0, -1, -2, -3], SEQ)
        dve.sem_inc(drained.sem, 1)
        dve.sem_inc(convolved.sem, 1)

    def silu(act, chunk, m, g, bank, before):
        tile = chunk * 4 + m
        if tile >= 4:
            act.wait_ge(*convolved.at(tile - 3))
            act.activation(QKV[:, tile - 4, :], QKV[:, tile - 4, :], ACT.Silu)

    product(k, "a_w_in", lambda t, s, n: k.h[:, t, s:s + n], [(0, SEQ)], vector=take, scalar=silu, loop=False, norm=norm)
    step.base += count[0]
    convolved.base += 12

    def gate(act, chunk, m, g, bank, before):
        act.activation(G[:, g, :], bank[:, 0:512], ACT.Silu).then_inc(drained.sem, 1)

    product(k, "a_w_gate", lambda t, s, n: k.h[:, t, s:s + n], [(i * P, P) for i in range(TT)], scalar=gate,
            stationary="tokens")


def delta_gates(k, wba, beta, ld, gcol, tmp):
    nc = k.nc
    made, a_step, v_step = k.counter("gates_product"), k.counter("gates_act"), k.counter("gates_dve")
    z, az, e, l, ea, eb = (tmp[:, i * 16:(i + 1) * 16] for i in range(6))
    ba = k.bank(0, 32).rearrange("p (t c) -> p t c", t=TT)

    def by_head(ap):
        return ap.rearrange("p (t h) -> p t h", t=TT)

    with nc.Block() as block:

        @block.sync
        def _(sp):
            k.prefetch(sp)

        @block.tensor
        def _(pe):
            for t in range(TT):
                for kt in range(KT):
                    mm = nc.tensor.matmul(k.bank(0)[:, t * 8:t * 8 + 8], k.h[:, kt, t * P:(t + 1) * P], wba[:, kt, :],
                                          start=(kt == 0), stop=(kt == KT - 1))
            mm.then_inc(made.sem, 1)
            pe.wait_ge(*v_step.at(12))
            nc.tensor.matmul(k.bank(1, 16), k.c("upto"), ld, start=True, stop=True).then_inc(made.sem, 1)

        @block.scalar
        def _(act):
            step = Chain(act, a_step)
            act.wait_ge(*made.at(1))
            step(nc.scalar.activation(by_head(eb), ba[:, :, 0:4], ACT.Exp, scale=-1.0))
            step(nc.scalar.activation(ea[:, 0:4], k.v("a_log"), ACT.Exp))
            act.wait_ge(*v_step.at(5))
            step(nc.scalar.activation(e, az, ACT.Exp, scale=-1.0))
            step(nc.scalar.activation(l, e, ACT.Ln, bias=1.0))

        @block.vector
        def _(dve):
            step = Chain(dve, v_step)
            dve.wait_ge(*a_step.at(2))
            for t in range(TT):
                step(nc.vector.tensor_tensor(by_head(z)[:, t, :], ba[:, t, 4:8], k.v("dt_bias"), ALU.add))
            step(nc.vector.scalar_tensor_tensor(out=az, in0=z, scalar=-1.0, in1=z, op0=ALU.mult, op1=ALU.max))
            step(nc.vector.tensor_scalar(eb, eb, 1.0, None, ALU.add))
            step(nc.vector.reciprocal(beta, eb))
            dve.wait_ge(*a_step.at(4))
            step(nc.vector.scalar_tensor_tensor(out=z, in0=z, scalar=0.0, in1=l, op0=ALU.max, op1=ALU.add))
            for t in range(TT):
                step(nc.vector.scalar_tensor_tensor(out=by_head(ld)[:, t, :], in0=by_head(z)[:, t, :], scalar=-1.0,
                                                    in1=ea[:, 0:4], op0=ALU.mult, op1=ALU.mult))
            dve.wait_ge(*made.at(2))
            step(nc.vector.tensor_copy(gcol, k.bank(1, 16)))

    made.base += 2
    a_step.base += 4
    v_step.base += 13


def pool_branch(k, U, pool_w, tmp, inverse_at):
    nc = k.nc
    v_step, made, meaned = k.counter("pool_step"), k.counter("pool_product"), k.counter("pool_mean")
    work = tmp[:, 0:2 * BANK].rearrange("p (a t) -> p a t", a=2)
    inv = inverse_at.rearrange("p (g t) -> p g t", g=4)
    mean = tmp[:, 6 * BANK:10 * BANK].rearrange("p (g t) -> p g t", g=4)
    n_steps = [0]
    with nc.Block() as block:

        @block.sync
        def _(sp):
            k.prefetch(sp)

        @block.vector
        def _(dve):
            step = Chain(dve, v_step)
            for g, window in enumerate(POOL_WINDOWS):
                src, r, b = U[:, g, :], 1, 0
                while r < window:
                    out = work[:, b, :]
                    step(nc.vector.tensor_copy(out[:, 0:r], src[:, 0:r]))
                    step(nc.vector.tensor_tensor(out[:, r:SEQ], src[:, r:SEQ], src[:, 0:SEQ - r], ALU.add))
                    src, r, b = out, 2 * r, 1 - b
                step(nc.vector.tensor_tensor(mean[:, g, :], src, inv[:, g, :], ALU.mult))
                nc.vector.tensor_tensor(mean[:, g, :], mean[:, g, :], U[:, g, :], ALU.subtract).then_inc(meaned.sem, 1)
            n_steps[0] = step.n

        @block.tensor
        def _(pe):
            for g in range(4):
                pe.wait_ge(*meaned.at(g + 1))
                nc.tensor.matmul(k.bank(g), pool_w[:, g, :], mean[:, g, :], start=True, stop=True).then_inc(made.sem, 1)

        @block.scalar
        def _(act):
            for g in range(4):
                act.wait_ge(*made.at(g + 1))
                nc.scalar.activation(k.h[:, g, 0:SEQ], k.bank(g), ACT.Copy, scale=k.v("pool_scale", g, 1))

    v_step.base += n_steps[0]
    made.base += 4
    meaned.base += 4


def inverse_rows(k, tiles, heads, squares, rows, n_list, src_rows=P, scale=1.0, sel=None):
    nc = k.nc
    squared, summed = k.counter("rows_squared"), k.counter("rows_summed")
    a_step, v_step = k.counter("rows_act"), k.counter("rows_dve")
    strip = k.c("strip")
    nb = len(n_list)
    with nc.Block() as block:

        @block.sync
        def _(sp):
            k.prefetch(sp)

        @block.scalar
        def _(act):
            for j in range(heads):
                if j >= 2:
                    act.wait_ge(*summed.at(nb * (j - 1)))
                o = 0
                for n in n_list:
                    nc.scalar.activation(squares[0:src_rows, j % 2, o:o + n], tiles(j)[:, o:o + n], ACT.Square).then_inc(squared.sem, 1)
                    o += n
            step = Chain(act, a_step)
            act.wait_ge(*summed.at(nb * heads))
            o = 0
            for b, n in enumerate(n_list):
                step(nc.scalar.activation(rows[0:heads, 0, o:o + n], k.bank(b, n, slice(0, heads)), ACT.Ln, scale=scale, bias=EPS))
                step(nc.scalar.activation(rows[0:heads, 1, o:o + n], rows[0:heads, 0, o:o + n], ACT.Exp, scale=-0.5))
                step(nc.scalar.activation(rows[0:heads, 0, o:o + n], rows[0:heads, 1, o:o + n], ACT.Square))
                o += n

        @block.tensor
        def _(pe):
            for j in range(heads):
                o = 0
                for b, n in enumerate(n_list):
                    pe.wait_ge(*squared.at(nb * j + b + 1))
                    nc.tensor.matmul(k.bank(b, n, slice(0, heads)), strip[0:src_rows, 15 - j:15 - j + heads],
                                     squares[0:src_rows, j % 2, o:o + n], start=(j == 0), stop=(j == heads - 1)).then_inc(summed.sem, 1)
                    o += n

        @block.vector
        def _(dve):
            step = Chain(dve, v_step)
            o = 0
            for b, n in enumerate(n_list):
                dve.wait_ge(*a_step.at(3 * b + 3))
                r = [rows[0:heads, i, o:o + n] for i in range(4)]
                step(nc.vector.tensor_scalar(r[2], k.bank(b, n, slice(0, heads)), scale, EPS, ALU.mult, ALU.add))
                step(nc.vector.scalar_tensor_tensor(out=r[3], in0=r[0], scalar=-0.5, in1=r[2], op0=ALU.mult, op1=ALU.mult))
                step(nc.vector.scalar_tensor_tensor(out=r[2], in0=r[3], scalar=1.5, in1=r[1], op0=ALU.add, op1=ALU.mult))
                o += n

    squared.base += nb * heads
    summed.base += nb * heads
    a_step.base += 3 * nb
    v_step.base += 3 * nb
    return rows[:, 2, :]


def spread_rows(k, rows, jobs):
    nc = k.nc
    made, used = k.counter("spread_ready"), k.counter("spread_used")
    with nc.Block() as block:

        @block.sync
        def _(sp):
            k.prefetch(sp)

        @block.tensor
        def _(pe):
            for i, (j, heads, parts, start, n, outs) in enumerate(jobs):
                if i >= BANKS:
                    pe.wait_ge(*used.at(i - BANKS + 1))
                lhs = k.c("ident")[0:heads, j:j + 1].to_broadcast([heads, parts])
                nc.tensor.matmul(k.bank(i % BANKS, n, slice(0, parts)), lhs, rows[0:heads, start:start + n],
                                 start=True, stop=True).then_inc(made.sem, 1)

        @block.vector
        def _(dve):
            for i, (j, heads, parts, start, n, outs) in enumerate(jobs):
                dve.wait_ge(*made.at(i + 1))
                for dst, src, factor in outs:
                    lo = dst[1]
                    bank = k.bank(i % BANKS, n, slice(lo, lo + dst[0].shape[0]))
                    op = nc.vector.scalar_tensor_tensor(out=dst[0], in0=bank, scalar=factor, in1=src,
                                                        op0=ALU.mult, op1=ALU.mult)
                op.then_inc(used.sem, 1)

    made.base += len(jobs)
    used.base += len(jobs)


def delta_rule(k, masks, QKV, beta, ld, gcol, col, A, attn, kdec, kbg, vb, dec, erow, Xi, XT, Aoff, WTs, G):
    nc = k.nc
    Q, K, V = QKV[:, 0:4, :], QKV[:, 4:8, :], QKV[:, 8:12, :]
    units = [(c, h) for c in range(TT) for h in range(DN_HEADS)]
    S2 = k.counter
    a, v, p = S2("delta_act"), S2("delta_dve"), S2("delta_pe")
    egc, ekd, ebg, ngc = (col[:, i * 16:(i + 1) * 16] for i in range(4))
    ldb = WTs

    def u128(ap, j):
        return ap[:, j * P:(j + 1) * P]

    with nc.Block() as block:

        @block.gpsimd
        def _(pool):
            for j in range(16):
                op = nc.gpsimd.tensor_copy(u128(ldb, j), ld[:, j:j + 1].to_broadcast([P, P]))
            op.then_inc(v.sem, 1)

        @block.tensor
        def _(pe):
            pe.wait_ge(*v.at(1))
            for j in range(16):
                mm = nc.tensor.matmul(k.psum[:, j * P:(j + 1) * P], u128(ldb, j), k.c("upto"), start=True, stop=True)
            mm.then_inc(p.sem, 1)

        @block.vector
        def _(dve):
            dve.wait_ge(*a.at(1))
            for j in range(16):
                g = gcol[:, j:j + 1]
                row = k.psum[:, j * P:(j + 1) * P]
                nc.vector.tensor_scalar(u128(dec, j), row, g, 0.0, ALU.subtract, ALU.max)
                nc.vector.tensor_scalar(u128(Xi, j), row, g, 0.0, ALU.subtract, ALU.min)
                op = nc.vector.tensor_tensor(ekd[:, j:j + 1], row[:, P - 1:P], g, ALU.subtract)
            op.then_inc(S2("delta_diff").sem, 1)

        @block.scalar
        def _(act):
            act.wait_ge(*p.at(1))
            nc.scalar.activation(egc, gcol, ACT.Exp)
            nc.scalar.activation(erow[:, :], k.psum[:, 0:16 * P], ACT.Exp).then_inc(a.sem, 1)
            act.wait_ge(*S2("delta_diff").at(1))
            nc.scalar.activation(dec[:, :], dec[:, :], ACT.Exp, scale=-1.0)
            nc.scalar.activation(Xi[:, :], Xi[:, :], ACT.Exp)
            nc.scalar.activation(ekd, ekd, ACT.Exp)

    v.base += 1
    p.base += 1
    a.base += 1
    S2("delta_diff").base += 1

    with nc.Block() as block:

        @block.tensor
        def _(pe):
            for n in range(8):
                c = n % 4
                for h in range(4):
                    rhs = (K if n < 4 else Q)[:, h, c * P:(c + 1) * P]
                    mm = nc.tensor.matmul(k.bank(n)[:, h * P:(h + 1) * P], K[:, h, c * P:(c + 1) * P], rhs, start=True, stop=True)
                mm.then_inc(p.sem, 1)

        @block.vector
        def _(dve):
            dve.tensor_tensor(ebg, beta, egc, ALU.mult)
            for c in range(4):
                dve.wait_ge(*p.at(c + 1))
                for h in range(4):
                    j = c * 4 + h
                    nc.vector.scalar_tensor_tensor(out=u128(A, j), in0=k.bank(c)[:, h * P:(h + 1) * P], scalar=beta[:, j:j + 1],
                                                   in1=u128(dec, j), op0=ALU.mult, op1=ALU.mult)
            for c in range(4):
                dve.wait_ge(*p.at(c + 5))
                op = nc.vector.tensor_tensor(attn[:, c * 512:(c + 1) * 512], k.bank(4 + c), Xi[:, c * 512:(c + 1) * 512], ALU.mult)
                op.then_inc(v.sem, 1)
                dve.wait_ge(*v.at(c + 1))
                for h in range(4):
                    j = c * 4 + h
                    nc.vector.tensor_tensor(u128(attn, j), u128(attn, j), k.c("upto"), ALU.mult)

        @block.gpsimd
        def _(pool):
            pool.wait_ge(*p.at(8))
            for c in range(4):
                for h in range(4):
                    q = Q[:, h, c * P:(c + 1) * P]
                    nc.gpsimd.tensor_tensor(q, q, u128(erow, c * 4 + h), ALU.mult)

    p.base += 8
    v.base += 4

    with nc.Block() as block:

        @block.tensor
        def _(pe):
            for n in range(8):
                c = n % 4
                for h in range(4):
                    src = (K if n < 4 else V)[:, h, c * P:(c + 1) * P]
                    mm = nc.tensor.transpose(k.bank(n)[:, h * P:(h + 1) * P], src, k.c("ident"))
                mm.then_inc(p.sem, 1)

        @block.vector
        def _(dve):
            for c in range(4):
                dve.wait_ge(*p.at(c + 1))
                for h in range(4):
                    j = c * 4 + h
                    src = k.bank(c)[:, h * P:(h + 1) * P]
                    nc.vector.tensor_scalar(u128(kbg, j), src, ebg[:, j:j + 1], None, ALU.mult)
                    op = nc.vector.tensor_scalar(u128(kdec, j), src, ekd[:, j:j + 1], None, ALU.mult)

        @block.scalar
        def _(act):
            for c in range(4):
                act.wait_ge(*p.at(c + 5))
                for h in range(4):
                    j = c * 4 + h
                    nc.scalar.activation(u128(vb, j), k.bank(4 + c)[:, h * P:(h + 1) * P], ACT.Copy, scale=beta[:, j:j + 1])

        @block.gpsimd
        def _(pool):
            for j in range(16):
                nc.gpsimd.tensor_copy(u128(Xi, j), k.c("ident"))
                nc.gpsimd.tensor_copy(u128(XT, j), k.c("ident"))

    p.base += 8

    masked, turned, joined, copied = (S2(n) for n in ("level_masked", "level_turned", "level_joined", "level_copied"))
    updated = S2("level_updated")
    with nc.Block() as block:

        @block.gpsimd
        def _(pool):
            for level in range(LEVELS):
                mask = masks[:, level * P:(level + 1) * P]
                for c in range(4):
                    if level:
                        pool.wait_ge(*turned.at(4 * (level - 1) + c + 1))
                    for h in range(4):
                        op = nc.gpsimd.tensor_tensor(u128(Aoff, c * 4 + h), u128(A, c * 4 + h), mask, ALU.mult)
                    op.then_inc(masked.sem, 1)

        @block.tensor
        def _(pe):
            for level in range(LEVELS):
                for c in range(4):
                    n = 4 * level + c
                    pe.wait_ge(*masked.at(n + 1))
                    if level:
                        pe.wait_ge(*updated.at(n - 3))
                    b = 3 * (c % 2)
                    if n >= 2:
                        pe.wait_ge(*copied.at(n - 1))
                    for h in range(4):
                        j = c * 4 + h
                        mm = nc.tensor.matmul(k.bank(b)[:, h * P:(h + 1) * P], u128(Aoff, j), u128(XT, j), start=True, stop=True)
                    mm.then_inc(turned.sem, 1)
                    pe.wait_ge(*copied.at(n + 1))
                    if n >= 2:
                        pe.wait_ge(*updated.at(n - 1))
                    for h in range(4):
                        j = c * 4 + h
                        nc.tensor.matmul(k.bank(b + 1)[:, h * P:(h + 1) * P], u128(WTs, j), u128(Xi, j), start=True, stop=True)
                        mm = nc.tensor.matmul(k.bank(b + 2)[:, h * P:(h + 1) * P], u128(Xi, j), u128(WTs, j), start=True, stop=True)
                    mm.then_inc(joined.sem, 1)

        @block.scalar
        def _(act):
            for level in range(LEVELS):
                for c in range(4):
                    n = 4 * level + c
                    act.wait_ge(*turned.at(n + 1))
                    nc.scalar.activation(WTs[:, c * 512:(c + 1) * 512], k.bank(3 * (c % 2)), ACT.Copy).then_inc(copied.sem, 1)

        @block.vector
        def _(dve):
            for level in range(LEVELS):
                for c in range(4):
                    n = 4 * level + c
                    dve.wait_ge(*joined.at(n + 1))
                    b = 3 * (c % 2)
                    x, xt = Xi[:, c * 512:(c + 1) * 512], XT[:, c * 512:(c + 1) * 512]
                    nc.vector.tensor_tensor(x, x, k.bank(b + 1), ALU.subtract)
                    nc.vector.tensor_tensor(xt, xt, k.bank(b + 2), ALU.subtract).then_inc(updated.sem, 1)

    for s in (masked, turned, joined, copied, updated):
        s.base += 4 * LEVELS

    wT, u_ = A, dec
    with nc.Block() as block:

        @block.tensor
        def _(pe):
            for c in range(4):
                for h in range(4):
                    j = c * 4 + h
                    nc.tensor.matmul(k.bank(2 * c)[:, h * P:(h + 1) * P], u128(kbg, j), u128(XT, j), start=True, stop=True)
                    mm = nc.tensor.matmul(k.bank(2 * c + 1)[:, h * P:(h + 1) * P], u128(XT, j), u128(vb, j), start=True, stop=True)
                mm.then_inc(p.sem, 1)

        @block.vector
        def _(dve):
            for c in range(4):
                dve.wait_ge(*p.at(c + 1))
                nc.vector.tensor_copy(wT[:, c * 512:(c + 1) * 512], k.bank(2 * c))

        @block.scalar
        def _(act):
            for c in range(4):
                act.wait_ge(*p.at(c + 1))
                nc.scalar.activation(u_[:, c * 512:(c + 1) * 512], k.bank(2 * c + 1), ACT.Copy)

    p.base += 4

    state = Xi[:, 0:1024].rearrange("p (b n) -> p b n", b=2)
    vnew = Xi[:, 1024:2048].rearrange("p (b n) -> p b n", b=2)
    O = kbg
    inner, outer, news, states, outs = (S2(n) for n in ("scan_inner", "scan_outer", "scan_new", "scan_state", "scan_out"))
    with nc.Block() as block:

        @block.tensor
        def _(pe):
            for c in range(4):
                if c:
                    pe.wait_ge(*states.at(c))
                    for h in range(4):
                        mm = nc.tensor.matmul(k.bank(0)[:, h * P:(h + 1) * P], u128(wT, c * 4 + h), state[:, (c - 1) % 2, h * P:(h + 1) * P],
                                              start=True, stop=True)
                    mm.then_inc(inner.sem, 1)
                pe.wait_ge(*news.at(c + 1))
                if c >= 2:
                    pe.wait_ge(*outs.at(c - 1))
                for h in range(4):
                    j = c * 4 + h
                    out = k.bank(2 + c % 2)[:, h * P:(h + 1) * P]
                    if c:
                        nc.tensor.matmul(out, Q[:, h, c * P:(c + 1) * P], state[:, (c - 1) % 2, h * P:(h + 1) * P], start=True, stop=False)
                    nc.tensor.matmul(out, u128(attn, j), vnew[:, c % 2, h * P:(h + 1) * P], start=(c == 0), stop=True)
                    mm = nc.tensor.matmul(k.bank(1)[:, h * P:(h + 1) * P], u128(kdec, j), vnew[:, c % 2, h * P:(h + 1) * P],
                                          start=True, stop=True)
                mm.then_inc(outer.sem, 1)

        @block.vector
        def _(dve):
            for c in range(4):
                u = u_[:, c * 512:(c + 1) * 512]
                if c:
                    dve.wait_ge(*inner.at(c))
                    nc.vector.tensor_tensor(vnew[:, c % 2, :], u, k.bank(0), ALU.subtract).then_inc(news.sem, 1)
                else:
                    nc.vector.tensor_copy(vnew[:, 0, :], u).then_inc(news.sem, 1)
                dve.wait_ge(*outer.at(c + 1))
                if c == 3:
                    break
                if c:
                    for h in range(4):
                        j = c * 4 + h
                        left = erow[:, j * P + P - 1:j * P + P]
                        op = nc.vector.scalar_tensor_tensor(
                            out=state[:, c % 2, h * P:(h + 1) * P], in0=state[:, (c - 1) % 2, h * P:(h + 1) * P],
                            scalar=left, in1=k.bank(1)[:, h * P:(h + 1) * P], op0=ALU.mult, op1=ALU.add)
                else:
                    op = nc.vector.tensor_copy(state[:, 0, :], k.bank(1))
                op.then_inc(states.sem, 1)

        @block.scalar
        def _(act):
            for c in range(4):
                act.wait_ge(*outer.at(c + 1))
                nc.scalar.activation(O[:, c * 512:(c + 1) * 512], k.bank(2 + c % 2), ACT.Copy).then_inc(outs.sem, 1)

    inner.base += 3
    outer.base += 4
    news.base += 4
    states.base += 3
    outs.base += 4

    sums, y = col[:, 64:80], col[:, 80:144]
    sq = kdec
    with nc.Block() as block:

        @block.scalar
        def _(act):
            nc.scalar.activation(sq[:, :], O[:, :], ACT.Square).then_inc(a.sem, 1)
            act.wait_ge(*v.at(1))
            step = [1]

            def chained(ins):
                step[0] += 1
                ins.then_inc(a.sem, 1)
                act.wait_ge(*a.at(step[0]))

            chained(nc.scalar.activation(y[:, 0:16], sums, ACT.Ln, scale=1.0 / P, bias=EPS))
            chained(nc.scalar.activation(y[:, 16:32], y[:, 0:16], ACT.Exp, scale=-0.5))
            chained(nc.scalar.activation(y[:, 0:16], y[:, 16:32], ACT.Square))

        @block.vector
        def _(dve):
            step = Chain(dve, v)
            dve.wait_ge(*a.at(1))
            step(nc.vector.tensor_reduce(sums, sq[:, :].rearrange("p (j d) -> p j d", d=P), AX_X, ALU.add))
            dve.wait_ge(*a.at(4))
            step(nc.vector.tensor_scalar(y[:, 32:48], sums, 1.0 / P, EPS, ALU.mult, ALU.add))
            step(nc.vector.scalar_tensor_tensor(out=y[:, 48:64], in0=y[:, 0:16], scalar=-0.5, in1=y[:, 32:48], op0=ALU.mult, op1=ALU.mult))
            step(nc.vector.scalar_tensor_tensor(out=y[:, 32:48], in0=y[:, 48:64], scalar=1.5, in1=y[:, 16:32], op0=ALU.add, op1=ALU.mult))
            for j in range(16):
                op = nc.vector.scalar_tensor_tensor(out=u128(O, j), in0=u128(O, j), scalar=y[:, 32 + j:33 + j], in1=k.v("o_norm"),
                                                    op0=ALU.mult, op1=ALU.mult)
            step(op)
            gate = G.rearrange("p t n -> p (t n)")
            step(nc.vector.tensor_tensor(O[:, :], O[:, :], gate, ALU.mult))

        @block.tensor
        def _(pe):
            pe.wait_ge(*v.at(6))
            for h in range(4):
                for c in range(4):
                    mm = nc.tensor.transpose(k.bank(h)[:, c * P:(c + 1) * P], u128(O, c * 4 + h), k.c("ident"))
                mm.then_inc(p.sem, 1)

    a.base += 4
    v.base += 6
    p.base += 4
    with nc.Block() as block:

        @block.scalar
        def _(act):
            for h in range(4):
                nc.scalar.activation(k.h[:, 4 + h, 0:SEQ], k.bank(h), ACT.Copy)


def pool_delta_layer(k):
    U, QKV, G = k.region(0, 4, 512), k.region(2048, 12, 512), k.region(8192, 4, 512)
    small = k.region(10240, 256)
    beta, ld, gcol, tmp = small[:, 0:16], small[:, 16:32], small[:, 32:48], small[:, 48:144]
    r = lambda at: k.region(at, 2048)
    norm = Norm(k, [norm_of(k, 0, SEQ, k.v("a_ln"))], 18688)
    masks = k.region(28928, LEVELS * P)
    wba, pool_w = k.region(10496, 8, 8), k.region(10560, 4, P)
    ptmp = k.region(18688, 10 * 512)
    inverse_at = k.region(12544, 2048)
    k.load_later([(flat(wba), k.dram["w_ba"]), (flat(pool_w), k.dram["pool_w"]), (inverse_at, k.dram["pool_inverse"]),
                  (masks, k.dram["level_masks"])], "pool_landed")
    pool_delta_inputs(k, U, QKV, G, norm)
    arrived(k, "pool_landed", 4)
    delta_gates(k, wba, beta, ld, gcol, tmp)
    pool_branch(k, U, pool_w, ptmp, inverse_at)
    rows = k.region(20000, 4, 512)
    inverse = inverse_rows(k, lambda j: QKV[:, j, :], 8, k.region(18688, 2, 512), rows, [SEQ])
    spread_rows(k, inverse, [(j, 8, P, 0, SEQ, [((QKV[:, j, :], 0), QKV[:, j, :], float(P) ** -0.5 if j < 4 else 1.0)])
                             for j in range(8)])
    delta_rule(k, masks, QKV, beta, ld, gcol, small[:, 48:192], r(14592), r(16640), r(18688), r(20736), r(22784), r(24832), r(26880),
               r(10496), r(12544), r(0), k.h_all[:, 4096:6144], G)
    output_product(k)




def cross_attention_layer(k, l):
    mem = k.region(0, KT, MEM)
    Q, K, V = k.region(2048, KT, SEQ), k.region(6144, KT, MEM), k.region(8192, 2, D)
    load(k, [(mem, k.dram["mem"])])
    norm = Norm(k, [norm_of(k, 0, SEQ, k.v("xa_ln", 8 * l, 8)),
                    (KT, MEM, lambda t: mem[:, t, :], lambda t: k.h[:, t, SEQ:TOK], k.v("xa_mem_ln", 8 * l, 8), None, D, SEQ)], 20000)
    drained = k.counter("bank_drained")
    tokens = lambda t, s, n: k.h[:, t, s:s + n]
    product(k, "xa_wq", tokens, [(0, SEQ)], scalar=copy_out(k, lambda c, m, g: Q[:, 4 * c + m, :]), norm=norm)
    product(k, "xa_wk", tokens, [(SEQ, MEM)], scalar=copy_out(k, lambda c, m, g: K[:, 4 * c + m, :]))
    product(k, "xa_wv", tokens, [(SEQ, P), (SEQ + P, P)], stationary="tokens",
            scalar=copy_out(k, lambda c, m, g: V[:, g, 512 * c:512 * c + 512]))
    heads = [(h, t) for h in range(XA_HEADS) for t in range(TT)]
    units = [{"keys": MEM, "opens": t % 2 == 0, "closes": t % 2 == 1} for h, t in heads]

    def scores(u):
        h, t = heads[u]
        return [(slice(0, MEM), Q[:, 2 * h + j, t * P:(t + 1) * P], K[:, 2 * h + j, :], j == 0, j == 1) for j in range(2)]

    def values(u, weights):
        h, t = heads[u]
        return [(slice(0, P), slice(half * 256 + (t % 2) * P, half * 256 + (t % 2) * P + P),
                 V[:, kb, h * XA_DIM + half * P:h * XA_DIM + half * P + P], weights[:, kb * P:(kb + 1) * P], kb == 0, kb == 1)
                for half in range(2) for kb in range(2)]

    def finish(u):
        h, t = heads[u]
        return k.h[:, 2 * h:2 * h + 2, (t // 2) * 256:(t // 2) * 256 + 256], slice(0, P), slice(0, 512)

    attention(k, units, scores, lambda u: [(0, P), (P, P)], values, finish, XA_DIM ** -0.5, 12000, MEM)
    output_product(k)


def squared_relu_layer(k, l):
    k.change_arena(SMALL_ARENA)
    parts_scope, parts = k.place_parts()
    hidden = k.region(0, FF_TILES, SEQ)
    positive = k.region(FF_TILES * SEQ, 2, SEQ)
    drained, rectified = k.counter("bank_drained"), k.counter("rectified")
    norm = Norm(k, [norm_of(k, 0, SEQ, k.v("ff_ln", 8 * l, 8))], 8192)

    def relu(act, chunk, m, g, bank, before):
        act.wait_ge(*drained.at(before - 1))
        act.activation(positive[:, m % 2, :], bank[:, 0:SEQ], ACT.Relu).then_inc(rectified.sem, 1)

    def square(dve, chunk, m, g, bank, before):
        dve.wait_ge(*rectified.at(before + 1))
        out = hidden[:, bass.ds(chunk * 4 + m, 1), :].rearrange("p a t -> p (a t)")
        dve.scalar_tensor_tensor(out=out, in0=bank[:, 0:SEQ], scalar=0.0, in1=positive[:, m % 2, :], op0=ALU.max,
                                 op1=ALU.mult).then_inc(drained.sem, 1)

    product(k, "ff_w1", lambda t, s, n: k.h[:, t, s:s + n], [(0, SEQ)], scalar=relu, vector=square, norm=norm,
            parts=parts)
    parts_scope.close()
    rectified.base += FF_TILES
    product_by_rows(k, hidden)
    k.change_arena()




def nsa_layer(k):
    nc = k.nc
    Q, KS, KW = k.region(0, KT, SEQ), k.region(4096, 4, SEQ), k.region(6144, 4, SEQ)
    V, gates = k.region(8192, TT, 512), k.region(10240, TT, 48)
    w1 = [k.region(10500, 16, P), k.region(12548, 16, P)]
    w2 = [k.region(14596, P), k.region(14724, NSA_DIM)]
    pe = [k.region(14788, 16), k.region(14804, 16)]
    pebias = k.region(14820, 4)
    hid = [k.region(14824, 4 * N_CMP), k.region(14948, 4 * N_CMP)]
    CK, CV = k.region(15072, 4, N_CMP), k.region(15196, 4, NSA_DIM)
    pcT = k.region(15460, NSA_HEADS, SEQ)
    cmp_bias = k.region(23660, TT, NSA_HEADS * N_CMP)
    pc = k.region(25650, 2, NSA_HEADS * N_CMP)
    KC = [k.region(15460, 4, SEQ), k.region(17508, 4, SEQ)]
    wgl = k.region(19556, KT, 48)
    table = k.region(30300, 512)
    small = k.region(26642, 4, NSA_HEADS)
    tokens = lambda t, s, n: k.h[:, t, s:s + n]
    drained = k.counter("bank_drained")
    k.load_later([(flat(wgl), k.dram["w_gl"]), (flat(w1[0]), k.dram["cmp_w1_k"][0]), (flat(w1[1]), k.dram["cmp_w1_v"][0]),
             (w2[0][:, 0:64], k.dram["cmp_w2_k"]), (w2[0][:, 64:128], k.dram["cmp_w2_k"]), (w2[1], k.dram["cmp_w2_v"]),
             (pe[0], k.dram["cmp_pe_k"]), (pe[1], k.dram["cmp_pe_v"]), (flat(cmp_bias), k.dram["cmp_bias"]),
             (table, k.dram["key_minus_query"])], "nsa_landed")
    norm = Norm(k, [norm_of(k, 0, SEQ, k.v("c_ln"))], 4096)
    product(k, "c_w_q", tokens, [(0, SEQ)], scalar=copy_out(k, lambda c, m, g: Q[:, 4 * c + m, :]), norm=norm)
    arrived(k, "nsa_landed", 10)

    lo, hi = slice(0, 64), slice(64, 128)

    def both_shifted(act, chunk, m, g, bank, before):
        dst = KC[m // 2]
        a, b = 2 * (m % 2), 2 * (m % 2) + 1
        act.activation(dst[lo, a, :], bank[lo, :], ACT.Copy)
        act.activation(dst[hi, a, 0:SEQ - 1], bank[lo, 1:SEQ], ACT.Copy)
        act.activation(dst[lo, b, :], bank[hi, :], ACT.Copy)
        act.activation(dst[hi, b, 0:SEQ - 1], bank[hi, 1:SEQ], ACT.Copy).then_inc(drained.sem, 1)

    def both_halves(act, chunk, m, g, bank, before):
        dst = (KS, KW)[m // 2]
        a, b = 2 * (m % 2), 2 * (m % 2) + 1
        act.activation(dst[lo, a, :], bank[lo, :], ACT.Copy)
        act.activation(dst[hi, a, :], bank[lo, :], ACT.Copy)
        act.activation(dst[lo, b, :], bank[hi, :], ACT.Copy)
        act.activation(dst[hi, b, :], bank[hi, :], ACT.Copy).then_inc(drained.sem, 1)

    product(k, "c_w_c", tokens, [(0, SEQ)], scalar=both_shifted)
    product(k, "c_w_k", tokens, [(0, SEQ)], scalar=both_halves)
    product(k, "c_w_v", tokens, [(i * P, P) for i in range(TT)], stationary="tokens",
            scalar=copy_out(k, lambda c, m, g: V[:, g, :]))

    made, acted = k.counter("cmp_made"), k.counter("cmp_acted")
    with nc.Block() as block:

        @block.sync
        def _(sp):
            k.prefetch(sp)

        @block.tensor
        def _(pe_):
            for t in range(TT):
                for kt in range(KT):
                    mm = nc.tensor.matmul(k.bank(0)[:, t * 48:t * 48 + 48], k.h[:, kt, t * P:(t + 1) * P], wgl[:, kt, :],
                                          start=(kt == 0), stop=(kt == KT - 1))
            mm.then_inc(made.sem, 1)
            for i in range(2):
                for l in range(16):
                    mm = nc.tensor.matmul(k.bank(1)[:, i:i + 1], w1[i][:, l, :], pe[i][:, l:l + 1], start=(l == 0), stop=(l == 15))
            mm.then_inc(made.sem, 1)
            for i in range(2):
                for l in range(16):
                    rhs = KC[i][:, :, 2 * l:2 * l + CMP_STRIDE * (N_CMP - 1) + 1:CMP_STRIDE]
                    mm = nc.tensor.matmul(k.bank(2 + i)[:, 0:4 * N_CMP], w1[i][:, l, :], rhs, start=(l == 0), stop=(l == 15))
                mm.then_inc(made.sem, 1)
            pe_.wait_ge(*acted.at(2))
            nc.tensor.matmul(k.bank(4, 4 * N_CMP), w2[0], hid[0], start=True, stop=True).then_inc(made.sem, 1)
            pe_.wait_ge(*acted.at(3))
            for g in range(4):
                mm = nc.tensor.matmul(k.bank(5)[0:N_CMP, g * 64:(g + 1) * 64], hid[1][:, g * N_CMP:(g + 1) * N_CMP], w2[1],
                                      start=True, stop=True)
            mm.then_inc(made.sem, 1)

        @block.scalar
        def _(act):
            act.wait_ge(*made.at(2))
            nc.scalar.activation(pebias[:, 0:2], k.bank(1, 2), ACT.Copy).then_inc(acted.sem, 1)
            act.wait_ge(*acted.at(1))
            for i in range(2):
                act.wait_ge(*made.at(3 + i))
                nc.scalar.activation(hid[i], k.bank(2 + i, 4 * N_CMP), ACT.Silu, bias=pebias[:, i:i + 1]).then_inc(acted.sem, 1)
            nc.scalar.activation(flat(gates), k.bank(0, TT * 48), ACT.Sigmoid)
            act.wait_ge(*made.at(5))
            nc.scalar.activation(flat(CK), k.bank(4, 4 * N_CMP), ACT.Copy)
            act.wait_ge(*made.at(6))
            nc.scalar.activation(flat(CV)[0:N_CMP, :], k.bank(5, 256)[0:N_CMP, :], ACT.Copy)

    made.base += 6
    acted.base += 3

    scale = NSA_DIM ** -0.5
    HN = NSA_HEADS * N_CMP
    s_ready, p_step, p_exp, t_ready, t_out = (k.counter(n) for n in ("cmp_scores", "cmp_step", "cmp_exp", "cmp_turned", "cmp_out"))
    by_head = lambda ap: ap.rearrange("p (h n) -> p h n", n=N_CMP)
    wide = lambda ap: ap.rearrange("p (h o) -> p h o", o=1).to_broadcast([P, NSA_HEADS, N_CMP])
    steps = [0]
    with nc.Block() as block:

        @block.tensor
        def _(pe_):
            def score(t):
                if t >= 2:
                    pe_.wait_ge(*p_step.at(8 * (t - 2) + 2))
                for h in range(NSA_HEADS):
                    rows, at = (lo, hi)[h % 2], (h // 2) * N_CMP
                    mm = nc.tensor.matmul(k.bank(2 * (t % 2) + h % 2)[:, at:at + N_CMP], Q[rows, h // 2, t * P:(t + 1) * P],
                                          CK[rows, h // NSA_REP, :], start=True, stop=True)
                mm.then_inc(s_ready.sem, 1)

            score(0)
            score(1)
            for t in range(TT):
                pe_.wait_ge(*p_step.at(8 * t + 8))
                if t:
                    pe_.wait_ge(*t_out.at(t))
                for h in range(NSA_HEADS):
                    mm = nc.tensor.transpose(k.bank(4 + h // 4)[0:N_CMP, (h % 4) * P:(h % 4 + 1) * P],
                                             pc[:, t % 2, h * N_CMP:(h + 1) * N_CMP], k.c("ident"))
                mm.then_inc(t_ready.sem, 1)
                if t + 2 < TT:
                    score(t + 2)

        @block.vector
        def _(dve):
            step = Chain(dve, p_step)
            for t in range(TT):
                p = pc[:, t % 2, :]
                dve.wait_ge(*s_ready.at(t + 1))
                if t >= 2:
                    dve.wait_ge(*t_ready.at(t - 1))
                for par in range(2):
                    step(nc.vector.scalar_tensor_tensor(out=by_head(p)[:, par::2, :], in0=by_head(k.bank(2 * (t % 2) + par, HN // 2)),
                                                        scalar=scale, in1=by_head(cmp_bias[:, t, :])[:, par::2, :],
                                                        op0=ALU.mult, op1=ALU.add))
                step(nc.vector.tensor_reduce(small[:, 0, :], by_head(p), AX_X, ALU.max))
                step(nc.vector.tensor_tensor(by_head(p), by_head(p), wide(small[:, 0, :]), ALU.subtract))
                dve.wait_ge(*p_exp.at(t + 1))
                step(nc.vector.tensor_reduce(small[:, 1, :], by_head(p), AX_X, ALU.add))
                step(nc.vector.reciprocal(small[:, 2, :], small[:, 1, :]))
                gate = gates[:, t, 0:48:3]
                some = k.c("cmp_rows") if t == 0 else 1.0
                step(nc.vector.scalar_tensor_tensor(out=small[:, 3, :], in0=small[:, 2, :], scalar=some, in1=gate, op0=ALU.mult, op1=ALU.mult))
                step(nc.vector.tensor_tensor(by_head(p), by_head(p), wide(small[:, 3, :]), ALU.mult))

        @block.scalar
        def _(act):
            for t in range(TT):
                p = pc[:, t % 2, :]
                act.wait_ge(*p_step.at(8 * t + 4))
                nc.scalar.activation(p, p, ACT.Exp).then_inc(p_exp.sem, 1)
                act.wait_ge(*t_ready.at(t + 1))
                for b in range(4):
                    src = k.bank(4 + b)[0:N_CMP, :].rearrange("p (h q) -> p h q", h=4)
                    op = nc.scalar.activation(pcT[0:N_CMP, 4 * b:4 * b + 4, t * P:(t + 1) * P], src, ACT.Copy)
                op.then_inc(t_out.sem, 1)

    s_ready.base += TT
    p_step.base += 8 * TT
    p_exp.base += TT
    t_ready.base += TT
    t_out.base += TT

    slopes = [2.0 ** (-8.0 * (h + 1) / NSA_HEADS) for h in range(NSA_HEADS)]
    which = [(h, t, b) for h in range(NSA_HEADS) for t in range(TT) for b in range(2)]
    units = [{"keys": (t + 1) * P, "opens": t == 0 and b == 0, "closes": t == TT - 1 and b == 1} for h, t, b in which]

    def scores(u):
        h, t, b = which[u]
        rows = (lo, hi)[h % 2]
        return [(slice(0, (t + 1) * P), Q[rows, h // 2, t * P:(t + 1) * P], (KS, KW)[b][rows, h // NSA_REP, 0:(t + 1) * P], True, True)]

    def values(u, weights):
        h, t, b = which[u]
        rows, cols, g = (lo, hi)[h % 2], slice(t * P, (t + 1) * P), h // NSA_REP
        out = [(rows, cols, V[:, kb, b * 256 + g * 64:b * 256 + g * 64 + 64], weights[:, kb * P:(kb + 1) * P], b == 0 and kb == 0, False)
               for kb in range(t + 1)]
        if b == 1:
            out.append((rows, cols, CV[0:N_CMP, g, :], pcT[0:N_CMP, h, cols], False, True))
        return out

    def finish(u):
        h = which[u][0]
        rows = (lo, hi)[h % 2]
        return k.h[rows, h // 2, 0:SEQ], rows, slice(0, SEQ)

    attention(k, units, scores, lambda u: [(kb * P, P) for kb in range(which[u][1] + 1)], values, finish, scale, 26640, 512,
              gates=lambda u: gates[:, which[u][1], 3 * which[u][0] + 1 + which[u][2]:3 * which[u][0] + 2 + which[u][2]],
              bias=lambda u: (table[:, 384 - P * which[u][1]:512], slopes[which[u][0]] / scale))
    output_product(k)




def modulation(k, l):
    nc = k.nc
    k.arena_scope.close()
    with ExitStack() as own:
        sb = lambda name, width, kind: own.enter_context(nc.sbuf_tensor(f"modulation_{name}_{l}", [P, width], kind))
        raw, rounded, rest = sb("weights", 3 * SLOT, F32), sb("rounded", 2 * SLOT, F32R), sb("rest", 2 * SLOT, F32R)
        parts, small = sb("condition_parts", KT * 4, F32R), sb("small", 32 + 2 * BANK, F32)
        mod = modulate(k, l, raw[:, :].rearrange("p (s n) -> p s n", s=3), rounded[:, :].rearrange("p (s n) -> p s n", s=2),
                       rest[:, :].rearrange("p (s n) -> p s n", s=2), parts[:, :].rearrange("p (k n) -> p k n", k=KT), small)
    k.open_arena()
    return mod


def modulate(k, l, raw, rounded, rest, parts, small):
    nc = k.nc
    cond = small[:, 0:16].rearrange("p (k n) -> p k n", k=KT)
    add_parts = small[:, 16:18]
    rows = small[:, 32:32 + 2 * BANK].rearrange("p (s n) -> p s n", s=2)
    mod = k.mods[:, 0:96].rearrange("p (c n) -> p c n", c=2)
    gains = k.mods[:, 96:128].rearrange("p (c j n) -> p c j n", c=2, j=2)
    slots, body, chunks = 3, 6, 12
    w = k.dram[f"w_mod_{l}"]
    landed = [k.counter(f"modulation_landed_{s}") for s in range(slots)]
    cond_step, used, chunk_rounded, split, copied, turned = (k.counter(n) for n in (
        "condition_step", "modulation_used", "modulation_rounded", "modulation_split", "modulation_copied", "modulation_turned"))
    with nc.Block() as block:

        @block.sync
        def _(sp):
            k.prefetch(sp)
            for c in range(slots):
                sp.dma_start(raw[:, c, :], w[c]).then_inc(landed[c].sem, 16)

        @block.scalar
        def _(act):
            nc.scalar.activation(flat(cond), k.v("cond"), ACT.Silu).then_inc(cond_step.sem, 1)
            act.wait_ge(*cond_step.at(1))
            nc.scalar.activation(parts[:, :, 0:2], cond, ACT.Copy).then_inc(used.sem, 2)

        @block.vector
        def _(dve):
            dve.wait_ge(*used.at(2))
            nc.vector.tensor_tensor(parts[:, :, 2:4], cond, parts[:, :, 0:2].bitcast(F32), ALU.subtract)
            nc.vector.tensor_tensor(add_parts[0:4, :], k.c("ident")[0:4, 0:2], k.c("ident")[0:4, 2:4],
                                    ALU.add).then_inc(turned.sem, 2)

    cond_step.base += 1
    used.base += 2
    turned.base += 2
    with nc.Block() as block:

        @block.sync
        def _(sp):
            for c in range(slots, chunks):
                sp.wait_ge(*split.at(c - slots + 1))
                sp.dma_start(raw[:, c % slots, :], w[c]).then_inc(landed[c % slots].sem, 16)

        @block.scalar
        def _(act):
            def round_chunk(i, s):
                act.wait_ge(*landed[s % slots].at(i * (16 * body // slots) + 16 * (s // slots + 1)))
                act.wait_ge(*used.at(i * body + (s - 1)))
                nc.scalar.activation(rounded[:, s % 2, :], raw[:, s % slots, :], ACT.Copy).then_inc(chunk_rounded.sem, 1)

            def copy_rows(i, s):
                act.wait_ge(*used.at(i * body + s + 1))
                act.wait_ge(*turned.at(i * body + (s - 1)))
                nc.scalar.activation(rows[0:4, s % 2, :], k.bank(1 + s % 2, parts=slice(0, 4)), ACT.Copy).then_inc(copied.sem, 1)

            with act.Fori(0, chunks // body) as i:
                round_chunk(i, 0)
                for s in range(1, body):
                    round_chunk(i, s)
                    copy_rows(i, s - 1)
                copy_rows(i, body - 1)

        @block.vector
        def _(dve):
            with dve.Fori(0, chunks // body) as i:
                for s in range(body):
                    dve.wait_ge(*chunk_rounded.at(i * body + s + 1))
                    nc.vector.tensor_tensor(rest[:, s % 2, :], raw[:, s % slots, :], rounded[:, s % 2, :].bitcast(F32),
                                            ALU.subtract).then_inc(split.sem, 1)
            dve.wait_ge(*turned.at(chunks))
            sums = k.bank(0, 96).rearrange("p (n c) -> p c n", c=2)
            for c in range(2):
                nc.vector.tensor_tensor(mod[:, c, :], sums[:, c, :], k.v("b_mod", 48 * l, 48), ALU.add)

        @block.tensor
        def _(pe):
            def multiply(i, s):
                pe.wait_ge(*split.at(i * body + s + 1))
                for part, source in enumerate((rounded[:, s % 2, :], rest[:, s % 2, :])):
                    chunk = source.rearrange("p (k n) -> p k n", k=KT)
                    for t in range(KT):
                        mm = nc.tensor.matmul(k.bank(1 + s % 2, parts=slice(0, 4)), parts[:, t, :], chunk[:, t, :],
                                              start=(part == 0 and t == 0), stop=(part == 1 and t == KT - 1))
                mm.then_inc(used.sem, 1)

            def turn(i, s):
                pe.wait_ge(*copied.at(i * body + s + 1))
                for m in range(4):
                    mm = nc.tensor.matmul(k.psum[:, bass.ds(i * (8 * body) + 8 * s + 2 * m, 2)], rows[0:4, s % 2, m * P:(m + 1) * P],
                                          add_parts[0:4, :], start=True, stop=True)
                mm.then_inc(turned.sem, 1)

            with pe.Fori(0, chunks // body) as i:
                multiply(i, 0)
                for s in range(1, body):
                    multiply(i, s)
                    turn(i, s - 1)
                turn(i, body - 1)

    for s in range(slots):
        landed[s].base += 16 * (chunks // slots)
    for counter in (used, chunk_rounded, split, copied, turned):
        counter.base += chunks
    with nc.Block() as block:

        @block.sync
        def _(sp):
            k.prefetch(sp)

        @block.vector
        def _(dve):
            for c in range(2):
                for j, norm in enumerate(("norm1", "norm2")):
                    sc = mod[:, c, 24 * j + 8:24 * j + 16]
                    nc.vector.scalar_tensor_tensor(out=gains[:, c, j, :], in0=sc, scalar=1.0, in1=k.v(norm, 8 * l, 8),
                                                   op0=ALU.add, op1=ALU.mult)

    parts = lambda c, i: mod[:, c, 8 * i:8 * i + 8]
    return {"gain": [[gains[:, c, j, :] for j in range(2)] for c in range(2)],
            "shift": [[parts(c, 0), parts(c, 3)] for c in range(2)], "gate": [[parts(c, 2), parts(c, 5)] for c in range(2)]}


def modulated_norm(k, mod, j, groups, scratch=20000):
    return Norm(k, [norm_of(k, s, n, mod["gain"][c][j], mod["shift"][c][j]) for c, (s, n) in enumerate(groups)], scratch)


def conv_ffn(k, l, mod, groups):
    k.change_arena(SMALL_ARENA)
    parts_scope, parts = k.place_parts()
    norm = modulated_norm(k, mod, 1, groups, 6144)
    hidden = k.region(0, FC, TOK)
    G = len(groups)
    drained, step, convolved, gated = (k.counter(n) for n in ("bank_drained", "ffn_conv_step", "ffn_convolved", "ffn_gated"))
    w_at, b_at = VECTORS["ffn_conv_w"][0] + 3 * FC * l, VECTORS["ffn_conv_b"][0] + FC * l

    def hidden_tile(chunk, m, g):
        s, n = groups[g]
        return hidden[:, bass.ds(chunk * 2 + m, 1), s:s + n].rearrange("p a t -> p (a t)")

    def take(dve, chunk, m, g, bank, before):
        n = groups[g][1]
        out = hidden_tile(chunk, m % 2, g)
        if m < 2:
            tap = lambda i: k.vec[:, bass.ds(w_at + i * FC + chunk * 2 + m, 1)]
            nth = ((chunk * 2 + m) * G + g) * 2
            dve.tensor_scalar(out, bank[:, 0:n], tap(1), k.vec[:, bass.ds(b_at + chunk * 2 + m, 1)], ALU.mult, ALU.add).then_inc(step.sem, 1)
            dve.wait_ge(*step.at(nth + 1))
            o = hidden[:, bass.ds(chunk * 2 + m, 1), groups[g][0] + 1:groups[g][0] + n].rearrange("p a t -> p (a t)")
            dve.scalar_tensor_tensor(out=o, in0=bank[:, 0:n - 1], scalar=tap(0), in1=o, op0=ALU.mult, op1=ALU.add).then_inc(step.sem, 1)
            dve.wait_ge(*step.at(nth + 2))
            o = hidden[:, bass.ds(chunk * 2 + m, 1), groups[g][0]:groups[g][0] + n - 1].rearrange("p a t -> p (a t)")
            dve.scalar_tensor_tensor(out=o, in0=bank[:, 1:n], scalar=tap(2), in1=o, op0=ALU.mult, op1=ALU.add).then_inc(drained.sem, 1)
        else:
            dve.wait_ge(*gated.at((chunk * 2 + m - 2) * G + g + 1))
            dve.tensor_tensor(out, out, bank[:, 0:n], ALU.mult).then_inc(drained.sem, 1)

    def silu(act, chunk, m, g, bank, before):
        if m < 2:
            act.wait_ge(*drained.at(before + 1))
            out = hidden_tile(chunk, m, g)
            act.activation(out, out, ACT.Silu).then_inc(gated.sem, 1)

    product(k, "ffn_up", lambda t, s, n: k.h[:, t, s:s + n], groups, vector=take, scalar=silu, norm=norm, parts=parts)
    parts_scope.close()
    step.base += 2 * FC * G
    gated.base += FC * G
    for c, (start, n) in enumerate(groups):
        product_by_rows(k, hidden[:, :, start:start + n], mod["gate"][c][1], start, n)
    k.change_arena()


def fourier(k, UF, n, start, tables):
    nc = k.nc
    nt = n // P
    PQ = k.region(12288, 4, nt, 256)
    group, table = tables
    rotated = table[:, :, :].rearrange("p i (t n) -> p i t n", t=nt)
    made, copied = k.counter("fourier_made"), k.counter("fourier_copied")
    U = 4 * nt
    with nc.Block() as block:

        @block.sync
        def _(sp):
            k.prefetch(sp)

        @block.tensor
        def _(pe):
            for u in range(U):
                g, t = u // nt, u % nt
                if u >= 4:
                    pe.wait_ge(*copied.at(u - 3))
                nc.tensor.matmul(k.bank(u % 4, 256), UF[:, g, start + t * P:start + (t + 1) * P], group, start=True,
                                 stop=True).then_inc(made.sem, 1)
            for g in range(4):
                pe.wait_ge(*copied.at((g + 1) * nt))
                for t in range(nt):
                    for i in range(2):
                        mm = nc.tensor.matmul(k.bank(4 + g, n), PQ[:, g, t, i * P:(i + 1) * P], rotated[:, i, t, :],
                                              start=(t == 0 and i == 0), stop=(t == nt - 1 and i == 1))
                mm.then_inc(made.sem, 1)

        @block.scalar
        def _(act):
            for u in range(U):
                act.wait_ge(*made.at(u + 1))
                nc.scalar.activation(PQ[:, u // nt, u % nt, :], k.bank(u % 4, 256), ACT.Copy).then_inc(copied.sem, 1)

        @block.vector
        def _(dve):
            for g in range(4):
                dve.wait_ge(*made.at(U + g + 1))
                nc.vector.tensor_copy(k.h[:, g, start:start + n], k.bank(4 + g, n))

    made.base += U + 4
    copied.base += U


def hyena(k, X0, W, n, start, name):
    nc = k.nc
    nt = n // P
    decay, WT = k.region(0, nt, 512), k.region(12288, nt, 512)
    total, diff = k.region(14336, nt, 512), k.region(16384, nt, 512)
    tables = k.region(18432, 4, nt * n)
    w1, w23, w4 = k.region(26624, 64), k.region(26688, 128), k.region(26816, 1024)
    pos = k.region(27840, n)
    hcur = k.region(28352, 2, 512)
    arg = k.region(29376, 512)
    norm = k.region(29888, 8)
    work = k.region(27840, 4, 512)
    Yre, Yim = k.region(0, nt, 512), k.region(6144, nt, 512)
    tab = tables[:, :, :].rearrange("p i (t n) -> p i t n", t=nt)
    load(k, [(w1[0:HY_EMB, :], k.dram["hy_w1"]), (w23[0:64, :], k.dram["hy_w23"]), (w4[0:64, :], k.dram["hy_w4"]),
             (pos[0:HY_EMB, :], k.dram["hy_pos_" + name]), (flat(decay), k.dram["hy_decay_" + name])]
         + [(tables[:, i, :], k.dram["odd_dft_" + name][i]) for i in range(4)])

    made, v_step, sine = k.counter("filter_made"), k.counter("filter_step"), k.counter("filter_sine")
    F64 = slice(0, HY_WIDTH)
    with nc.Block() as block:

        @block.sync
        def _(sp):
            k.prefetch(sp)

        @block.tensor
        def _(pe):
            for layer in range(3):
                if layer == 0:
                    lhs, rhs = w1[0:HY_EMB, :], pos[0:HY_EMB, :]
                else:
                    pe.wait_ge(*sine.at(layer))
                    lhs, rhs = w23[F64, (layer - 1) * 64:layer * 64], hcur[F64, (layer - 1) % 2, 0:n]
                nc.tensor.matmul(k.bank(layer, n, F64), lhs, rhs, start=True, stop=True).then_inc(made.sem, 1)

        @block.vector
        def _(dve):
            step = Chain(dve, v_step)
            for layer in range(3):
                dve.wait_ge(*made.at(layer + 1))
                a, r = arg[F64, 0:n], hcur[F64, layer % 2, 0:n]
                step(nc.vector.tensor_scalar(a, k.bank(layer, n, F64), k.v("hy_b", layer, 1)[F64], k.v("hy_freq")[F64], ALU.add, ALU.mult))
                step(nc.vector.tensor_scalar(r, a, 1.0 / (2 * math.pi), ROUND, ALU.mult, ALU.add))
                step(nc.vector.tensor_scalar(r, r, ROUND, None, ALU.subtract))
                step(nc.vector.scalar_tensor_tensor(out=a, in0=r, scalar=-TWO_PI_HI, in1=a, op0=ALU.mult, op1=ALU.add))
                step(nc.vector.scalar_tensor_tensor(out=a, in0=r, scalar=-TWO_PI_LO, in1=a, op0=ALU.mult, op1=ALU.add))
                step(nc.vector.tensor_scalar(r, a, 3.141592, -3.141592, ALU.min, ALU.max))
                if layer < 2:
                    dve.wait_ge(*sine.at(layer + 1))

        @block.scalar
        def _(act):
            for layer in range(3):
                act.wait_ge(*v_step.at(6 * layer + 6))
                h = hcur[F64, layer % 2, 0:n]
                nc.scalar.activation(h, h, ACT.Sin).then_inc(sine.sem, 1)

    made.base += 3
    v_step.base += 18
    sine.base += 3

    last = hcur[F64, 0, :]
    p, v, a = k.counter("hyena_pe"), k.counter("hyena_dve"), k.counter("hyena_act")
    sides = k.region(28864, 2, 512)
    with nc.Block() as block:

        @block.sync
        def _(sp):
            k.prefetch(sp)

        @block.tensor
        def _(pe):
            for t in range(nt):
                if t:
                    pe.wait_ge(*v.at(4 * t - 2))
                for side in range(2):
                    mm = nc.tensor.matmul(k.bank(side), last[:, t * P:(t + 1) * P], w4[F64, side * 512:(side + 1) * 512],
                                          start=True, stop=True)
                mm.then_inc(p.sem, 1)
                if t >= 2:
                    pe.wait_ge(*k.counter("hyena_turned").at(t - 1))
                for c in range(4):
                    mm = nc.tensor.transpose(k.bank(2 + t % 2)[:, c * P:(c + 1) * P], W[:, c, start + t * P:start + (t + 1) * P], k.c("ident"))
                mm.then_inc(k.counter("hyena_transposed").sem, 1)
                pe.wait_ge(*a.at(t + 1))
                for c in range(4):
                    for side in range(2):
                        mm = nc.tensor.matmul(k.bank(4 + c, 1), sides[:, side, c * P:(c + 1) * P], k.c("ones", 0, 1),
                                              start=(t == 0 and side == 0), stop=(t == nt - 1 and side == 1))
                mm.then_inc(k.counter("hyena_summed").sem, 1)

        @block.vector
        def _(dve):
            for t in range(nt):
                dve.wait_ge(*p.at(t + 1))
                if t:
                    dve.wait_ge(*k.counter("hyena_summed").at(t))
                first = k.c("not_first") if t == 0 else 1.0
                nc.vector.tensor_tensor(sides[:, 0, :], k.bank(0), decay[:, t, :], ALU.mult).then_inc(v.sem, 1)
                nc.vector.scalar_tensor_tensor(out=sides[:, 1, :], in0=k.bank(1), scalar=first, in1=decay[:, t, :],
                                               op0=ALU.mult, op1=ALU.mult).then_inc(v.sem, 1)
                dve.wait_ge(*v.at(4 * t + 2))
                nc.vector.tensor_tensor(total[:, t, :], sides[:, 0, :], sides[:, 1, :], ALU.add).then_inc(v.sem, 1)
                nc.vector.tensor_tensor(diff[:, t, :], sides[:, 0, :], sides[:, 1, :], ALU.subtract).then_inc(v.sem, 1)
            dve.wait_ge(*k.counter("hyena_summed").at(nt))
            sums = k.psum[:, 4 * BANK:8 * BANK].rearrange("p (b n) -> p b n", b=4)[:, :, 0:1].rearrange("p b n -> p (b n)")
            nc.vector.reciprocal(norm[:, 0:4], sums)

        @block.scalar
        def _(act):
            for t in range(nt):
                act.wait_ge(*k.counter("hyena_transposed").at(t + 1))
                nc.scalar.activation(WT[:, t, :], k.bank(2 + t % 2), ACT.Copy).then_inc(k.counter("hyena_turned").sem, 1)
                act.wait_ge(*v.at(4 * t + 4))
                nc.scalar.activation(flat(sides), flat(sides), ACT.Abs).then_inc(a.sem, 1)

    p.base += nt
    v.base += 4 * nt
    a.base += nt
    for s in ("hyena_turned", "hyena_transposed", "hyena_summed"):
        k.counter(s).base += nt

    spectra, copied, multiplied = k.counter("spectra_made"), k.counter("spectra_copied"), k.counter("spectra_multiplied")
    back = k.counter("hyena_back")
    with nc.Block() as block:

        @block.sync
        def _(sp):
            k.prefetch(sp)

        @block.tensor
        def _(pe):
            for f in range(nt):
                if f:
                    pe.wait_ge(*multiplied.at(6 * f))
                for bank, table, src in ((0, 0, WT), (1, 1, WT), (2, 0, total), (3, 1, diff)):
                    for t in range(nt):
                        mm = nc.tensor.matmul(k.bank(bank), tab[:, table, t, f * P:(f + 1) * P], src[:, t, :], start=(t == 0), stop=(t == nt - 1))
                mm.then_inc(spectra.sem, 1)
            pe.wait_ge(*multiplied.at(6 * nt))
            for c in range(4):
                for f in range(nt):
                    for i, Y in enumerate((Yre, Yim)):
                        mm = nc.tensor.matmul(k.bank(4 + c, n), Y[:, f, c * P:(c + 1) * P], tab[:, 2 + i, f, :],
                                              start=(f == 0 and i == 0), stop=(f == nt - 1 and i == 1))
                mm.then_inc(back.sem, 1)

        @block.scalar
        def _(act):
            for f in range(nt):
                act.wait_ge(*spectra.at(f + 1))
                if f:
                    act.wait_ge(*multiplied.at(6 * f))
                nc.scalar.activation(work[:, 0, :], k.bank(2), ACT.Copy)
                nc.scalar.activation(work[:, 1, :], k.bank(3), ACT.Copy).then_inc(copied.sem, 1)

        @block.vector
        def _(dve):
            step = Chain(dve, multiplied)
            for f in range(nt):
                dve.wait_ge(*copied.at(f + 1))
                hre, him = work[:, 0, :], work[:, 1, :]
                step(nc.vector.tensor_tensor(Yre[:, f, :], k.bank(0), hre, ALU.mult))
                step(nc.vector.tensor_tensor(work[:, 2, :], k.bank(1), him, ALU.mult))
                step(nc.vector.tensor_tensor(Yre[:, f, :], Yre[:, f, :], work[:, 2, :], ALU.subtract))
                step(nc.vector.tensor_tensor(Yim[:, f, :], k.bank(0), him, ALU.mult))
                step(nc.vector.tensor_tensor(work[:, 2, :], k.bank(1), hre, ALU.mult))
                step(nc.vector.tensor_tensor(Yim[:, f, :], Yim[:, f, :], work[:, 2, :], ALU.add))
            for c in range(4):
                y, w = work[:, 3, 0:n], W[:, c, start:start + n]
                step(nc.vector.tensor_scalar(y, w, k.v("hy_bias", c, 1), None, ALU.mult))
                dve.wait_ge(*back.at(c + 1))
                step(nc.vector.scalar_tensor_tensor(out=y, in0=k.bank(4 + c, n), scalar=norm[:, c:c + 1], in1=y, op0=ALU.mult, op1=ALU.add))
                step(nc.vector.tensor_tensor(k.h[:, 4 + c, start:start + n], y, X0[:, c, start:start + n], ALU.mult))

    spectra.base += nt
    copied.base += nt
    multiplied.base += 6 * nt + 12
    back.base += 4


def fourier_hyena_layer(k, mod, groups):
    nc = k.nc
    UF, HY = k.region(0, 4, TOK), k.region(3072, 12, TOK)
    norm = modulated_norm(k, mod, 0, groups, 17408)
    group_table = k.region(26624, 256)
    seq_tables = [k.region(26880, 2, 2048), k.region(16384, 2, 512)]
    k.load_later([(group_table, k.dram["group_dft"])] + [(table[:, i, :], k.dram["seq_dft_" + name][i])
                                                        for table, name in zip(seq_tables, "xc") for i in range(2)], "fourier_landed")
    drained, step = k.counter("bank_drained"), k.counter("hy_conv_step")
    count = [0]

    def take(dve, chunk, m, g, bank, before):
        tile = chunk * 4 + m
        s, n = groups[g]
        if tile < 4:
            dve.tensor_copy(UF[:, tile, s:s + n], bank[:, 0:n]).then_inc(drained.sem, 1)
            return
        j = tile - 4

        def chained(ins):
            count[0] += 1
            ins.then_inc(step.sem, 1)
            dve.wait_ge(*step.at(count[0]))

        taps = [k.v("hy_conv_w", i * 12 + j, 1) for i in (1, 0, 2)]
        conv_taps(dve, chained, HY[:, j, s:s + n], bank, taps, k.v("hy_conv_b", j, 1), [0, -1, 1], n)
        dve.sem_inc(drained.sem, 1)

    product(k, "fh_w_in", lambda t, s, n: k.h[:, t, s:s + n], groups, vector=take, loop=False, norm=norm)
    step.base += count[0]
    X0, X1, W = HY[:, 0:4, :], HY[:, 4:8, :], HY[:, 8:12, :]
    with nc.Block() as block:

        @block.gpsimd
        def _(pool):
            for c in range(4):
                nc.gpsimd.tensor_tensor(W[:, c, :], W[:, c, :], X1[:, c, :], ALU.mult)

    arrived(k, "fourier_landed", 5)
    for (s, n), table in zip(groups, seq_tables):
        fourier(k, UF, n, s, (group_table, table))
    for (s, n), name in zip(groups, "xc"):
        hyena(k, X0, W, n, s, name)
    product(k, "fh_w_out", lambda t, s, n: k.h[:, t, s:s + n], groups,
            vector=add_to_residual(k, 4, groups, [mod["gate"][c][0] for c in range(2)]))


def mla_layer(k, mod, groups):
    nc = k.nc
    K, Q, V = k.region(0, MLA_HEADS, TOK), k.region(12288, MLA_HEADS, SEQ), k.region(20480, TOK // P, D)
    A = k.region(26624, 4, TOK)
    aq = k.h_all[:, 0:1024].rearrange("p (k t) -> p k t", k=2)
    akv = k.h_all[:, 1024:1792]
    wukv, rope = k.h_all[:, 2048:4096], k.h_all[:, 4096:5120]
    pe_rows = slice(MLA_NOPE, MLA_QK)
    norm = modulated_norm(k, mod, 0, groups)
    drained = k.counter("bank_drained")

    def latent(act, chunk, m, g, bank, before):
        s, n = groups[g]
        if m < 3:
            act.activation(A[:, m, s:s + n], bank[:, 0:n], ACT.Copy).then_inc(drained.sem, 1)
        else:
            act.activation(A[pe_rows, 3, s:s + n], bank[0:MLA_ROPE, 0:n], ACT.Copy).then_inc(drained.sem, 1)

    product(k, "mla_w_in", lambda t, s, n: k.h[:, t, s:s + n], groups, scalar=latent, norm=norm)
    load(k, [(wukv, k.dram["mla_w_ukv"][0]), (rope, k.dram["rope"])])
    Norm(k, [(2, SEQ, lambda t: A[:, t, 0:SEQ], lambda t: aq[:, t, :], k.v("q_a_norm"), None, 2 * P, 0)]
         + [(1, n, lambda t, s=s, n=n: A[:, 2, s:s + n], lambda t, s=s, n=n: akv[:, s:s + n], k.v("kv_a_norm"), None, P, s)
            for s, n in groups], 12288).alone()
    product(k, "mla_w_uq", lambda t, s, n: aq[:, t, s:s + n], [(0, SEQ)], tile=MLA_QK,
            scalar=copy_heads(k, Q))

    made, used = k.counter("kv_made"), k.counter("kv_copied")
    jobs = [(h, s, n) for h in range(MLA_HEADS) for s, n in groups]
    with nc.Block() as block:

        @block.sync
        def _(sp):
            k.prefetch(sp)

        @block.tensor
        def _(pe):
            for i, (h, s, n) in enumerate(jobs):
                if i >= 4:
                    pe.wait_ge(*used.at(i - 3))
                nc.tensor.matmul(k.bank(i % 4, n, slice(0, 64)), wukv[:, h * 64:(h + 1) * 64], akv[:, s:s + n],
                                 start=True, stop=True).then_inc(made.sem, 1)
            for i in range(12):
                if i >= 4:
                    pe.wait_ge(*k.counter("values_copied").at(i - 3))
                nc.tensor.matmul(k.bank(4 + i % 4), akv[:, (i // 2) * P:(i // 2 + 1) * P],
                                 wukv[:, 1024 + (i % 2) * 512:1536 + (i % 2) * 512], start=True, stop=True).then_inc(made.sem, 1)

        @block.scalar
        def _(act):
            for i, (h, s, n) in enumerate(jobs):
                act.wait_ge(*made.at(i + 1))
                nc.scalar.activation(K[0:64, h, s:s + n], k.bank(i % 4, n, slice(0, 64)), ACT.Copy).then_inc(used.sem, 1)

        @block.vector
        def _(dve):
            for i in range(12):
                dve.wait_ge(*made.at(len(jobs) + i + 1))
                nc.vector.tensor_copy(V[:, i // 2, (i % 2) * 512:(i % 2 + 1) * 512], k.bank(4 + i % 4)).then_inc(
                    k.counter("values_copied").sem, 1)

        @block.gpsimd
        def _(pool):
            for h in range(MLA_HEADS):
                nc.gpsimd.tensor_copy(K[pe_rows, h, :], A[pe_rows, 3, :])

    made.base += len(jobs) + 12
    used.base += len(jobs)
    k.counter("values_copied").base += 12

    squares = k.region(26624, 2, TOK)
    rows = k.h_all[:, 0:3072].rearrange("p (i t) -> p i t", i=4)
    qn = slice(0, MLA_QK)
    inverse = inverse_rows(k, lambda j: K[qn, j, :], MLA_HEADS, squares, rows, [n for _, n in groups], src_rows=MLA_QK, scale=1.0 / MLA_QK)
    turn_rotary(k, A[:, 3, :], rope, k.v("k_norm"))
    spread_rows(k, inverse, [(h, MLA_HEADS, MLA_QK, s, n,
                              [((K[0:64, h, s:s + n], 0), K[0:64, h, s:s + n], k.v("k_norm")[0:64]),
                               ((K[pe_rows, h, s:s + n], 64), A[pe_rows, 3, s:s + n], 1.0)]) for h, s, n in jobs])
    inverse = inverse_rows(k, lambda j: Q[qn, j, :], MLA_HEADS, squares, rows, [SEQ], src_rows=MLA_QK, scale=1.0 / MLA_QK)
    spread_rows(k, inverse, [(h, MLA_HEADS, MLA_QK, 0, SEQ, [((Q[qn, h, :], 0), Q[qn, h, :], k.v("q_norm")[qn])])
                             for h in range(MLA_HEADS)])
    turn_queries(k, Q, rope)

    heads = [(h, t) for h in range(MLA_HEADS) for t in range(TT)]
    units = [{"keys": TOK, "opens": t == 0, "closes": t == TT - 1} for h, t in heads]

    def scores(u):
        h, t = heads[u]
        return [(slice(s, s + n), Q[qn, h, t * P:(t + 1) * P], K[qn, h, s:s + n], True, True) for s, n in groups]

    def values(u, weights):
        h, t = heads[u]
        rows_ = slice(64 * (h % 2), 64 * (h % 2) + 64)
        return [(rows_, slice(t * P, (t + 1) * P), V[:, kb, h * 64:(h + 1) * 64], weights[:, kb * P:(kb + 1) * P], kb == 0, kb == 5)
                for kb in range(6)]

    def finish(u):
        h = heads[u][0]
        rows_ = slice(64 * (h % 2), 64 * (h % 2) + 64)
        return k.h[rows_, h // 2, 0:SEQ], rows_, slice(0, SEQ)

    attention(k, units, scores, lambda u: [(kb * P, P) for kb in range(6)], values, finish, float(MLA_QK) ** -0.5, 26624, TOK)
    output_product(k, mod["gate"][0][0])


def copy_heads(k, Q):
    drained = k.counter("bank_drained")

    def take(act, chunk, m, g, bank, before):
        act.activation(Q[0:MLA_QK, m, :], bank[0:MLA_QK, 0:SEQ], ACT.Copy).then_inc(drained.sem, 1)

    return take


def turn_rotary(k, kpe, rope, gain):
    nc = k.nc
    rows = slice(MLA_NOPE, MLA_QK)
    tmp = k.h_all[:, 5120:5632]
    step, made = k.counter("rotary_step"), k.counter("rotary_made")
    with nc.Block() as block:

        @block.tensor
        def _(pe):
            pe.wait_ge(*step.at(1))
            nc.tensor.matmul(k.bank(0, SEQ, rows), k.c("rope_swap")[rows, :], kpe[rows, 0:SEQ], start=True, stop=True).then_inc(made.sem, 1)

        @block.vector
        def _(dve):
            chain = Chain(dve, step)
            chain(nc.vector.tensor_scalar(kpe[rows, :], kpe[rows, :], gain[rows], None, ALU.mult))
            dve.wait_ge(*made.at(1))
            chain(nc.vector.tensor_tensor(tmp[rows, :], k.bank(0, SEQ, rows), rope[rows, SEQ:2 * SEQ], ALU.mult))
            chain(nc.vector.tensor_tensor(kpe[rows, 0:SEQ], kpe[rows, 0:SEQ], rope[rows, 0:SEQ], ALU.mult))
            chain(nc.vector.tensor_tensor(kpe[rows, 0:SEQ], kpe[rows, 0:SEQ], tmp[rows, :], ALU.add))

    step.base += 4
    made.base += 1


def turn_queries(k, Q, rope):
    nc = k.nc
    rows = slice(MLA_NOPE, MLA_QK)
    tmp = k.h_all[:, 5120:6144].rearrange("p (b t) -> p b t", b=2)
    step, made, turned = k.counter("turn_step"), k.counter("turn_made"), k.counter("turn_cosine")
    with nc.Block() as block:

        @block.sync
        def _(sp):
            k.prefetch(sp)

        @block.tensor
        def _(pe):
            for h in range(MLA_HEADS):
                if h >= 4:
                    pe.wait_ge(*step.at(2 * (h - 4) + 1))
                nc.tensor.matmul(k.bank(h % 4, SEQ, rows), k.c("rope_swap")[rows, :], Q[rows, h, :], start=True, stop=True).then_inc(made.sem, 1)

        @block.gpsimd
        def _(pool):
            for h in range(MLA_HEADS):
                pool.wait_ge(*made.at(h + 1))
                nc.gpsimd.tensor_tensor(Q[rows, h, :], Q[rows, h, :], rope[rows, 0:SEQ], ALU.mult).then_inc(turned.sem, 1)

        @block.vector
        def _(dve):
            chain = Chain(dve, step)
            for h in range(MLA_HEADS):
                dve.wait_ge(*made.at(h + 1))
                chain(nc.vector.tensor_tensor(tmp[rows, h % 2, :], k.bank(h % 4, SEQ, rows), rope[rows, SEQ:2 * SEQ], ALU.mult))
                dve.wait_ge(*turned.at(h + 1))
                chain(nc.vector.tensor_tensor(Q[rows, h, :], Q[rows, h, :], tmp[rows, h % 2, :], ALU.add))

    step.base += 2 * MLA_HEADS
    made.base += MLA_HEADS
    turned.base += MLA_HEADS



PLAN = [("a_w_in", KT, 512, 4), ("a_w_gate", KT, 512, 1), ("a_w_out", ROWS_OF_CHUNK, D, 2)]
XA = lambda l: [(f"xa_w{n}_{l}", KT, 512, 2) for n in "qkv"] + [(f"xa_wo_{l}", ROWS_OF_CHUNK, D, 2)]
FF = lambda l: [(f"ff_w1_{l}", KT, 512, 8), (f"ff_w2_{l}", ROWS_OF_CHUNK, D, FF_TILES // ROWS_OF_CHUNK)]
FFN = lambda l: [(f"ffn_up_{l}", KT, 512, FC // 2)] + [(f"ffn_down_{l}", 2, D, FC // 2)] * (2 - l)
PLAN += XA(0) + FF(0)
PLAN += [("c_w_q", KT, 512, 2), ("c_w_c", KT, 512, 1), ("c_w_k", KT, 512, 1), ("c_w_v", KT, 512, 1), ("c_w_out", ROWS_OF_CHUNK, D, 2)]
PLAN += XA(1) + FF(1)
PLAN += [("fh_w_in", KT, 512, 4), ("fh_w_out", KT, 512, 2)] + FFN(0)
PLAN += [("mla_w_in", KT, 416, 1), ("mla_w_uq", 2, 1536, 1), ("mla_w_o", ROWS_OF_CHUNK, D, 2)] + FFN(1)


def final_norm(k):
    Norm(k, [(KT, SEQ, lambda t: k.x[:, t, 0:SEQ], lambda t: k.x[:, t, 0:SEQ], k.v("final_ln"), None, D, 0)], 20000).alone()


def plan_weights(dram, entries):
    plan, chunks = [], 0
    for entry in entries:
        w = weight(dram, *entry)
        w["first"] = chunks % 2
        chunks += w["chunks"]
        plan.append(w)
    return plan


def build(nc, dram, out):
    with ExitStack() as ctx:
        k = Kernel(nc, ctx, dram)
        k.plan = plan_weights(dram, PLAN)
        drained, stored = k.counter("bank_drained"), k.counter("output_stored")
        with nc.Block() as block:

            @block.vector
            def _(dve):
                dve.sem_inc(drained.sem, BANKS)

        drained.base += BANKS
        load(k, [(k.vec[:, :], dram["vectors"]), (k.const[:, :], dram["consts"]), (k.x[:, :, 0:SEQ], dram["x"]),
                 (k.x[:, :, SEQ:TOK], dram["ctx"])])
        pool_delta_layer(k)
        cross_attention_layer(k, 0)
        squared_relu_layer(k, 0)
        nsa_layer(k)
        cross_attention_layer(k, 1)
        squared_relu_layer(k, 1)
        final_norm(k)
        both, x_only = [(0, SEQ), (SEQ, CTX)], [(0, SEQ)]
        mod = modulation(k, 0)
        fourier_hyena_layer(k, mod, both)
        conv_ffn(k, 0, mod, both)
        mod = modulation(k, 1)
        mla_layer(k, mod, both)
        conv_ffn(k, 1, mod, x_only)
        with nc.Block() as block:

            @block.sync
            def _(sp):
                sp.dma_start(out, k.x[:, :, 0:SEQ]).then_inc(stored.sem, 16)
                sp.wait_ge(*stored.at(16))




def chunked(w, cols, rows=P):
    kt, chunks = w.shape[0] // rows, w.shape[1] // cols
    return np.ascontiguousarray(w.reshape(kt, rows, chunks, cols).transpose(2, 1, 0, 3)).reshape(chunks, rows, kt * cols)


def by_rows(w, tiles):
    n = w.shape[1]
    return np.ascontiguousarray(w.reshape(-1, tiles, P, n).transpose(0, 2, 1, 3)).reshape(-1, P, tiles * n)


def by_feature(x):
    n, d = x.shape
    return np.ascontiguousarray(x.T.reshape(d // P, P, n).transpose(1, 0, 2))


def columns(v):
    d = v.shape[-1]
    if d % P:
        out = np.zeros((P, v.size // d), v.dtype)
        out[:d] = v.reshape(-1, d).T
        return out
    return np.ascontiguousarray(v.reshape(-1, P).T)


def spread(v):
    return np.broadcast_to(v.reshape(1, -1), (P, v.size))


def pack(entries, total, parts):
    out = np.zeros((P, total), np.float32)
    for name, (at, width) in entries.items():
        value = parts[name]
        assert value.shape[1] == width and value.shape[0] <= P, (name, value.shape, width)
        out[:value.shape[0], at:at + width] = value
    return out


def shape_constants():
    f = np.float32
    i = np.arange(P)
    levels = []
    for level in range(LEVELS):
        half = 1 << level
        pair = i // (2 * half)
        low = (i // half) % 2
        levels.append(((pair[:, None] == pair[None, :]) & (low[:, None] == 1) & (low[None, :] == 0)).astype(f))
    strip = np.zeros((P, 31), f)
    strip[:, 15] = 1
    swap = np.zeros((P, 32), f)
    for half in range(2):
        for j in range(8):
            a, b = MLA_NOPE + half * 16 + j, MLA_NOPE + half * 16 + 8 + j
            swap[b, half * 16 + j] = -1
            swap[a, half * 16 + 8 + j] = 1
    consts = pack(CONSTS, N_CONSTS, {
        "ident": np.eye(P, dtype=f), "ones": np.ones((P, P), f), "upto": (i[:, None] <= i[None, :]).astype(f),
        "strip": strip, "cmp_rows": (i[:, None] >= CMP_LEN - 1).astype(f),
        "not_first": (i[:, None] > 0).astype(f), "rope_swap": swap,
    })
    out = {"consts": consts, "level_masks": np.concatenate(levels, 1)}
    pos1 = np.arange(1, SEQ + 1, dtype=f)
    out["pool_inverse"] = np.ascontiguousarray(np.broadcast_to(
        np.concatenate([f(1) / np.minimum(pos1, f(w)) for w in POOL_WINDOWS]).reshape(1, -1), (P, 4 * SEQ))).astype(f)
    c = np.arange(SEQ)
    dist = (c[None, :] - 384 - i[:, None]).astype(f)
    out["key_minus_query"] = np.where(dist > 0, f(NEG * 1e3), dist).astype(f)
    end = np.arange(N_CMP) * CMP_STRIDE + CMP_LEN - 1
    slopes = np.exp2(-8.0 * np.arange(1, NSA_HEADS + 1) / NSA_HEADS)
    t = np.arange(SEQ)
    dc = t[:, None] - end[None, :]
    cb = np.where(dc[:, None, :] >= 0, -slopes[None, :, None] * dc[:, None, :], NEG)
    out["cmp_bias"] = np.ascontiguousarray(cb.reshape(TT, P, -1).transpose(1, 0, 2)).reshape(P, -1).astype(f)
    g = 128
    cc = 2 * np.pi * np.outer(np.arange(g), np.arange(g)) / g
    out["group_dft"] = np.concatenate([np.cos(cc), np.sin(cc)], 1).astype(f)
    for name, n in (("x", SEQ), ("c", CTX)):
        ss = 2 * np.pi * (np.outer(np.arange(n), np.arange(n)) % n) / n
        tiled = lambda a: np.ascontiguousarray(a.reshape(-1, P, a.shape[1]).transpose(1, 0, 2)).reshape(P, -1).astype(f)
        norm = (n * g) ** -0.5
        out["seq_dft_" + name] = np.stack([tiled(np.cos(ss) * norm), tiled(-np.sin(ss) * norm)])
        th = np.pi * (np.outer(np.arange(n), 2 * np.arange(n) + 1) % (4 * n)) / (2 * n)
        out["odd_dft_" + name] = np.stack([tiled(np.cos(th)), tiled(-np.sin(th)), tiled(np.cos(th).T / n), tiled(-np.sin(th).T / n)])
        pos = np.arange(n, dtype=f)
        tt = pos / f(max(n - 1, 1))
        bands = np.linspace(1e-4, (HY_EMB - 1) // 2 - 1, (HY_EMB - 1) // 2, dtype=f)
        ang = f(2.0 * math.pi / n) * pos[:, None] * bands[None, :]
        z = np.concatenate([tt[:, None], np.cos(ang), -np.sin(ang)], -1)
        out["hy_pos_" + name] = np.ascontiguousarray(z.T).astype(f)
        deltas = np.linspace(math.log(1e-2) / 0.3, math.log(1e-2) / 1.5, HY_CH, dtype=f)
        decay = np.exp(-tt[:, None] * np.abs(deltas)[None, :])
        out["hy_decay_" + name] = tiled(decay)
    rows = np.repeat(np.arange(SEQ // GRID_W, dtype=f), GRID_W)
    cols = np.tile(np.arange(GRID_W, dtype=f), SEQ // GRID_W)
    inv = (f(10000.0) ** (-np.arange(8, dtype=f) / 8)).astype(f)
    ar, ac = rows[None, :] * inv[:, None], cols[None, :] * inv[:, None]
    ang = np.concatenate([ar, ar, ac, ac])
    rope = np.zeros((P, 2 * SEQ), f)
    rope[MLA_NOPE:MLA_QK] = np.concatenate([np.cos(ang), np.sin(ang)], 1)
    out["rope"] = rope
    return out


def device_arrays(a):
    out = shape_constants()
    out["x"], out["mem"], out["ctx"] = by_feature(a["x"][0]), by_feature(a["mem"][0]), by_feature(a["ctx_2"][0])
    cond = np.stack([a["c_2"][0], a["c_ctx_2"]])
    out["vectors"] = pack(VECTORS, N_VECTORS, {
        "a_ln": columns(a["a_ln"]), "pool_scale": columns(a["a_pool_scale"]), "conv_w": columns(a["a_conv_w"][0]),
        "c_ln": columns(a["c_ln"]), "xa_ln": columns(a["xa_ln"]), "xa_mem_ln": columns(a["xa_mem_ln"]),
        "ff_ln": columns(a["ff_ln"]), "final_ln": columns(a["final_ln"]), "norm1": columns(a["norm1_2"]),
        "norm2": columns(a["norm2_2"]), "b_mod": columns(a["b_mod_2"]), "ffn_conv_w": columns(a["ffn_conv_w_2"]),
        "ffn_conv_b": columns(a["ffn_conv_b_2"]), "hy_conv_w": columns(a["hy_conv_w_2"]), "hy_conv_b": columns(a["hy_conv_b_2"]),
        "hy_bias": columns(a["hy_bias_2"]), "hy_b": columns(np.stack([a[f"hy_filt_b{i}_2"][0] for i in (1, 2, 3)])),
        "hy_freq": columns(a["hy_freq_2"]), "q_a_norm": columns(a["mla_q_a_norm_2"]), "kv_a_norm": columns(a["mla_kv_a_norm_2"]),
        "q_norm": columns(a["mla_q_norm_2"]), "k_norm": columns(a["mla_k_norm_2"]), "a_log": spread(a["a_a_log"]),
        "dt_bias": spread(a["a_dt_bias"]), "o_norm": spread(a["a_o_norm"]),
        "cond": by_feature(cond).reshape(P, 16),
    })
    w = a["a_w_in"][0]
    out["a_w_in"] = chunked(w[:, 0:2048], 512)
    out["a_w_gate"] = chunked(w[:, 2048:2560], 512)
    out["w_ba"] = chunked(w[:, 2560:2568], 8)[0]
    out["pool_w"] = np.ascontiguousarray(a["a_pool_w"][0].transpose(1, 0, 2)).reshape(P, -1)
    out["a_w_out"] = by_rows(a["a_w_out"][0], ROWS_OF_CHUNK)
    for l in range(2):
        for n in "qkv":
            out[f"xa_w{n}_{l}"] = chunked(a[f"xa_w{n}"][l], 512)
        out[f"xa_wo_{l}"] = by_rows(a["xa_wo"][l], ROWS_OF_CHUNK)
        out[f"ff_w1_{l}"] = chunked(a["ff_w1"][l], 512)
        out[f"ff_w2_{l}"] = by_rows(a["ff_w2"][l], ROWS_OF_CHUNK)
        up = a["ffn_w_up_2"][l].reshape(D, 2, FC // 2, 2 * P).transpose(0, 2, 1, 3).reshape(D, -1)
        out[f"ffn_up_{l}"] = chunked(up, 512)
        out[f"ffn_down_{l}"] = by_rows(a["ffn_w_down_2"][l], 2)
        out[f"w_mod_{l}"] = chunked(a["w_mod_2"][l], 512)
    w = a["c_w_in"][0]
    out["c_w_q"] = chunked(w[:, 0:1024], 512)
    out["c_w_c"] = chunked(w[:, 1024:1536], 512)
    kk = np.concatenate([w[:, 1536:1792], w[:, 2048:2304]], 1)
    out["c_w_k"] = chunked(kk, 512)
    out["c_w_v"] = chunked(np.concatenate([w[:, 1792:2048], w[:, 2304:2560]], 1), 512)
    out["w_gl"] = chunked(w[:, 2560:2608], 48)[0]
    for n in "kv":
        out["cmp_w1_" + n] = chunked(a[f"c_w1_{n}"][0], 128)
        out["cmp_w2_" + n] = np.ascontiguousarray(a[f"c_w2_{n}"][0])
        out["cmp_pe_" + n] = np.ascontiguousarray(a[f"c_pe_{n}"][0].reshape(16, 128).T)
    out["c_w_out"] = by_rows(a["c_w_out"][0], ROWS_OF_CHUNK)
    out["fh_w_in"] = chunked(a["fh_w_in_2"][0], 512)
    out["fh_w_out"] = chunked(a["fh_w_out_2"][0], 512)
    out["hy_w1"] = np.ascontiguousarray(a["hy_filt_w1_2"][0])
    out["hy_w23"] = np.concatenate([a["hy_filt_w2_2"][0], a["hy_filt_w3_2"][0]], 1)
    out["hy_w4"] = np.ascontiguousarray(a["hy_filt_w4_2"][0])
    out["mla_w_in"] = chunked(a["mla_w_in_2"][0], 416)
    out["mla_w_uq"] = chunked(a["mla_w_uq_2"][0], 1536)
    ukv = a["mla_w_ukv_2"][0].reshape(128, MLA_HEADS, 2, 64)
    out["mla_w_ukv"] = np.ascontiguousarray(ukv.transpose(0, 2, 1, 3)).reshape(1, P, 2048)
    out["mla_w_o"] = by_rows(a["mla_w_o_2"][0], ROWS_OF_CHUNK)
    return {n: np.ascontiguousarray(v, dtype=np.float32) if v.dtype != np.float32 else np.ascontiguousarray(v) for n, v in out.items()}




def kernel(**inputs):
    import concourse.bacc as bacc
    from concourse.bass_utils import run_bass_kernel_spmd

    arrays = device_arrays({n: np.asarray(v) for n, v in inputs.items()})
    nc = bacc.Bacc("TRN2", target_bir_lowering=False, num_devices=1)
    dram = {n: nc.dram_tensor("in_" + n, v.shape, mybir.dt.from_np(v.dtype), kind="ExternalInput").ap() for n, v in arrays.items()}
    out = nc.dram_tensor("out_x", (P, KT, SEQ), F32, kind="ExternalOutput").ap()
    build(nc, dram, out)
    r = run_bass_kernel_spmd(nc, [{"in_" + n: v for n, v in arrays.items()}], core_ids=[0])
    y = r.results[0]["out_x"]
    return np.ascontiguousarray(y.transpose(2, 1, 0)).reshape(1, SEQ, D)
```
